# Optimizing a Trainium2 kernel written in Bass

```python
import math
import jax, jax.numpy as jnp
from jax import lax
import numpy as np

D_MODEL = 1024
BATCH = 1
SEQ = 512
DEPTH = 2

N_BRANCHES = 4
BRANCH_WIDTH = D_MODEL // 2
D_FF = 2816
ROPE_THETA = 10000.0
NORM_EPS = 1e-6

M2_HEAD_DIM = 64
M2_HEADS = BRANCH_WIDTH // M2_HEAD_DIM
M2_GROUPS = 2
M2_STATE = 64
M2_CONV = 4
M2_CHUNK = 128
M2_CONV_DIM = BRANCH_WIDTH + 2 * M2_GROUPS * M2_STATE
M2_IN = BRANCH_WIDTH + M2_CONV_DIM + M2_HEADS

S5_GROUP = 16
S5_GROUPS = BRANCH_WIDTH // S5_GROUP
S5_STATE = 64
S5_IN = BRANCH_WIDTH

DSA_HEAD_DIM = 64
DSA_HEADS = BRANCH_WIDTH // DSA_HEAD_DIM
DSA_IDX_HEADS = 4
DSA_IDX_DIM = 64
DSA_TOPK = 256
DSA_QBLOCK = 128
DSA_IN = 3 * BRANCH_WIDTH + DSA_IDX_HEADS * DSA_IDX_DIM + DSA_IDX_DIM + DSA_IDX_HEADS

HG_HEADS = 4
HG_KDIM = 128
HG_VDIM = BRANCH_WIDTH // HG_HEADS
HG_CHUNK = 32
HG_IN = 2 * HG_HEADS * HG_KDIM + 2 * BRANCH_WIDTH

D_IN = M2_IN + S5_IN + DSA_IN + HG_IN
IN_SPLITS = [M2_IN, M2_IN + S5_IN, M2_IN + S5_IN + DSA_IN]

kernel_name = "hybrid_gated_ssd_s5_dsa_hgrn2_macaron"

def rms_norm(x, gain):
    xf = x.astype(jnp.float32)
    xf = xf * lax.rsqrt(jnp.mean(xf * xf, axis=-1, keepdims=True) + NORM_EPS)
    return (xf * gain.astype(jnp.float32)).astype(x.dtype)

def swiglu(x, w1, w3, w2):
    return (jax.nn.silu(x @ w1) * (x @ w3)) @ w2

def rope(x, positions):
    half = x.shape[-1] // 2
    inv_freq = ROPE_THETA ** (-jnp.arange(half, dtype=jnp.float32) / half)
    ang = positions.astype(jnp.float32)[..., None] * inv_freq
    cos = jnp.cos(ang)[:, :, None, :]
    sin = jnp.sin(ang)[:, :, None, :]
    xf = x.astype(jnp.float32)
    x1, x2 = xf[..., :half], xf[..., half:]
    return jnp.concatenate([x1 * cos - x2 * sin, x2 * cos + x1 * sin], axis=-1).astype(x.dtype)

def ssd_chunked(xh, dt, a, bg, cg):
    b, L, H, P = xh.shape
    nc = L // M2_CHUNK
    rep = H // M2_GROUPS
    bh = jnp.repeat(bg, rep, axis=2).reshape(b, nc, M2_CHUNK, H, M2_STATE)
    ch = jnp.repeat(cg, rep, axis=2).reshape(b, nc, M2_CHUNK, H, M2_STATE)
    xdt = (xh * dt[..., None]).reshape(b, nc, M2_CHUNK, H, P)
    ad = (dt * a).reshape(b, nc, M2_CHUNK, H).transpose(0, 3, 1, 2)
    a_cs = jnp.cumsum(ad, axis=-1)
    causal = jnp.tril(jnp.ones((M2_CHUNK, M2_CHUNK), dtype=bool))
    seg = a_cs[..., :, None] - a_cs[..., None, :]
    decay_in = jnp.exp(jnp.where(causal, seg, -jnp.inf))
    scores = jnp.einsum("bcqhn,bcshn->bhcqs", ch, bh) * decay_in
    y_diag = jnp.einsum("bhcqs,bcshp->bcqhp", scores, xdt)
    decay_to_end = jnp.exp(a_cs[..., -1:] - a_cs)
    states = jnp.einsum("bcshn,bhcs,bcshp->bchpn", bh, decay_to_end, xdt)
    a_tot = jnp.pad(a_cs[..., -1], ((0, 0), (0, 0), (1, 0)))
    tot_cs = jnp.cumsum(a_tot, axis=-1)
    causal_c = jnp.tril(jnp.ones((nc + 1, nc + 1), dtype=bool))
    decay_chunk = jnp.exp(jnp.where(causal_c, tot_cs[..., :, None] - tot_cs[..., None, :], -jnp.inf))
    states = jnp.concatenate([jnp.zeros_like(states[:, :1]), states], axis=1)
    states_in = jnp.einsum("bhzc,bchpn->bzhpn", decay_chunk, states)[:, :-1]
    y_off = jnp.einsum("bcqhn,bchpn,bhcq->bcqhp", ch, states_in, jnp.exp(a_cs))
    return (y_diag + y_off).reshape(b, L, H, P)

def mamba2_branch(p_in, conv_w, conv_b, dt_bias, a_log, d_skip, norm_g):
    b, L, _ = p_in.shape
    z, xbc, dt_raw = jnp.split(p_in, [BRANCH_WIDTH, BRANCH_WIDTH + M2_CONV_DIM], axis=-1)
    xbc = lax.conv_general_dilated(xbc, conv_w[:, None, :], window_strides=(1,),
                                   padding=[(M2_CONV - 1, 0)],
                                   dimension_numbers=("NWC", "WIO", "NWC"),
                                   feature_group_count=M2_CONV_DIM)
    xbc = jax.nn.silu(xbc + conv_b)
    xs, bs, cs = jnp.split(xbc, [BRANCH_WIDTH, BRANCH_WIDTH + M2_GROUPS * M2_STATE], axis=-1)
    dt = jax.nn.softplus(dt_raw + dt_bias)
    a = -jnp.exp(a_log)
    xh = xs.reshape(b, L, M2_HEADS, M2_HEAD_DIM)
    y = ssd_chunked(xh, dt, a, bs.reshape(b, L, M2_GROUPS, M2_STATE), cs.reshape(b, L, M2_GROUPS, M2_STATE))
    y = (y + d_skip[:, None] * xh).reshape(b, L, BRANCH_WIDTH)
    return rms_norm(y * jax.nn.silu(z), norm_g)

def _complex_affine_combine(e1, e2):
    a1r, a1i, b1r, b1i = e1
    a2r, a2i, b2r, b2i = e2
    return (a2r * a1r - a2i * a1i, a2r * a1i + a2i * a1r,
            a2r * b1r - a2i * b1i + b2r, a2r * b1i + a2i * b1r + b2i)

def s5_branch(u, lam_re, lam_im, b_re, b_im, c_re, c_im, d_skip, log_dt, w_glu):
    b, L, _ = u.shape
    ug = u.reshape(b, L, S5_GROUPS, S5_GROUP)
    step = jnp.exp(log_dt)[:, None]
    ldt_re, ldt_im = lam_re * step, lam_im * step
    mag = jnp.exp(ldt_re)
    ab_re, ab_im = mag * jnp.cos(ldt_im), mag * jnp.sin(ldt_im)
    den = lam_re * lam_re + lam_im * lam_im
    q_re = ((ab_re - 1.0) * lam_re + ab_im * lam_im) / den
    q_im = (ab_im * lam_re - (ab_re - 1.0) * lam_im) / den
    bb_re = q_re[..., None] * b_re - q_im[..., None] * b_im
    bb_im = q_re[..., None] * b_im + q_im[..., None] * b_re
    bu_re = jnp.einsum("blgi,gpi->blgp", ug, bb_re)
    bu_im = jnp.einsum("blgi,gpi->blgp", ug, bb_im)
    a_re = jnp.broadcast_to(ab_re, (1, L) + ab_re.shape)
    a_im = jnp.broadcast_to(ab_im, (1, L) + ab_im.shape)
    _, _, s_re, s_im = lax.associative_scan(_complex_affine_combine, (a_re, a_im, bu_re, bu_im), axis=1)
    y = jnp.einsum("blgp,gip->blgi", s_re, c_re) - jnp.einsum("blgp,gip->blgi", s_im, c_im)
    y = y.reshape(b, L, BRANCH_WIDTH) + d_skip * u
    y = jax.nn.gelu(y)
    g_lin, g_gate = jnp.split(y @ w_glu, 2, axis=-1)
    return g_lin * jax.nn.sigmoid(g_gate)

def dsa_branch(p_in, positions, q_norm, k_norm):
    b, L, _ = p_in.shape
    bw = BRANCH_WIDTH
    idx_q = DSA_IDX_HEADS * DSA_IDX_DIM
    q, k, v, qi, ki, wi = jnp.split(p_in, [bw, 2 * bw, 3 * bw, 3 * bw + idx_q, 3 * bw + idx_q + DSA_IDX_DIM], axis=-1)
    q = rope(rms_norm(q.reshape(b, L, DSA_HEADS, DSA_HEAD_DIM), q_norm), positions)
    k = rope(rms_norm(k.reshape(b, L, DSA_HEADS, DSA_HEAD_DIM), k_norm), positions).reshape(b, L, bw)
    qi = qi.reshape(b, L, DSA_IDX_HEADS, DSA_IDX_DIM)
    wi = wi * (DSA_IDX_HEADS ** -0.5)
    topk = min(DSA_TOPK, L // 4)
    nb = L // DSA_QBLOCK
    key_pos = jnp.arange(L)
    att_scale = DSA_HEAD_DIM ** -0.5
    gather = jax.vmap(lambda arr, ix: arr[ix])

    def block(args):
        blk, qb, qib, wib = args
        t = blk * DSA_QBLOCK + jnp.arange(DSA_QBLOCK)
        rel = jax.nn.relu(jnp.einsum("bqhd,bsd->bqhs", qib, ki) * (DSA_IDX_DIM ** -0.5))
        score = jnp.einsum("bqh,bqhs->bqs", wib, rel).astype(jnp.float32)
        score = jnp.where((key_pos[None, :] <= t[:, None])[None], score, -jnp.inf)
        _, idx = lax.top_k(score, topk)
        valid = idx <= t[None, :, None]
        k_sel = gather(k, idx).reshape(b, DSA_QBLOCK, topk, DSA_HEADS, DSA_HEAD_DIM)
        v_sel = gather(v, idx).reshape(b, DSA_QBLOCK, topk, DSA_HEADS, DSA_HEAD_DIM)
        logits = jnp.einsum("bqhd,bqkhd->bhqk", qb, k_sel).astype(jnp.float32) * att_scale
        logits = jnp.where(valid[:, None], logits, -jnp.inf)
        prob = jax.nn.softmax(logits, axis=-1).astype(v.dtype)
        return jnp.einsum("bhqk,bqkhd->bqhd", prob, v_sel)

    def to_blocks(t):
        return t.reshape((b, nb, DSA_QBLOCK) + t.shape[2:]).swapaxes(0, 1)

    out = lax.map(block, (jnp.arange(nb), to_blocks(q), to_blocks(qi), to_blocks(wi)))
    return out.swapaxes(0, 1).reshape(b, L, bw)

def hgrn2_chunked(q, k, v, log_f):
    b, L, H, K = q.shape
    V = v.shape[-1]
    nc = L // HG_CHUNK
    dt = v.dtype

    def shp(t):
        return t.reshape((b, nc, HG_CHUNK) + t.shape[2:])

    q, k, v, log_f = shp(q), shp(k), shp(v), shp(log_f)
    cum = jnp.cumsum(log_f, axis=2)
    last = cum[:, :, -1:]
    q_dec = (q * jnp.exp(cum)).astype(dt)
    k_dec = (k * jnp.exp(-cum)).astype(dt)
    k_end = (k * jnp.exp(last - cum)).astype(dt)
    causal = jnp.tril(jnp.ones((HG_CHUNK, HG_CHUNK), dtype=bool))
    att = jnp.where(causal, jnp.einsum("bcqhk,bcshk->bchqs", q_dec, k_dec), 0.0).astype(dt)
    o_intra = jnp.einsum("bchqs,bcshv->bcqhv", att, v)
    chunk_state = jnp.einsum("bcshk,bcshv->bchkv", k_end, v)
    chunk_decay = jnp.exp(last[:, :, 0]).astype(dt)

    def step(state, inp):
        decay, upd = inp
        return decay[..., None] * state + upd, state

    init = jnp.zeros((b, H, K, V), dtype=dt)
    _, states_in = lax.scan(step, init, (chunk_decay.swapaxes(0, 1), chunk_state.swapaxes(0, 1)))
    states_in = states_in.swapaxes(0, 1)
    o_inter = jnp.einsum("bcqhk,bchkv->bcqhv", q_dec, states_in)
    return (o_intra + o_inter).reshape(b, L, H, V)

def hgrn2_branch(p_in, lower_bound, norm_g):
    b, L, _ = p_in.shape
    hk = HG_HEADS * HG_KDIM
    q, f, i, g = jnp.split(p_in, [hk, 2 * hk, 2 * hk + BRANCH_WIDTH], axis=-1)
    q = jax.nn.silu(q).reshape(b, L, HG_HEADS, HG_KDIM)
    f = f.reshape(b, L, HG_HEADS, HG_KDIM)
    lb = lower_bound.reshape(HG_HEADS, HG_KDIM).astype(p_in.dtype)
    forget = lb + (1.0 - lb) * jax.nn.sigmoid(f)
    log_f = jnp.log(forget.astype(jnp.float32))
    key = (1.0 - lb) * jax.nn.sigmoid(-f)
    v = i.reshape(b, L, HG_HEADS, HG_VDIM)
    o = hgrn2_chunked(q, key, v, log_f)
    o = rms_norm(o, norm_g.reshape(HG_HEADS, HG_VDIM)).reshape(b, L, BRANCH_WIDTH)
    return o * jax.nn.sigmoid(g)

def setup_inputs(seed: int = 0) -> dict:
    key = jax.random.key(seed)
    ks = iter(jax.random.split(key, 48))
    f32 = jnp.float32

    def nrm(shape, scale):
        return jax.random.normal(next(ks), shape, f32) * scale

    def gain(shape):
        return 1.0 + nrm(shape, 0.02)

    L = DEPTH
    x = jax.random.normal(next(ks), (BATCH, SEQ, D_MODEL), f32)
    positions = jnp.broadcast_to(jnp.arange(SEQ, dtype=jnp.int32), (BATCH, SEQ))
    ffn1_norm = gain((L, D_MODEL))
    ffn1_w1 = nrm((L, D_MODEL, D_FF), D_MODEL ** -0.5)
    ffn1_w3 = nrm((L, D_MODEL, D_FF), D_MODEL ** -0.5)
    ffn1_w2 = nrm((L, D_FF, D_MODEL), D_FF ** -0.5)
    mix_norm = gain((L, D_MODEL))
    w_in = nrm((L, D_MODEL, D_IN), D_MODEL ** -0.5)
    w_gate = nrm((L, D_MODEL, N_BRANCHES * D_MODEL), D_MODEL ** -0.5)
    w_branch = nrm((L, N_BRANCHES, BRANCH_WIDTH, D_MODEL), BRANCH_WIDTH ** -0.5)
    w_out = nrm((L, D_MODEL, D_MODEL), D_MODEL ** -0.5)
    m2_conv_w = nrm((L, M2_CONV, M2_CONV_DIM), M2_CONV ** -0.5)
    m2_conv_b = nrm((L, M2_CONV_DIM), 0.01)
    dt0 = jnp.exp(jax.random.uniform(next(ks), (L, M2_HEADS), f32, math.log(1e-3), math.log(1e-1)))
    m2_dt_bias = dt0 + jnp.log(-jnp.expm1(-dt0))
    m2_a_log = jnp.log(jax.random.uniform(next(ks), (L, M2_HEADS), f32, 1.0, 16.0))
    m2_d = 1.0 + nrm((L, M2_HEADS), 0.1)
    m2_norm = gain((L, BRANCH_WIDTH))
    s5_lam_re = -0.5 + nrm((L, S5_GROUPS, S5_STATE), 0.01)
    s5_lam_im = math.pi * jnp.arange(S5_STATE, dtype=f32) + nrm((L, S5_GROUPS, S5_STATE), 0.01)
    s5_b_re = nrm((L, S5_GROUPS, S5_STATE, S5_GROUP), (2 * S5_GROUP) ** -0.5)
    s5_b_im = nrm((L, S5_GROUPS, S5_STATE, S5_GROUP), (2 * S5_GROUP) ** -0.5)
    s5_c_re = nrm((L, S5_GROUPS, S5_GROUP, S5_STATE), (2 * S5_STATE) ** -0.5)
    s5_c_im = nrm((L, S5_GROUPS, S5_GROUP, S5_STATE), (2 * S5_STATE) ** -0.5)
    s5_d = nrm((L, BRANCH_WIDTH), 1.0)
    s5_log_dt = jax.random.uniform(next(ks), (L, S5_GROUPS), f32, math.log(1e-3), math.log(1e-1))
    s5_w_glu = nrm((L, BRANCH_WIDTH, 2 * BRANCH_WIDTH), BRANCH_WIDTH ** -0.5)
    dsa_q_norm = gain((L, DSA_HEAD_DIM))
    dsa_k_norm = gain((L, DSA_HEAD_DIM))
    hg_gamma = nrm((L, HG_HEADS * HG_KDIM), 0.1)
    hg_norm = gain((L, BRANCH_WIDTH))
    ffn2_norm = gain((L, D_MODEL))
    ffn2_w1 = nrm((L, D_MODEL, D_FF), D_MODEL ** -0.5)
    ffn2_w3 = nrm((L, D_MODEL, D_FF), D_MODEL ** -0.5)
    ffn2_w2 = nrm((L, D_FF, D_MODEL), D_FF ** -0.5)
    return {"x": x, "positions": positions,
            "ffn1_norm": ffn1_norm, "ffn1_w1": ffn1_w1, "ffn1_w3": ffn1_w3, "ffn1_w2": ffn1_w2,
            "mix_norm": mix_norm, "w_in": w_in, "w_gate": w_gate, "w_branch": w_branch, "w_out": w_out,
            "m2_conv_w": m2_conv_w, "m2_conv_b": m2_conv_b, "m2_dt_bias": m2_dt_bias,
            "m2_a_log": m2_a_log, "m2_d": m2_d, "m2_norm": m2_norm,
            "s5_lam_re": s5_lam_re, "s5_lam_im": s5_lam_im, "s5_b_re": s5_b_re, "s5_b_im": s5_b_im,
            "s5_c_re": s5_c_re, "s5_c_im": s5_c_im, "s5_d": s5_d, "s5_log_dt": s5_log_dt,
            "s5_w_glu": s5_w_glu, "dsa_q_norm": dsa_q_norm, "dsa_k_norm": dsa_k_norm,
            "hg_gamma": hg_gamma, "hg_norm": hg_norm,
            "ffn2_norm": ffn2_norm, "ffn2_w1": ffn2_w1, "ffn2_w3": ffn2_w3, "ffn2_w2": ffn2_w2}

def reference(x, positions, ffn1_norm, ffn1_w1, ffn1_w3, ffn1_w2, mix_norm, w_in, w_gate, w_branch, w_out,
              m2_conv_w, m2_conv_b, m2_dt_bias, m2_a_log, m2_d, m2_norm,
              s5_lam_re, s5_lam_im, s5_b_re, s5_b_im, s5_c_re, s5_c_im, s5_d, s5_log_dt, s5_w_glu,
              dsa_q_norm, dsa_k_norm, hg_gamma, hg_norm, ffn2_norm, ffn2_w1, ffn2_w3, ffn2_w2):
    b, L, _ = x.shape
    lbs = jnp.cumsum(jax.nn.softmax(hg_gamma.astype(jnp.float32), axis=0), axis=0)
    lbs = lbs - lbs[0]
    for l in range(DEPTH):
        x = x + 0.5 * swiglu(rms_norm(x, ffn1_norm[l]), ffn1_w1[l], ffn1_w3[l], ffn1_w2[l])
        h = rms_norm(x, mix_norm[l])
        p = h @ w_in[l]
        p_m2, p_s5, p_dsa, p_hg = jnp.split(p, IN_SPLITS, axis=-1)
        y_a = mamba2_branch(p_m2, m2_conv_w[l], m2_conv_b[l], m2_dt_bias[l], m2_a_log[l], m2_d[l], m2_norm[l])
        y_b = s5_branch(p_s5, s5_lam_re[l], s5_lam_im[l], s5_b_re[l], s5_b_im[l], s5_c_re[l], s5_c_im[l],
                        s5_d[l], s5_log_dt[l], s5_w_glu[l])
        y_c = dsa_branch(p_dsa, positions, dsa_q_norm[l], dsa_k_norm[l])
        y_d = hgrn2_branch(p_hg, lbs[l], hg_norm[l])
        ys = jnp.stack([y_a, y_b, y_c, y_d], axis=2)
        proj = jnp.einsum("blgc,gcd->blgd", ys, w_branch[l])
        gates = jax.nn.sigmoid(h @ w_gate[l]).reshape(b, L, N_BRANCHES, D_MODEL)
        merged = jnp.einsum("blgd,blgd->bld", gates, proj)
        x = x + merged @ w_out[l]
        x = x + 0.5 * swiglu(rms_norm(x, ffn2_norm[l]), ffn2_w1[l], ffn2_w3[l], ffn2_w2[l])
    return x


_drawn_inputs = setup_inputs


def setup_inputs(seed=0):
    import zlib

    import numpy as np

    out = dict(_drawn_inputs(seed))
    spreads = {}
    factors = {'ffn1_norm': 3.465,
     'm2_conv_b': 6.347,
     'm2_norm': 14.046,
     's5_lam_re': 64.0,
     's5_lam_im': 29.336,
     's5_b_re': 39.512,
     's5_b_im': 40.168,
     's5_c_re': 40.256,
     's5_c_im': 40.512,
     's5_log_dt': 30.744,
     'dsa_q_norm': 8.0,
     'dsa_k_norm': 8.0,
     'hg_gamma': 31.633,
     'hg_norm': 23.804,
     'ffn2_norm': 5.412}
    for name, (base, spread) in spreads.items():
        noise = np.random.default_rng([zlib.crc32(name.encode()), seed]).standard_normal(out[name].shape)
        drawn = base * np.exp(spread * noise) if base else spread * noise
        out[name] = __import__('jax').numpy.asarray(drawn.astype(out[name].dtype))
    for name, factor in factors.items():
        out[name] = (out[name] * factor).astype(out[name].dtype)
    return out
```

```python
import math
import numpy as np
import concourse.bass as bass
from concourse import mybir
from contextlib import ExitStack

DEPTH, SEQ, DM, DFF = 2, 512, 1024, 2816
BW = DM // 2
P = 128
KT = DM // P
NB = SEQ // P
BT = BW // P
EPS = 1e-6
TOPK = min(256, SEQ // 4)
HG_CHUNK = 32
NCH = SEQ // HG_CHUNK
S5_TILES = 16
PI = math.pi
ROUND = 12582912.0
ROUND13 = 1536.0
NEG = -1.0e30
TAKEN = -3.0e38

FF_TILES = DFF // P
THIRDS = [8, 8, 6]
FFN_LOTS = 2 * FF_TILES + KT * len(THIRDS)


ORDER = (1, 2, 0, 3)
BRANCH_LOTS = {
    1: [("u", i) for i in range(4)] + [("glu", i) for i in range(4)],
    2: [("small", 0)] + [(w, i) for w in "qkv" for i in range(4)] + [("qi", 0), ("qi", 1), ("ki", 0)],
    0: [("z", i) for i in range(4)] + [("xbc", i) for i in range(6)],
    3: [(w, i) for w in ("hq", "hf", "hv", "hg") for i in range(4)],
}


def mix_lots():
    lots = []
    for g in ORDER:
        lots += BRANCH_LOTS[g] + merge_lots(g)
    return lots + [("out", i) for i in range(KT)]


def merge_lots(g):
    lots = []
    for pair in range(KT // 2):
        lots += [("gate%d" % g, 2 * pair), ("gate%d" % g, 2 * pair + 1), ("branch%d" % g, pair)]
    return lots


MIX = mix_lots()
MIX_LOTS = len(MIX)
NLOT = 2 * FFN_LOTS + MIX_LOTS
MIX0, FFN2_0 = FFN_LOTS, FFN_LOTS + MIX_LOTS


def outputs_of(kind):
    return 2 if kind == "glu" or kind.startswith("branch") else 1


OUT0 = [0]
for _n in range(NLOT):
    _mixing = FFN_LOTS <= _n < FFN_LOTS + MIX_LOTS
    OUT0.append(OUT0[-1] + (outputs_of(MIX[_n - FFN_LOTS][0]) if _mixing else 1))
LOT_AT = {MIX[_i]: MIX0 + _i for _i in range(MIX_LOTS)}


def out_at(kind, i, half=0):
    return OUT0[LOT_AT[(kind, i)]] + half


PAR_SIZES = dict(ffn1_norm=8, mix_norm=8, ffn2_norm=8, conv_w=24, conv_b=6, dt_bias=8, a_log=8, m2_d=4,
                 m2_norm=4, lam_re=16, lam_im=16, log_dt=16, s5_d=4, q_norm=1, k_norm=1, hg_norm=4)
PAR_AT, NPAR = {}, 0
for _name, _n in PAR_SIZES.items():
    PAR_AT[_name] = NPAR
    NPAR += _n
CON_SIZES = dict(ident=128, upper=512, blk=128, rot=128, hgmask=128, hgreset=512, tvec=512, cmask=128,
                 invfreq=1)
CON_AT, NCON = {}, 0
for _name, _n in CON_SIZES.items():
    CON_AT[_name] = NCON
    NCON += _n
UNITS = [(hp, b, e) for hp in range(4) for b in range(NB) for e in range(2)]
DA_OFF = [P * b * (b + 1) // 2 for b in range(NB)]
M2_OFF = [0, SEQ, 2 * SEQ - P, 3 * SEQ - 3 * P]


TILE = SEQ * 4
X_AT, H_AT, RING_AT = 0, 8, 24
MERGED_AT, YHL_AT, ARENA_AT = 48, 56, 64
CON_OFF = 97 * TILE


def trunk(nc, x_in, positions, w_lots, par_in, s5_in, con_in, gamma_in, out):
    f32, f32r, i32, u32 = mybir.dt.float32, mybir.dt.float32r, mybir.dt.int32, mybir.dt.uint32
    ALU, ACT, AX = mybir.AluOpType, mybir.ActivationFunctionType, mybir.AxisListType
    MUL, ADD, SUB = ALU.mult, ALU.add, ALU.subtract
    AFT = ACT
    ctx = ExitStack()
    with ctx:
        def at(name, shape, dt, tile, byte=0):
            return nc.alloc_sbuf_tensor_at(name, shape, dt, offset=BASE + tile * TILE + byte)

        BASE = -(-nc.sbuf_base // 32) * 32

        x = at("x", [P, KT, SEQ], f32, X_AT)
        h_hi = at("h_hi", [P, KT, SEQ], f32r, H_AT)
        h_lo = at("h_lo", [P, KT, SEQ], f32r, H_AT + 8)
        raw = at("raw", [P, 4, 8, P], f32, RING_AT)
        w_hi = at("w_hi", [P, 4, 8, P], f32r, RING_AT + 8)
        w_lo = at("w_lo", [P, 4, 8, P], f32r, RING_AT + 16)
        merged = at("merged", [P, KT, SEQ], f32, MERGED_AT)
        y_hi = at("y_hi", [P, BT, SEQ], f32r, YHL_AT)
        y_lo = at("y_lo", [P, BT, SEQ], f32r, YHL_AT + 4)
        con = at("con", [P, NCON], f32, 0, CON_OFF)
        par_off = CON_OFF + -(-4 * NCON // 32) * 32
        par = at("par", [P, NPAR], f32, 0, par_off)
        tail = par_off + -(-4 * NPAR // 32) * 32
        lower = at("lower", [P, DEPTH, 4], f32, 0, tail)
        epsc = at("epsc", [P, 1], f32, 0, tail + 32)
        half_pi = at("half_pi", [P, 1], f32, 0, tail + 64)
        rope_cos = at("rope_cos", [P, SEQ], f32, 0, tail + 96)
        rope_sin = at("rope_sin", [P, SEQ], f32, 0, tail + 96 + TILE)

        def C(name, a=0, b=None):
            k = CON_AT[name]
            return con[:, k + a:k + (CON_SIZES[name] if b is None else b)]

        def PR(name, a=0, b=None):
            k = PAR_AT[name]
            return par[:, k + a:k + (PAR_SIZES[name] if b is None else b)]

        def PC(name, i):
            return PR(name, i, i + 1)

        ident, ones = C("ident"), C("upper", P, 2 * P)

        g_hi = at("g_hi", [P, 8, SEQ], f32r, MERGED_AT)
        g_lo = at("g_lo", [P, 8, SEQ], f32r, MERGED_AT + 8)
        silu_a = at("silu_a", [P, 2, SEQ], f32, ARENA_AT)
        gated = at("gated", [P, 2, SEQ], f32, ARENA_AT + 2)
        sq = at("sq", [P, 2, SEQ], f32, ARENA_AT + 28)
        rms = at("rms", [P, SEQ], f32, ARENA_AT + 30)
        gate_th = at("gate_th", [P, 2, SEQ], f32, ARENA_AT + 31)
        normed = at("normed", [P, 2, SEQ], f32, ARENA_AT + 31)

        s5_u = at("s5_u", [P, 4, SEQ], f32, ARENA_AT)
        s5_bc = at("s5_bc", [P, 4, 16, 32], f32, ARENA_AT + 4)
        s5_bb = at("s5_bb", [P, 2, 16, 32], f32, ARENA_AT + 8)
        s5_bbt = at("s5_bbt", [P, 2, 4, P], f32, ARENA_AT + 10)
        s5_cos = at("s5_cos", [P, 2, SEQ], f32, ARENA_AT + 12)
        s5_sin = at("s5_sin", [P, 2, SEQ], f32, ARENA_AT + 14)
        s5_ph = at("s5_ph", [P, 4, SEQ], f32, ARENA_AT + 16)
        s5_pr = at("s5_pr", [P, 4, SEQ], f32, ARENA_AT + 20)
        s5_v = at("s5_v", [P, 2, SEQ], f32, ARENA_AT + 24)
        s5_z = at("s5_z", [P, 2, SEQ], f32, ARENA_AT + 26)
        s5_s = at("s5_s", [P, 2, 2, SEQ], f32, ARENA_AT + 28)
        s5_k = at("s5_k", [P, 24, 16], f32, ARENA_AT + 32)
        gel = at("gel", [P, 2, SEQ], f32, ARENA_AT + 12)
        gel_hi = at("gel_hi", [P, 4, SEQ], f32r, ARENA_AT + 16)
        gel_lo = at("gel_lo", [P, 4, SEQ], f32r, ARENA_AT + 20)
        glu_th = at("glu_th", [P, 2, SEQ], f32, ARENA_AT + 24)
        glu_y = at("glu_y", [P, 2, SEQ], f32, ARENA_AT + 26)

        da_qk = at("da_qk", [P, 8, SEQ], f32, ARENA_AT)
        da_v = at("da_v", [P, NB, BW], f32, ARENA_AT + 8)
        da_qi = at("da_qi", [P, 2, SEQ], f32, ARENA_AT + 12)
        da_ki = at("da_ki", [P, SEQ], f32, ARENA_AT + 14)
        da_t = at("da_t", [P, 4, SEQ], f32, ARENA_AT + 15)
        da_r = at("da_r", [P, 4, SEQ], f32, ARENA_AT + 15)
        da_sc = at("da_sc", [P, SEQ], f32, ARENA_AT + 19)
        da_wk = at("da_wk", [P, SEQ], f32, ARENA_AT + 20)
        da_mb = at("da_mb", [P, 1280], f32, ARENA_AT + 21)
        da_lg = at("da_lg", [P, 2, SEQ], f32, ARENA_AT + 24)
        da_p = at("da_p", [P, 2, SEQ], f32, ARENA_AT + 26)
        da_pt = at("da_pt", [P, 2, SEQ], f32, ARENA_AT + 28)
        da_st = at("da_st", [P, 32, 4], f32, ARENA_AT + 30)
        da_m8 = at("da_m8", [P, 8], f32, ARENA_AT + 31)
        small = at("small", [P, NB, 12], f32, 0, tail + 96 + 2 * TILE)

        m2_z = at("m2_z", [P, 4, SEQ], f32, ARENA_AT)
        m2_xr = at("m2_xr", [P, 6, SEQ + 4], f32, ARENA_AT + 4)
        m2_xc = at("m2_xc", [P, 6, SEQ], f32, ARENA_AT + 11)
        m2_cb = at("m2_cb", [P, 2, 1280], f32, ARENA_AT + 17)
        m2_xdt = at("m2_xdt", [P, NB, BW], f32, ARENA_AT + 22)
        m2_e = at("m2_e", [P, 2, 1280], f32, ARENA_AT + 26)
        m2_dt = at("m2_dt", [P, 6, NB, 8], f32, ARENA_AT + 31)
        m2_yv = at("m2_yv", [P, 4, SEQ], f32, ARENA_AT + 4)
        m2_t = at("m2_t", [P, 3, SEQ], f32, ARENA_AT + 8)

        hq = at("hq", [P, 4, SEQ], f32, ARENA_AT)
        hf = at("hf", [P, 4, SEQ], f32, ARENA_AT + 4)
        hv = at("hv", [P, NB, BW], f32, ARENA_AT + 8)
        hg = at("hg", [P, 4, SEQ], f32, ARENA_AT + 12)
        he = at("he", [P, 10, SEQ], f32, ARENA_AT + 16)
        hken = at("hken", [P, NB, P], f32, ARENA_AT + 26)
        hatt = at("hatt", [P, NB, P], f32, ARENA_AT + 27)
        hS = at("hS", [P, NCH, P], f32, ARENA_AT + 28)
        hdec = at("hdec", [P, NCH], f32, ARENA_AT + 32)
        hlb = at("hlb", [P, 2, 4], f32, ARENA_AT + 32, 256)

        x_nat = at("x_nat", [P, NB, DM], f32, ARENA_AT)
        pos_i = at("pos_i", [P, SEQ], i32, ARENA_AT + 16)
        ang = at("ang", [P, 4, SEQ], f32, ARENA_AT + 17)
        gam = at("gam", [P, DEPTH, 4], f32, ARENA_AT + 21)
        gtmp = at("gtmp", [P, 6, DEPTH, 4], f32, ARENA_AT + 22)
        o_nat = at("o_nat", [P, NB, DM], f32, ARENA_AT)

        bank = [nc.alloc_psum_tensor("bank%d" % i, [P, SEQ], f32) for i in range(8)]

        LAYER = """raw_in0 raw_in1 raw_in2 raw_in3 hi_done lo_done out_done free0 free1 free2 free3
            sq_done sq_used rms_ready normed_ready h_hi_done h_done g_hi_done g_done
            act_seq dve_seq par_in s5_in
            s5_k_ready s5_bb_ready s5_bbt_psum s5_bbt_ready s5_phase s5_trig s5_bu s5_bu_used s5_state
            s5_y s5_y_used s5_gelu gel_hi_done gel_done glu_th_done glu_y_done y_hi_done y_done
            th_done merge_used merged_done
            da_sq da_ms da_rms da_qn da_rot da_rot_done da_rel da_relu da_relu_used da_score da_causal
            da_mask da_logit da_max da_exp da_prob da_pt_psum da_pt_ready da_pv da_pv_hi da_logit_used
            m2_dtb m2_abs m2_dt_ready m2_acs m2_acs_done m2_ct m2_xdt_done m2_conv m2_silu m2_cbp m2_cb_done m2_acb
            m2_seg m2_decay m2_m m2_yp m2_y m2_sq m2_ms m2_rms m2_yn
            hg_e hg_fg hg_lf hg_cum hg_ec hg_ke hg_ket hg_ken hg_attp hg_att hg_upd hg_updu hg_S hg_op
            hg_o hg_sq hg_ms hg_rms hg_yn hg_lc hg_el
            layer_end""".split()
        sems = {}
        for name in LAYER:
            sems[name] = ctx.enter_context(nc.semaphore(name))
        for name in """go_sp go_act go_dve go_pe c_con c_x c_pos c_gam p_x p_xt p_ang p_trig p_gam1 p_gam2 p_seq
                e_x e_o e_out""".split():
            sems[name] = ctx.enter_context(nc.semaphore(name))
        S = sems
        first, last = sems[LAYER[0]].num, sems["layer_end"].num
        assert last - first == len(LAYER) - 1
        raw_in = [S["raw_in%d" % i] for i in range(4)]
        free = [S["free%d" % i] for i in range(4)]

        block = ctx.enter_context(nc.Block())

        def wait_out(eng, t):
            eng.wait_ge(S["out_done"], t + 1)

        def wait_taken(eng, t):
            t0, it = t if isinstance(t, tuple) else (t, 0)
            if isinstance(t, tuple) or t >= 0:
                eng.wait_ge(free[t0 % 4], it + (t0 // 4 + 1))

        def end_of_layer(eng, go):
            eng.drain()
            eng.sem_inc(S["layer_end"], 1)
            eng.wait_ge(go, 1)
            eng.sem_clear(go)

        def split_hi(act, n0, it=0):
            if isinstance(it, int) and n0 >= NLOT:
                return
            s = n0 % 4
            act.wait_ge(raw_in[s], 16 * (it + n0 // 4 + 1))
            if n0 >= 4:
                act.wait_ge(S["out_done"], OUT0[n0 - 3] + 4 * it)
            act.activation(w_hi[:, s], raw[:, s], AFT.Copy).then_inc(S["hi_done"], 1)

        def split_lo(eng, n0, it=0):
            if isinstance(it, int) and n0 >= NLOT:
                return
            s = n0 % 4
            eng.wait_ge(S["hi_done"], n0 + 1 + 4 * it)
            eng.tensor_tensor(w_lo[:, s], raw[:, s], w_hi[:, s].bitcast(f32), SUB).then_inc(S["lo_done"], 1)

        class Order:

            def __init__(self, eng, sem):
                self.eng, self.sem, self.n = eng, sem, 0

            def do(self, ins):
                self.n += 1
                ins.then_inc(self.sem, 1)
                return self.n

            def need(self, n):
                self.eng.wait_ge(self.sem, n)

        def gsplit(n):
            return OUT0[n]

        @block.tensor
        def _(pe):
            def gemm(n0, it, xh, xl, nk, k0=0, t0=None, lastin=True):
                s, t0 = n0 % 4, OUT0[n0] if t0 is None else t0
                pe.wait_ge(S["lo_done"], it * 4 + (n0 + 1))
                if t0 >= 4:
                    pe.wait_ge(free[t0 % 4], it + t0 // 4)
                b = bank[t0 % 4]
                for k in range(nk):
                    pe.matmul(b[:, :], w_hi[:, s, k0 + k], xh[:, k], start=(k == 0), stop=False)
                    pe.matmul(b[:, :], w_hi[:, s, k0 + k], xl[:, k], start=False, stop=False)
                    m = pe.matmul(b[:, :], w_lo[:, s, k0 + k], xh[:, k], start=False, stop=(k == nk - 1))
                m.then_inc(S["out_done"], 1)

            def gemm_tokens(n0, cols):
                s, t0 = n0 % 4, OUT0[n0]
                pe.wait_ge(S["lo_done"], n0 + 1)
                pe.wait_ge(free[t0 % 4], t0 // 4)
                for b in range(NB):
                    o = bank[t0 % 4][:, P * b:P * b + cols]
                    tok = slice(P * b, P * (b + 1))
                    for k in range(KT):
                        pe.matmul(o, h_hi[:, k, tok], w_hi[:, s, k, 0:cols], start=(k == 0), stop=False)
                        pe.matmul(o, h_lo[:, k, tok], w_hi[:, s, k, 0:cols], start=False, stop=False)
                        m = pe.matmul(o, h_hi[:, k, tok], w_lo[:, s, k, 0:cols], start=False, stop=(k == KT - 1))
                m.then_inc(S["out_done"], 1)

            def norm_sums(r):
                for i in range(KT):
                    pe.wait_ge(S["sq_done"], KT * r + i + 1)
                    pe.matmul(bank[7][:, :], ones, sq[:, i % 2], start=(i == 0), stop=(i == KT - 1)) \
                      .then_inc(S["sq_used"], 1)

            def ffn(which, nb):
                norm_sums(2 * which)
                pe.wait_ge(S["h_done"], KT * (3 * which + 1))
                n, g0 = nb, FF_TILES * which
                for J in THIRDS:
                    with pe.Fori(0, J // 2) as it:
                        for j in range(4):
                            gemm(n + j, it, h_hi, h_lo, KT)
                    n, g0 = n + 2 * J, g0 + J
                    pe.wait_ge(S["g_done"], g0)
                    with pe.Fori(0, 2) as it:
                        for j in range(4):
                            gemm(n + j, it, g_hi, g_lo, J)
                    n += KT

            def gemm_h(n):
                gemm(n, 0, h_hi, h_lo, KT)

            def merge(g, order):
                for pair in range(KT // 2):
                    gemm_h(LOT_AT[("gate%d" % g, 2 * pair)])
                    gemm_h(LOT_AT[("gate%d" % g, 2 * pair + 1)])
                    n = LOT_AT[("branch%d" % g, pair)]
                    if pair == 0:
                        pe.wait_ge(S["y_done"], BT * (order + 1))
                    for half in range(2):
                        gemm(n, 0, y_hi, y_lo, BT, k0=BT * half, t0=OUT0[n] + half)
            def s5(order):
                for i in range(4):
                    gemm_h(LOT_AT[("u", i)])
                pe.wait_ge(S["s5_bb_ready"], 2)
                for c in range(2):
                    for jt in range(4):
                        m = pe.transpose(bank[4 + c][:, P * jt:P * (jt + 1)],
                                         s5_bb[:, c].rearrange("p s i -> p (s i)")[:, P * jt:P * (jt + 1)], ident)
                    m.then_inc(S["s5_bbt_psum"], 1)
                pe.wait_ge(S["s5_bbt_ready"], 2)

                def drive(st):
                    q, jt = st % 4, st // 4
                    wait_taken(pe, out_at("u", jt))
                    if st:
                        pe.wait_ge(S["s5_bu_used"], st)
                    for c in range(2):
                        m = pe.matmul(bank[4 + c][:, :], s5_bbt[32 * q:32 * q + 32, c, jt], s5_u[32 * q:32 * q + 32, jt],
                                      start=True, stop=True)
                    m.then_inc(S["s5_bu"], 1)

                def read(st):
                    q, jt = st % 4, st // 4
                    pe.wait_ge(S["s5_state"], 2 * (st + 1))
                    if q == 0 and jt:
                        pe.wait_ge(S["s5_y_used"], jt)
                    for c in range(2):
                        m = pe.matmul(bank[6][32 * q:32 * q + 32, :], s5_bc[:, 2 + c, st], s5_s[:, st % 2, c],
                                      start=(c == 0), stop=(c == 1))
                    m.then_inc(S["s5_y"], 1)
                for st in range(S5_TILES):
                    drive(st)
                    if st:
                        read(st - 1)
                read(S5_TILES - 1)
                pe.wait_ge(S["gel_done"], 4)
                for i in range(4):
                    n = LOT_AT[("glu", i)]
                    for half in range(2):
                        gemm(n, 0, gel_hi, gel_lo, BT, k0=4 * half, t0=OUT0[n] + half)

            def dsa(order):
                gemm_tokens(LOT_AT[("small", 0)], 12)
                for w in "qk":
                    for i in range(4):
                        gemm_h(LOT_AT[(w, i)])
                for i in range(4):
                    gemm_tokens(LOT_AT[("v", i)], P)
                for lot in (("qi", 0), ("qi", 1), ("ki", 0)):
                    gemm_h(LOT_AT[lot])
                for g in range(2):
                    for j in range(4):
                        pe.wait_ge(S["da_sq"], 4 * g + j + 1)
                        pe.matmul(bank[4 + j][:, :], C("blk"), da_t[:, j], start=True, stop=True) \
                          .then_inc(S["da_ms"], 1)
                    for j in range(4):
                        pe.wait_ge(S["da_qn"], 4 * g + j + 1)
                        pe.matmul(bank[4 + j][:, :], C("rot"), da_qk[:, 4 * g + j], start=True, stop=True) \
                          .then_inc(S["da_rot"], 1)
                pe.wait_ge(S["da_rot_done"], 8)
                wait_taken(pe, out_at("ki", 0))
                for b in range(1, NB):
                    if b > 1:
                        pe.wait_ge(S["da_relu"], 4 * (b - 1))
                    for hh in range(4):
                        r = slice(64 * (hh % 2), 64 * (hh % 2) + 64)
                        m = pe.matmul(bank[4 + hh][:, 0:P * (b + 1)], da_qi[r, hh // 2, P * b:P * (b + 1)],
                                      da_ki[r, 0:P * (b + 1)], start=True, stop=True)
                    m.then_inc(S["da_rel"], 1)
                pe.wait_ge(S["da_relu"], 12)

                def logits(u):
                    hp, b, e = UNITS[u]
                    r = slice(64 * e, 64 * e + 64)
                    if u >= 2:
                        pe.wait_ge(S["da_max"], u - 1)
                    pe.matmul(bank[4 + u % 2][:, 0:P * (b + 1)], da_qk[r, hp, P * b:P * (b + 1)],
                              da_qk[r, 4 + hp, 0:P * (b + 1)], start=True, stop=True).then_inc(S["da_logit"], 1)

                def turn(u):
                    hp, b, e = UNITS[u]
                    pe.wait_ge(S["da_prob"], u + 1)
                    if u:
                        pe.wait_ge(S["da_pt_ready"], u)
                    for j in range(b + 1):
                        m = pe.transpose(bank[6][:, P * j:P * (j + 1)], da_p[:, u % 2, P * j:P * (j + 1)], ident)
                    m.then_inc(S["da_pt_psum"], 1)

                def values(u):
                    hp, b, e = UNITS[u]
                    h = 2 * hp + e
                    pe.wait_ge(S["da_pt_ready"], u + 1)
                    if u % 8 == 0 and hp:
                        pe.wait_ge(S["y_done"], BT * order + hp)
                    for j in range(b + 1):
                        m = pe.matmul(bank[7][64 * e:64 * e + 64, P * b:P * (b + 1)], da_v[:, j, 64 * h:64 * h + 64],
                                      da_pt[:, u % 2, P * j:P * (j + 1)], start=(j == 0), stop=(j == b))
                    m.then_inc(S["da_pv"], 1)
                logits(0)
                logits(1)
                for u in range(32):
                    turn(u)
                    if u + 2 < 32:
                        logits(u + 2)
                    values(u)

            def mamba(order):
                for i in range(4):
                    gemm_h(LOT_AT[("z", i)])
                for i in range(6):
                    gemm_h(LOT_AT[("xbc", i)])
                pe.wait_ge(S["m2_dt_ready"], 1)
                for b in range(NB):
                    for j in range(b + 1):
                        m = pe.matmul(bank[4][:, 8 * b:8 * b + 8], C("upper", 0, P) if j == b else ones, m2_dt[:, 4, j],
                                      start=(j == 0), stop=(j == b))
                m.then_inc(S["m2_acs"], 1)
                pe.wait_ge(S["m2_silu"], 4)
                for b in range(NB):
                    if b >= 2:
                        pe.wait_ge(S["m2_xdt_done"], b - 1)
                    for i in range(4):
                        m = pe.transpose(bank[5 + b % 2][:, P * i:P * (i + 1)], m2_xc[:, i, P * b:P * (b + 1)], ident)
                    m.then_inc(S["m2_ct"], 1)
                pe.wait_ge(S["m2_silu"], 6)
                pe.wait_ge(S["m2_acs_done"], 1)
                for c in range(8):
                    g, j = c // 4, c % 4
                    r = slice(64 * g, 64 * g + 64)
                    if c >= 2:
                        pe.wait_ge(S["m2_cb_done"], c - 1)
                    pe.matmul(bank[4 + 3 * (c % 2)][:, 0:SEQ - P * j], m2_xc[r, 4, P * j:P * (j + 1)],
                              m2_xc[r, 5, P * j:SEQ], start=True, stop=True).then_inc(S["m2_cbp"], 1)
                pe.wait_ge(S["m2_cb_done"], 8)
                pe.wait_ge(S["m2_xdt_done"], 4)

                def decays(h):
                    if h >= 2:
                        pe.wait_ge(S["m2_seg"], h - 1)
                    for j in range(NB):
                        m = pe.matmul(bank[4 + h % 2][:, P * j:SEQ], m2_dt[:, 4, j, h:h + 1].broadcast_to([P, P]),
                                      C("upper", 0, SEQ - P * j), start=(j == 0), stop=(j == NB - 1))
                    m.then_inc(S["m2_acb"], 1)

                def outs(h):
                    pe.wait_ge(S["m2_m"], h + 1)
                    if h % 2 == 0 and h >= 4:
                        pe.wait_ge(S["m2_y"], h // 2 - 1)
                    e = 64 * (h % 2)
                    for j in range(NB):
                        m = pe.matmul(bank[6 + h // 2 % 2][e:e + 64, P * j:SEQ], m2_xdt[:, j, 64 * h:64 * h + 64],
                                      m2_e[:, h % 2, M2_OFF[j]:M2_OFF[j] + SEQ - P * j], start=(j == 0), stop=(j == NB - 1))
                    m.then_inc(S["m2_yp"], 1)
                decays(0)
                for h in range(8):
                    if h < 7:
                        decays(h + 1)
                    outs(h)
                for i in range(BT):
                    pe.wait_ge(S["m2_sq"], i + 1)
                    pe.matmul(bank[4][:, :], ones, m2_t[:, i % 2], start=(i == 0), stop=(i == BT - 1)) \
                      .then_inc(S["m2_ms"], 1)

            def hgrn(order):
                for i in range(4):
                    gemm_h(LOT_AT[("hq", i)])
                for i in range(4):
                    gemm_h(LOT_AT[("hf", i)])
                for i in range(4):
                    gemm_tokens(LOT_AT[("hv", i)], P)
                for i in range(4):
                    gemm_h(LOT_AT[("hg", i)])
                for h in range(4):
                    v = slice(P * h, P * (h + 1))
                    pe.wait_ge(S["hg_ke"], 3 * h + 2)
                    if h:
                        pe.wait_ge(S["hg_att"], h)
                    for j in range(NB):
                        t = slice(P * j, P * (j + 1))
                        m = pe.matmul(bank[4][:, t], he[:, 8, t], he[:, 7, t], start=True, stop=True)
                    m.then_inc(S["hg_attp"], 1)
                    pe.wait_ge(S["hg_ke"], 3 * h + 3)
                    if h:
                        pe.wait_ge(S["hg_o"], h)
                    for j in range(NB):
                        t = slice(P * j, P * (j + 1))
                        m = pe.transpose(bank[5][:, t], he[:, 9, t], ident)
                    m.then_inc(S["hg_ket"], 1)
                    pe.wait_ge(S["hg_ken"], h + 1)
                    pe.wait_ge(S["hg_att"], h + 1)
                    for j in range(NB):
                        for q in range(4 if j < NB - 1 else 3):
                            r = slice(32 * q, 32 * q + 32)
                            m = pe.matmul(bank[4 + q][:, P * j:P * (j + 1)], hken[r, j], hv[r, j, v],
                                          start=True, stop=True)
                        m.then_inc(S["hg_upd"], 1)
                    pe.wait_ge(S["hg_updu"], 4 * h + 4)
                    for j in range(NB):
                        t = slice(P * j, P * (j + 1))
                        m = pe.matmul(bank[5][:, t], hv[:, j, v], hatt[:, j], start=True, stop=False)
                        for c in range(4 * j, 4 * j + 4):
                            if c:
                                tc = slice(HG_CHUNK * c, HG_CHUNK * (c + 1))
                                m = pe.matmul(bank[5][:, tc], hS[:, c], he[:, 7, tc], start=False, stop=(c % 4 == 3))
                    m.then_inc(S["hg_op"], 1)
                for h in range(4):
                    pe.wait_ge(S["hg_sq"], h + 1)
                    if h == 0:
                        pe.wait_ge(S["hg_o"], 4)
                    pe.matmul(bank[4 + h][:, :], ones, he[:, h % 2], start=True, stop=True).then_inc(S["hg_ms"], 1)

            MIXERS = {0: mamba, 1: s5, 2: dsa, 3: hgrn}

            def mixers():
                for order, g in enumerate(ORDER):
                    MIXERS[g](order)
                    merge(g, order)

            pe.wait_ge(S["c_con"], 16)
            pe.wait_ge(S["c_x"], 16)
            for i in range(KT):
                for b in range(NB):
                    m = pe.transpose(bank[i][:, P * b:P * (b + 1)], x_nat[:, b, P * i:P * (i + 1)], ident)
                m.then_inc(S["p_x"], 1)
            pe.wait_ge(S["p_xt"], KT)
            with pe.Fori(0, DEPTH) as layer:
                ffn(0, 0)
                norm_sums(1)
                pe.wait_ge(S["h_done"], KT * 2)
                mixers()
                pe.wait_ge(S["h_done"], KT * 3)
                for i in range(KT):
                    gemm_h(LOT_AT[("out", i)])
                ffn(1, FFN2_0)
                end_of_layer(pe, S["go_pe"])
            for b in range(NB):
                for i in range(KT):
                    m = pe.transpose(bank[2 * b + i // 4][:, P * (i % 4):P * (i % 4 + 1)],
                                     x[:, i, P * b:P * (b + 1)], ident)
                    if i % 4 == 3:
                        m.then_inc(S["e_x"], 1)

        @block.sync
        def _(sp):
            sp.dma_start(con[:, :], con_in).then_inc(S["c_con"], 16)
            sp.dma_start(x_nat[:, :, :], x_in.rearrange("(b p) d -> p b d", p=P)).then_inc(S["c_x"], 16)
            sp.dma_start(pos_i[:, :], positions.partition_broadcast(P)).then_inc(S["c_pos"], 16)
            sp.dma_start(gam[:, :, :], gamma_in).then_inc(S["c_gam"], 16)
            sp.wait_ge(S["p_xt"], KT)
            sp.wait_ge(S["p_gam2"], 1)
            sp.wait_ge(S["p_trig"], 3)
            with sp.Fori(0, DEPTH) as layer:
                sp.dma_start(par[:, :], par_in[layer]).then_inc(S["par_in"], 16)
                sp.dma_start(s5_bc[:, :, :, :].rearrange("p a b c -> p (a b c)"), s5_in[layer]) \
                  .then_inc(S["s5_in"], 16)
                for n in range(4):
                    sp.dma_start(raw[:, n].rearrange("p k m -> p (k m)"), w_lots[layer * NLOT + n]) \
                      .then_inc(raw_in[n], 16)
                with sp.Fori(1, NLOT // 4) as it:
                    for s in range(4):
                        sp.wait_ge(S["lo_done"], it * 4 + (s - 3))
                        sp.dma_start(raw[:, s].rearrange("p k m -> p (k m)"),
                                     w_lots[layer * NLOT + it * 4 + s]).then_inc(raw_in[s], 16)
                for n in range(NLOT // 4 * 4, NLOT):
                    sp.wait_ge(S["lo_done"], n - 3)
                    sp.dma_start(raw[:, n % 4].rearrange("p k m -> p (k m)"), w_lots[layer * NLOT + n]) \
                      .then_inc(raw_in[n % 4], 16)
                end_of_layer(sp, S["go_sp"])
            for b in range(NB):
                sp.wait_ge(S["e_o"], 2 * (b + 1))
                sp.dma_start(out[P * b:P * (b + 1), :], o_nat[:, b]).then_inc(S["e_out"], 16)
            sp.wait_ge(S["e_out"], 16 * NB)

        @block.gpsimd
        def _(pool):
            def split_lots():
                a, b = MIX0 + 4, FFN2_0 + 4
                pool.wait_ge(S["lo_done"], a)
                with pool.Fori(0, (b - a) // 4) as it:
                    for j in range(4):
                        split_lo(pool, a + j, it)
                for n in range(b - (b - a) % 4, b):
                    split_lo(pool, n)
            def mixers(*a):
                pass

            with pool.Fori(0, DEPTH) as layer:
                split_lots()
                pool.wait_ge(S["layer_end"], 4)
                pool.sem_clear(range(first, last + 1))
                for go in ("go_sp", "go_act", "go_dve", "go_pe"):
                    pool.sem_inc(S[go], 1)

        @block.scalar
        def _(act):
            seq = Order(act, S["act_seq"])

            def norm(r, x_ready):
                for i in range(KT):
                    x_ready(i)
                    if KT * r + i >= 2:
                        act.wait_ge(S["sq_used"], KT * r + i - 1)
                    act.activation(sq[:, i % 2], x[:, i], AFT.Square).then_inc(S["sq_done"], 1)
                act.wait_ge(S["sq_used"], KT * (r + 1))
                act.activation(rms[:, :], bank[7][:, :], AFT.Sqrt, scale=1.0 / DM, bias=epsc[:, :]) \
                   .then_inc(S["rms_ready"], 1)
                high_parts(KT * r)

            def high_parts(n0):
                for i in range(KT):
                    act.wait_ge(S["normed_ready"], n0 + i + 1)
                    act.activation(h_hi[:, i], normed[:, i % 2], AFT.Copy).then_inc(S["h_hi_done"], 1)

            def ffn(which, nb):
                n, g0 = nb, FF_TILES * which
                for th, J in enumerate(THIRDS):
                    with act.Fori(0, J // 2) as it:
                        for q in range(2):
                            na, nbb = n + 2 * q, n + 2 * q + 1
                            ta, tb = OUT0[na], OUT0[nbb]
                            act.wait_ge(S["out_done"], it * 4 + (ta + 1))
                            if tb >= 4:
                                act.wait_ge(free[tb % 4], it + tb // 4)
                            act.activation(silu_a[:, q], bank[ta % 4][:, :], AFT.Silu).then_inc(free[ta % 4], 1)
                            split_hi(act, na + 4, it)
                            split_hi(act, nbb + 4, it)
                            act.wait_ge(free[tb % 4], it + (tb // 4 + 1))
                            act.activation(g_hi[:, it * 2 + q], gated[:, q], AFT.Copy).then_inc(S["g_hi_done"], 1)
                    n += 2 * J
                    if nb == FFN2_0 and th == len(THIRDS) - 1:
                        for j in range(KT):
                            split_hi(act, n + j + 4)
                    else:
                        with act.Fori(0, 2) as it:
                            for j in range(4):
                                split_hi(act, n + j + 4, it)
                    n += KT

            def evac(dst, n, func=AFT.Copy, **kw):
                t = OUT0[n]
                wait_out(act, t)
                src = bank[t % 4][:, :]
                act.activation(dst, src, func, **kw).then_inc(free[t % 4], 1)
                split_hi(act, n + 4)

            def merge(g, order):
                for pair in range(KT // 2):
                    for e in range(2):
                        n = LOT_AT[("gate%d" % g, 2 * pair + e)]
                        t, i = OUT0[n], KT * order + 2 * pair + e
                        wait_out(act, t)
                        if i >= 2:
                            act.wait_ge(S["merge_used"], i - 1)
                        act.activation(gate_th[:, e], bank[t % 4][:, :], AFT.Tanh, scale=0.5).then_inc(free[t % 4], 1)
                        split_hi(act, n + 4)
                    split_hi(act, LOT_AT[("branch%d" % g, pair)] + 4)
            def chain(ins):
                seq.need(seq.do(ins))

            def split_y(i, src, order, ready, scale=1.0):
                ready()
                if order:
                    wait_out(act, out_at("branch%d" % ORDER[order - 1], KT // 2 - 1, 1))
                act.activation(y_hi[:, i], src, AFT.Copy, scale=scale).then_inc(S["y_hi_done"], 1)

            def s5(order):
                act.wait_ge(S["par_in"], 16)
                act.wait_ge(S["h_done"], 2 * KT)
                act.wait_ge(S["h_hi_done"], 2 * KT)
                K = lambda i: s5_k[:, i]
                act.activation(K(0), PR("log_dt"), AFT.Exp).then_inc(S["s5_k_ready"], 1)
                for i in range(4):
                    evac(s5_u[:, i], LOT_AT[("u", i)])
                act.wait_ge(S["s5_k_ready"], 2)
                act.activation(K(3), K(1), AFT.Exp).then_inc(S["s5_k_ready"], 1)
                act.wait_ge(S["s5_k_ready"], 4)
                act.activation(K(7), K(5), AFT.Sin, scale=2 * PI).then_inc(S["s5_k_ready"], 1)
                act.activation(K(8), K(6), AFT.Sin, scale=-2 * PI, bias=half_pi[:, :]).then_inc(S["s5_k_ready"], 1)
                for c in range(2):
                    act.wait_ge(S["s5_bbt_psum"], c + 1)
                    act.activation(s5_bbt[:, c].rearrange("p a b -> p (a b)"), bank[4 + c][:, :], AFT.Copy) \
                       .then_inc(S["s5_bbt_ready"], 1)
                for st in range(S5_TILES):
                    act.wait_ge(S["s5_phase"], 2 * (st + 1))
                    e = st % 2
                    act.activation(s5_sin[:, e], s5_ph[:, 2 * e], AFT.Sin, scale=2 * PI).then_inc(S["s5_trig"], 1)
                    act.activation(s5_cos[:, e], s5_ph[:, 2 * e + 1], AFT.Sin, scale=-2 * PI, bias=half_pi[:, :]) \
                       .then_inc(S["s5_trig"], 1)
                for i in range(4):
                    act.wait_ge(S["s5_y_used"], i + 1)
                    if i >= 2:
                        act.wait_ge(S["gel_done"], i - 1)
                    if i == 0:
                        act.wait_ge(S["s5_y_used"], 4)
                    chain(act.activation(gel[:, i % 2], s5_u[:, i], AFT.Gelu_apprx_tanh))
                    act.activation(gel_hi[:, i], gel[:, i % 2], AFT.Copy).then_inc(S["gel_hi_done"], 1)
                for i in range(4):
                    n = LOT_AT[("glu", i)]
                    t = OUT0[n] + 1
                    wait_out(act, t)
                    if i >= 2:
                        act.wait_ge(S["glu_y_done"], i - 1)
                    act.activation(glu_th[:, i % 2], bank[t % 4][:, :], AFT.Tanh, scale=0.5).then_inc(free[t % 4], 1)
                    split_hi(act, n + 4)
                    split_y(i, glu_y[:, i % 2], order, lambda: act.wait_ge(S["glu_y_done"], i + 1), scale=0.5)

            def evac_tokens(dst, n, cols, func=AFT.Copy):
                t = OUT0[n]
                wait_out(act, t)
                src = bank[t % 4][:, :].rearrange("p (b m) -> p b m", m=P)[:, :, 0:cols]
                act.activation(dst, src, func).then_inc(free[t % 4], 1)
                split_hi(act, n + 4)

            def dsa(order):
                if order:
                    act.wait_ge(S["merge_used"], KT * order)
                act.wait_ge(S["h_done"], 2 * KT)
                evac_tokens(small[:, :, :], LOT_AT[("small", 0)], 12)
                for g, w in enumerate("qk"):
                    for i in range(4):
                        evac(da_qk[:, 4 * g + i], LOT_AT[(w, i)])
                for i in range(4):
                    evac_tokens(da_v[:, :, P * i:P * (i + 1)], LOT_AT[("v", i)], P)
                for i in range(2):
                    evac(da_qi[:, i], LOT_AT[("qi", i)])
                evac(da_ki[:, :], LOT_AT[("ki", 0)])
                for g in range(2):
                    if g:
                        act.wait_ge(S["da_rot_done"], 4)
                    wait_taken(act, out_at("qk"[g], 3))
                    for j in range(4):
                        act.activation(da_t[:, j], da_qk[:, 4 * g + j], AFT.Square).then_inc(S["da_sq"], 1)
                    for j in range(4):
                        act.wait_ge(S["da_ms"], 4 * g + j + 1)
                        act.activation(da_t[:, j], bank[4 + j][:, :], AFT.Sqrt, scale=1.0 / 64, bias=epsc[:, :]) \
                           .then_inc(S["da_rms"], 1)
                act.wait_ge(S["da_rot_done"], 8)
                for b in range(1, NB):
                    act.wait_ge(S["da_rel"], b)
                    if b > 1:
                        act.wait_ge(S["da_score"], b - 1)
                    for hh in range(4):
                        act.activation(da_r[:, hh, 0:P * (b + 1)], bank[4 + hh][:, 0:P * (b + 1)], AFT.Relu) \
                           .then_inc(S["da_relu"], 1)

                def exps(u):
                    hp, b, e = UNITS[u]
                    w = P * (b + 1)
                    act.wait_ge(S["da_max"], u + 1)
                    if u >= 2:
                        act.wait_ge(S["da_pt_psum"], u - 1)
                    act.activation(da_p[:, u % 2, 0:w], da_lg[:, u % 2, 0:w], AFT.Exp, scale=0.125,
                                   bias=da_st[:, u, 1:2], accum_out=da_st[:, u, 2:3]).then_inc(S["da_exp"], 1)

                def copy(u):
                    hp, b, e = UNITS[u]
                    w = P * (b + 1)
                    act.wait_ge(S["da_pt_psum"], u + 1)
                    if u >= 2:
                        act.wait_ge(S["da_pv"], u - 1)
                    act.activation(da_pt[:, u % 2, 0:w], bank[6][:, 0:w], AFT.Copy).then_inc(S["da_pt_ready"], 1)
                exps(0)
                for u in range(32):
                    if u < 31:
                        exps(u + 1)
                    copy(u)
                    if u % 8 == 0 and u:
                        split_y(u // 8 - 1, bank[7][:, :], order, lambda: act.wait_ge(S["da_pv"], u))
                split_y(3, bank[7][:, :], order, lambda: act.wait_ge(S["da_pv"], 32))

            def mamba(order):
                if order:
                    act.wait_ge(S["merge_used"], KT * order)
                act.wait_ge(S["h_done"], 2 * KT)
                for i in range(4):
                    evac(m2_z[:, i], LOT_AT[("z", i)], AFT.Silu)
                for i in range(6):
                    evac(m2_xr[:, i, 4:4 + SEQ], LOT_AT[("xbc", i)])
                D = lambda i: m2_dt[:, i]
                act.wait_ge(S["par_in"], 16)
                act.wait_ge(S["m2_dtb"], 2)
                act.activation(D(5)[:, 0], PR("a_log"), AFT.Exp).then_inc(S["m2_abs"], 1)
                chain(act.activation(D(2), D(1), AFT.Exp, scale=-1.0))
                act.activation(D(2), D(2), AFT.Ln, bias=1.0).then_inc(S["m2_abs"], 1)
                for i in range(6):
                    act.wait_ge(S["m2_conv"], i + 1)
                    act.activation(m2_xc[:, i], m2_xc[:, i], AFT.Silu).then_inc(S["m2_silu"], 1)
                for h in range(8):
                    act.wait_ge(S["m2_seg"], h + 1)
                    act.activation(m2_e[:, h % 2], m2_e[:, h % 2], AFT.Exp).then_inc(S["m2_decay"], 1)
                for i in range(BT):
                    act.wait_ge(S["m2_yn"], i + 1)
                    if i >= 2:
                        act.wait_ge(S["m2_ms"], i - 1)
                    act.activation(m2_t[:, i % 2], m2_yv[:, i], AFT.Square).then_inc(S["m2_sq"], 1)
                act.wait_ge(S["m2_ms"], 4)
                act.activation(m2_t[:, 2], bank[4][:, :], AFT.Sqrt, scale=1.0 / BW, bias=epsc[:, :]).then_inc(S["m2_rms"], 1)
                for i in range(BT):
                    split_y(i, m2_yv[:, i], order, lambda: act.wait_ge(S["m2_yn"], BT + i + 1))

            def hgrn(order):
                if order:
                    act.wait_ge(S["merge_used"], KT * order)
                act.wait_ge(S["h_done"], 2 * KT)
                for i in range(4):
                    evac(hq[:, i], LOT_AT[("hq", i)], AFT.Silu)
                for i in range(4):
                    evac(hf[:, i], LOT_AT[("hf", i)])
                for i in range(4):
                    evac_tokens(hv[:, :, P * i:P * (i + 1)], LOT_AT[("hv", i)], P)
                for i in range(4):
                    evac(hg[:, i], LOT_AT[("hg", i)], AFT.Tanh, scale=0.5)
                wait_taken(act, out_at("hf", 3))
                for h in range(4):
                    if h:
                        act.wait_ge(S["hg_ke"], 3 * h)
                    act.activation(he[:, 0], hf[:, h], AFT.Exp, scale=-1.0).then_inc(S["hg_e"], 1)
                    act.activation(he[:, 1], hf[:, h], AFT.Exp).then_inc(S["hg_e"], 1)
                    act.wait_ge(S["hg_fg"], h + 1)
                    act.activation(he[:, 2], he[:, 2], AFT.Ln).then_inc(S["hg_lf"], 1)
                    act.wait_ge(S["hg_cum"], h + 1)
                    act.activation(he[:, 4], he[:, 3], AFT.Exp).then_inc(S["hg_ec"], 1)
                    act.activation(he[:, 5], he[:, 3], AFT.Exp, scale=-1.0).then_inc(S["hg_ec"], 1)
                    if h:
                        act.wait_ge(S["hg_updu"], 4 * h)
                    act.activation(hdec[:, :], he[:, 3, HG_CHUNK - 1::HG_CHUNK], AFT.Exp).then_inc(S["hg_ec"], 1)
                    act.wait_ge(S["hg_lc"], h + 1)
                    act.activation(he[:, 6], he[:, 6], AFT.Exp).then_inc(S["hg_el"], 1)
                    act.wait_ge(S["hg_ket"], h + 1)
                    act.activation(hken[:, :, :].rearrange("p a b -> p (a b)"), bank[5][:, :], AFT.Copy) \
                       .then_inc(S["hg_ken"], 1)
                    act.wait_ge(S["hg_op"], h + 1)
                    act.activation(hf[:, h], bank[5][:, :], AFT.Copy).then_inc(S["hg_o"], 1)
                act.wait_ge(S["hg_o"], 4)
                for h in range(4):
                    if h >= 2:
                        act.wait_ge(S["hg_ms"], h - 1)
                    act.activation(he[:, h % 2], hf[:, h], AFT.Square).then_inc(S["hg_sq"], 1)
                for h in range(4):
                    act.wait_ge(S["hg_ms"], h + 1)
                    act.activation(he[:, 2 + h], bank[4 + h][:, :], AFT.Sqrt, scale=1.0 / P, bias=epsc[:, :]) \
                       .then_inc(S["hg_rms"], 1)
                for h in range(4):
                    split_y(h, he[:, 6 + h], order, lambda: act.wait_ge(S["hg_yn"], h + 1), scale=0.5)

            MIXERS = {0: mamba, 1: s5, 2: dsa, 3: hgrn}

            def mixers():
                for order, g in enumerate(ORDER):
                    MIXERS[g](order)
                    merge(g, order)

            def high_parts_of_merged():
                act.wait_ge(S["merge_used"], KT * len(ORDER))
                for i in range(KT):
                    act.activation(h_hi[:, i], merged[:, i], AFT.Copy).then_inc(S["h_hi_done"], 1)

            for i in range(KT):
                act.wait_ge(S["p_x"], i + 1)
                act.activation(x[:, i], bank[i][:, :], AFT.Copy).then_inc(S["p_xt"], 1)
            act.wait_ge(S["p_ang"], 2)
            act.activation(rope_sin[:, :], ang[:, 0], AFT.Sin).then_inc(S["p_trig"], 1)
            act.activation(rope_cos[:, :], ang[:, 1], AFT.Sin, scale=-1.0, bias=half_pi[:, :]).then_inc(S["p_trig"], 1)
            act.wait_ge(S["p_gam1"], 1)
            act.activation(gtmp[:, 1], gtmp[:, 0], AFT.Exp).then_inc(S["p_trig"], 1)
            with act.Fori(0, DEPTH) as layer:
                seq.n = 0
                for n in range(4):
                    split_hi(act, n)
                norm(0, lambda i: None)
                ffn(0, 0)
                base = OUT0[FFN_LOTS - KT]
                norm(1, lambda i: wait_taken(act, (base + i, 0)))
                mixers()
                high_parts_of_merged()
                for i in range(KT):
                    n = LOT_AT[("out", i)]
                    split_hi(act, n + 4)
                norm(2, lambda i: wait_taken(act, (out_at("out", i), 0)))
                ffn(1, FFN2_0)
                end_of_layer(act, S["go_act"])
            for b in range(NB):
                for half in range(2):
                    act.wait_ge(S["e_x"], 2 * b + half + 1)
                    act.activation(o_nat[:, b, BW * half:BW * (half + 1)], bank[2 * b + half][:, :], AFT.Copy) \
                       .then_inc(S["e_o"], 1)

        @block.vector
        def _(dve):
            seq = Order(dve, S["dve_seq"])
            do, need = seq.do, seq.need
            V = dve

            def norm(r, gain):
                V.wait_ge(S["rms_ready"], r + 1)
                n = do(V.reciprocal(rms[:, :], rms[:, :]))
                need(n)
                h0 = KT * (3 * r // 2)
                if r == 0:
                    V.wait_ge(S["par_in"], 16)

                def low(i):
                    V.wait_ge(S["h_hi_done"], h0 + i + 1)
                    V.tensor_tensor(h_lo[:, i], normed[:, i % 2], h_hi[:, i].bitcast(f32), SUB) \
                     .then_inc(S["h_done"], 1)
                for i in range(KT):
                    if i >= 2:
                        V.wait_ge(S["h_done"], h0 + i - 1)
                    V.scalar_tensor_tensor(normed[:, i % 2], x[:, i], PC(gain, i), rms[:, :], MUL, MUL) \
                     .then_inc(S["normed_ready"], 1)
                    if i:
                        low(i - 1)
                low(KT - 1)

            def ffn(which, nb):
                n, g0 = nb, FF_TILES * which
                for th, J in enumerate(THIRDS):
                    with V.Fori(0, J // 2) as it:
                        for q in range(2):
                            na, nbb = n + 2 * q, n + 2 * q + 1
                            ta, tb = OUT0[na], OUT0[nbb]
                            split_lo(V, na + 4, it)
                            V.wait_ge(free[ta % 4], it + (ta // 4 + 1))
                            V.wait_ge(S["out_done"], it * 4 + (tb + 1))
                            V.tensor_tensor(gated[:, q], silu_a[:, q], bank[tb % 4][:, :], MUL).then_inc(free[tb % 4], 1)
                            split_lo(V, nbb + 4, it)
                            V.wait_ge(S["g_hi_done"], it * 2 + (g0 + q + 1))
                            V.tensor_tensor(g_lo[:, it * 2 + q], gated[:, q], g_hi[:, it * 2 + q].bitcast(f32), SUB) \
                             .then_inc(S["g_done"], 1)
                    n, g0 = n + 2 * J, g0 + J

                    def down(j, it):
                        split_lo(V, n + j + 4, it)
                        t = OUT0[n + j]
                        V.wait_ge(S["out_done"], it * 4 + (t + 1))
                        i = it * 4 + j if not isinstance(it, int) else j
                        V.scalar_tensor_tensor(x[:, i], bank[t % 4][:, :], 0.5, x[:, i], MUL, ADD) \
                         .then_inc(free[t % 4], 1)
                    if nb == FFN2_0 and th == len(THIRDS) - 1:
                        for j in range(KT):
                            down(j, 0)
                    else:
                        with V.Fori(0, 2) as it:
                            for j in range(4):
                                down(j, it)
                    n += KT

            def merge(g, order):
                for i in range(KT):
                    e, pair = i % 2, i // 2
                    tp, tg = out_at("branch%d" % g, pair, e), out_at("gate%d" % g, i)
                    wait_taken(V, tg)
                    wait_out(V, tp)
                    V.scalar_tensor_tensor(gate_th[:, e], gate_th[:, e], 1.0, bank[tp % 4][:, :], ADD, MUL) \
                     .then_inc(free[tp % 4], 1)
                    wait_taken(V, tp)
                    if order == 0:
                        V.tensor_copy(merged[:, i], gate_th[:, e]).then_inc(S["merge_used"], 1)
                    else:
                        V.wait_ge(S["merge_used"], KT * (order - 1) + i + 1)
                        V.tensor_tensor(merged[:, i], merged[:, i], gate_th[:, e], ADD).then_inc(S["merge_used"], 1)
            def chain(ins):
                need(do(ins))

            def s5(order, layer):
                K = lambda i: s5_k[:, i]
                TT, TS, STT = V.tensor_tensor, V.tensor_scalar, V.scalar_tensor_tensor
                V.wait_ge(S["s5_k_ready"], 1)
                chain(TT(K(2), PR("lam_im"), K(0), MUL))
                TT(K(1), PR("lam_re"), K(0), MUL).then_inc(S["s5_k_ready"], 1)
                chain(TS(K(2), K(2), 1.0 / (2 * PI), None, MUL))
                chain(TS(K(4), K(2), ROUND, -ROUND, ADD, ADD))
                chain(TT(K(5), K(2), K(4), SUB))
                V.wait_ge(S["s5_k_ready"], 3)
                STT(K(6), K(5), -1.0, K(5), MUL, ALU.max).then_inc(S["s5_k_ready"], 1)
                chain(TS(K(9), K(5), ROUND13, -ROUND13, ADD, ADD))
                do(TT(K(10), K(5), K(9), SUB))
                V.wait_ge(S["s5_k_ready"], 6)
                do(TT(K(11), K(3), K(8), MUL))
                chain(TT(K(12), K(3), K(7), MUL))
                do(TS(K(13), K(11), -1.0, None, ADD))
                do(TT(K(14), PR("lam_re"), PR("lam_re"), MUL))
                chain(TT(K(15), PR("lam_im"), PR("lam_im"), MUL))
                chain(TT(K(14), K(14), K(15), ADD))
                do(V.reciprocal(K(14), K(14)))
                do(TT(K(15), K(13), PR("lam_re"), MUL))
                chain(TT(K(16), K(12), PR("lam_im"), MUL))
                do(TT(K(15), K(15), K(16), ADD))
                do(TT(K(17), K(12), PR("lam_re"), MUL))
                chain(TT(K(18), K(13), PR("lam_im"), MUL))
                chain(TT(K(17), K(17), K(18), SUB))
                do(TT(K(19), K(15), K(14), MUL))
                chain(TT(K(20), K(17), K(14), MUL))
                V.wait_ge(S["s5_in"], 16)
                qre, qim = (K(c).unsqueeze(2).broadcast_to([P, 16, 32]) for c in (19, 20))
                T = lambda i: s5_pr[:, i].rearrange("p (s c) -> p s c", c=32)
                do(TT(T(0), s5_bc[:, 0], qre, MUL))
                do(TT(T(1), s5_bc[:, 1], qim, MUL))
                do(TT(T(2), s5_bc[:, 1], qre, MUL))
                chain(TT(T(3), s5_bc[:, 0], qim, MUL))
                TT(s5_bb[:, 0], T(0), T(1), SUB).then_inc(S["s5_bb_ready"], 1)
                TT(s5_bb[:, 1], T(2), T(3), ADD).then_inc(S["s5_bb_ready"], 1)
                chain(TS(s5_bc[:, 3], s5_bc[:, 3], -1.0, None, MUL))
                V.wait_ge(S["s5_bb_ready"], 2)
                tv = C("tvec")

                def phases(st):
                    e, k1 = st % 2, slice(st, st + 1)
                    f, fa = s5_ph[:, 2 * e], s5_ph[:, 2 * e + 1]
                    if st >= 2:
                        V.wait_ge(S["s5_trig"], 2 * (st - 1))
                    do(TS(f, tv, K(9)[:, k1], None, MUL))
                    chain(TS(fa, tv, K(5)[:, k1], ROUND, MUL, ADD))
                    chain(STT(f, fa, -ROUND, f, ADD, SUB))
                    chain(STT(f, tv, K(10)[:, k1], f, MUL, SUB))
                    TS(f, f, 0.5, -0.5, ALU.min, ALU.max).then_inc(S["s5_phase"], 1)
                    V.wait_ge(S["s5_phase"], 2 * st + 1)
                    STT(fa, f, -1.0, f, MUL, ALU.max).then_inc(S["s5_phase"], 1)

                def states(st):
                    e = st % 2
                    re, im, cs, sn = bank[4][:, :], bank[5][:, :], s5_cos[:, e], s5_sin[:, e]
                    pr = [s5_pr[:, i] for i in range(4)]
                    V.wait_ge(S["s5_bu"], st + 1)
                    V.wait_ge(S["s5_trig"], 2 * (st + 1))
                    if st:
                        V.wait_ge(S["s5_state"], 2 * st)
                    do(TT(pr[0], re, cs, MUL))
                    n = do(TT(pr[1], im, sn, MUL))
                    do(TT(pr[2], im, cs, MUL))
                    TT(pr[3], re, sn, MUL).then_inc(S["s5_bu_used"], 1)
                    need(n)
                    n = do(TT(s5_v[:, 0], pr[0], pr[1], ADD))
                    V.wait_ge(S["s5_bu_used"], st + 1)
                    m = do(TT(s5_v[:, 1], pr[2], pr[3], SUB))
                    mag = K(3)[:, st:st + 1].broadcast_to([P, SEQ])
                    need(n)
                    n = do(V.tensor_tensor_scan(s5_z[:, 0], mag, s5_v[:, 0], 0.0, MUL, ADD))
                    need(m)
                    m = do(V.tensor_tensor_scan(s5_z[:, 1], mag, s5_v[:, 1], 0.0, MUL, ADD))
                    need(n)
                    do(TT(pr[0], s5_z[:, 0], cs, MUL))
                    do(TT(pr[2], s5_z[:, 0], sn, MUL))
                    need(m)
                    n = do(TT(pr[1], s5_z[:, 1], sn, MUL))
                    m = do(TT(pr[3], s5_z[:, 1], cs, MUL))
                    if st >= 2:
                        V.wait_ge(S["s5_y"], st - 1)
                    need(n)
                    TT(s5_s[:, e, 0], pr[0], pr[1], SUB).then_inc(S["s5_state"], 1)
                    need(m)
                    TT(s5_s[:, e, 1], pr[2], pr[3], ADD).then_inc(S["s5_state"], 1)

                def skip(jt):
                    V.wait_ge(S["s5_y"], 4 * (jt + 1))
                    STT(s5_u[:, jt], s5_u[:, jt], PC("s5_d", jt), bank[6][:, :], MUL, ADD).then_inc(S["s5_y_used"], 1)
                phases(0)
                for st in range(S5_TILES):
                    if st + 1 < S5_TILES:
                        phases(st + 1)
                    states(st)
                    if st % 4 == 1 and st > 4:
                        skip(st // 4 - 1)
                skip(3)
                for i in range(4):
                    V.wait_ge(S["gel_hi_done"], i + 1)
                    TT(gel_lo[:, i], gel[:, i % 2], gel_hi[:, i].bitcast(f32), SUB).then_inc(S["gel_done"], 1)
                for i in range(4):
                    n = LOT_AT[("glu", i)]
                    t = OUT0[n]
                    wait_out(V, t)
                    wait_taken(V, t + 1)
                    if i >= 2:
                        V.wait_ge(S["y_done"], 4 * order + i - 1)
                    STT(glu_y[:, i % 2], glu_th[:, i % 2], 1.0, bank[t % 4][:, :], ADD, MUL).then_inc(free[t % 4], 1)
                    wait_taken(V, t)
                    V.sem_inc(S["glu_y_done"], 1)
                    V.wait_ge(S["y_hi_done"], 4 * order + i + 1)
                    STT(y_lo[:, i], glu_y[:, i % 2], 0.5, y_hi[:, i].bitcast(f32), MUL, SUB).then_inc(S["y_done"], 1)

            TT, TS, STT = V.tensor_tensor, V.tensor_scalar, V.scalar_tensor_tensor

            def low_y(i, src, order, scale=None):
                V.wait_ge(S["y_hi_done"], BT * order + i + 1)
                hi = y_hi[:, i].bitcast(f32)
                ins = TT(y_lo[:, i], src, hi, SUB) if scale is None else STT(y_lo[:, i], src, scale, hi, MUL, SUB)
                ins.then_inc(S["y_done"], 1)

            def dsa(order, layer):
                wait_taken(V, out_at("k", 3))
                for g, gain in enumerate(("q_norm", "k_norm")):
                    for j in range(4):
                        V.wait_ge(S["da_rms"], 4 * g + j + 1)
                        chain(V.reciprocal(da_t[:, j], da_t[:, j]))
                        STT(da_qk[:, 4 * g + j], da_qk[:, 4 * g + j], PR(gain), da_t[:, j], MUL, MUL) \
                            .then_inc(S["da_qn"], 1)
                    for j in range(4):
                        V.wait_ge(S["da_rot"], 4 * g + j + 1)
                        V.wait_ge(S["da_qn"], 4 * g + j + 1)
                        do(TT(da_t[:, j], bank[4 + j][:, :], rope_sin[:, :], MUL))
                        chain(TT(da_qk[:, 4 * g + j], da_qk[:, 4 * g + j], rope_cos[:, :], MUL))
                        TT(da_qk[:, 4 * g + j], da_qk[:, 4 * g + j], da_t[:, j], ADD).then_inc(S["da_rot_done"], 1)
                chain(V.tensor_copy(da_mb[:, 0:P], C("cmask")))
                wait_taken(V, out_at("small", 0))
                for b in range(1, NB):
                    w = P * (b + 1)
                    for hh in range(4):
                        V.wait_ge(S["da_relu"], 4 * (b - 1) + hh + 1)
                        sc, r, wi = da_sc[:, 0:w], da_r[:, hh, 0:w], small[:, b, hh:hh + 1]
                        if hh == 0:
                            chain(TS(sc, r, wi, None, MUL))
                        elif hh < 3:
                            chain(STT(sc, r, wi, sc, MUL, ADD))
                        else:
                            STT(sc, r, wi, sc, MUL, ADD).then_inc(S["da_score"], 1)
                    V.wait_ge(S["da_score"], b)
                    chain(TT(da_sc[:, P * b:w], da_sc[:, P * b:w], C("cmask"), ADD))
                    src = da_sc
                    for r in range(TOPK // 8):
                        chain(V.max(da_m8[:, :], src[:, 0:w]))
                        chain(V.match_replace(da_wk[:, 0:w], da_m8[:, :], src[:, 0:w], TAKEN))
                        src = da_wk
                    chain(TS(da_mb[:, DA_OFF[b]:DA_OFF[b] + w], da_wk[:, 0:w], -2.0e38, NEG, ALU.is_gt, MUL))

                def masked(u):
                    hp, b, e = UNITS[u]
                    w = P * (b + 1)
                    V.wait_ge(S["da_logit"], u + 1)
                    if u >= 2:
                        V.wait_ge(S["da_exp"], u - 1)
                    chain(V.tensor_tensor_reduce(out=da_lg[:, u % 2, 0:w], in0=bank[4 + u % 2][:, 0:w],
                                                 in1=da_mb[:, DA_OFF[b]:DA_OFF[b] + w], scale=1.0, scalar=TAKEN,
                                                 op0=ADD, op1=ALU.max, accum_out=da_st[:, u, 0:1]))
                    TS(da_st[:, u, 1:2], da_st[:, u, 0:1], -0.125, None, MUL).then_inc(S["da_max"], 1)

                def normalise(u):
                    hp, b, e = UNITS[u]
                    w = P * (b + 1)
                    V.wait_ge(S["da_exp"], u + 1)
                    chain(V.reciprocal(da_st[:, u, 3:4], da_st[:, u, 2:3]))
                    TS(da_p[:, u % 2, 0:w], da_p[:, u % 2, 0:w], da_st[:, u, 3:4], None, MUL).then_inc(S["da_prob"], 1)
                masked(0)
                for u in range(32):
                    if u < 31:
                        masked(u + 1)
                    normalise(u)
                    if u % 8 == 1 and u > 8:
                        low_y(u // 8 - 1, bank[7][:, :], order)
                low_y(3, bank[7][:, :], order)

            def mamba(order, layer):
                D = lambda i: m2_dt[:, i]
                heads = lambda a: a.unsqueeze(1).broadcast_to([P, NB, 8])
                if order:
                    V.wait_ge(S["merge_used"], KT * order)
                V.wait_ge(S["h_done"], 2 * KT)
                chain(V.memset(m2_xr[:, :, 0:4], 0.0))
                wait_taken(V, out_at("small", 0) if ("small", 0) in LOT_AT else out_at("z", 0))
                TT(D(0), small[:, :, 4:12], heads(PR("dt_bias")), ADD).then_inc(S["m2_dtb"], 1)
                V.wait_ge(S["m2_dtb"], 1)
                STT(D(1), D(0), -1.0, D(0), MUL, ALU.max).then_inc(S["m2_dtb"], 1)
                n = {}
                for k in (3, 2, 1, 0):
                    for i in range(6):
                        xs, wk = m2_xr[:, i, 1 + k:1 + k + SEQ], PC("conv_w", 6 * k + i)
                        if k == 3:
                            wait_taken(V, out_at("xbc", i))
                            n[i] = do(TS(m2_xc[:, i], xs, wk, PC("conv_b", i), MUL, ADD))
                        else:
                            need(n[i])
                            ins = STT(m2_xc[:, i], xs, wk, m2_xc[:, i], MUL, ADD)
                            if k:
                                n[i] = do(ins)
                            else:
                                ins.then_inc(S["m2_conv"], 1)
                V.wait_ge(S["m2_abs"], 2)
                chain(STT(D(3), D(0), 0.0, D(2), ALU.max, ADD))
                STT(D(4), D(3), -1.0, heads(D(5)[:, 0]), MUL, MUL).then_inc(S["m2_dt_ready"], 1)
                V.wait_ge(S["m2_acs"], 1)
                V.tensor_copy(D(0).rearrange("p b h -> p (b h)"), bank[4][:, 0:32]).then_inc(S["m2_acs_done"], 1)
                V.wait_ge(S["m2_acs_done"], 1)
                for b in range(NB):
                    V.wait_ge(S["m2_ct"], b + 1)
                    TT(m2_xdt[:, b].rearrange("p (h d) -> p h d", d=64),
                       bank[5 + b % 2][:, :].rearrange("p (h d) -> p h d", d=64),
                       D(3)[:, b].unsqueeze(2).broadcast_to([P, 8, 64]), MUL).then_inc(S["m2_xdt_done"], 1)
                for c in range(8):
                    g, j = c // 4, c % 4
                    V.wait_ge(S["m2_cbp"], c + 1)
                    w = SEQ - P * j
                    TT(m2_cb[:, g, M2_OFF[j]:M2_OFF[j] + w], bank[4 + 3 * (c % 2)][:, 0:w], C("upper", 0, w), MUL) \
                        .then_inc(S["m2_cb_done"], 1)
                V.wait_ge(S["m2_cb_done"], 8)

                def segments(h):
                    V.wait_ge(S["m2_acb"], h + 1)
                    if h >= 2:
                        V.wait_ge(S["m2_yp"], h - 1)
                    for j in range(NB):
                        ins = TS(m2_e[:, h % 2, M2_OFF[j]:M2_OFF[j] + SEQ - P * j], bank[4 + h % 2][:, P * j:SEQ],
                                 D(0)[:, j, h:h + 1], 0.0, SUB, ALU.min)
                        if j < NB - 1:
                            do(ins)
                    ins.then_inc(S["m2_seg"], 1)

                def y_of(hp):
                    V.wait_ge(S["m2_yp"], 2 * hp + 2)
                    STT(m2_yv[:, hp], m2_xc[:, hp], PC("m2_d", hp), bank[6 + hp % 2][:, :], MUL, ADD) \
                        .then_inc(S["m2_y"], 1)
                segments(0)
                for h in range(8):
                    if h < 7:
                        segments(h + 1)
                    V.wait_ge(S["m2_decay"], h + 1)
                    TT(m2_e[:, h % 2], m2_e[:, h % 2], m2_cb[:, h // 4], MUL).then_inc(S["m2_m"], 1)
                    if h >= 2 and h % 2 == 0:
                        y_of(h // 2 - 1)
                y_of(3)
                for i in range(BT):
                    V.wait_ge(S["m2_y"], i + 1)
                    TT(m2_yv[:, i], m2_yv[:, i], m2_z[:, i], MUL).then_inc(S["m2_yn"], 1)
                V.wait_ge(S["m2_rms"], 1)
                chain(V.reciprocal(m2_t[:, 2], m2_t[:, 2]))
                for i in range(BT):
                    STT(m2_yv[:, i], m2_yv[:, i], PC("m2_norm", i), m2_t[:, 2], MUL, MUL).then_inc(S["m2_yn"], 1)
                for i in range(BT):
                    low_y(i, m2_yv[:, i], order)

            def hgrn(order, layer):
                if order:
                    V.wait_ge(S["merge_used"], KT * order)
                V.wait_ge(S["h_done"], 2 * KT)
                do(V.memset(hatt[:, :, :], 0.0))
                chain(V.tensor_copy(hlb[:, 0], lower[:, layer]))
                chain(TS(hlb[:, 1], hlb[:, 0], -1.0, 1.0, MUL, ADD))
                E = lambda i: he[:, i]
                chunks = lambda a: a.rearrange("p (c t) -> p c t", t=HG_CHUNK)
                for h in range(4):
                    lb, oml = hlb[:, 0, h:h + 1], hlb[:, 1, h:h + 1]
                    if h:
                        V.wait_ge(S["hg_ke"], 3 * h)
                        V.wait_ge(S["hg_op"], h)
                    V.wait_ge(S["hg_e"], 2 * h + 2)
                    do(TS(E(0), E(0), 1.0, None, ADD))
                    chain(TS(E(1), E(1), 1.0, None, ADD))
                    n = do(V.reciprocal(E(0), E(0)))
                    m = do(V.reciprocal(E(1), E(1)))
                    need(n)
                    TS(E(2), E(0), oml, lb, MUL, ADD).then_inc(S["hg_fg"], 1)
                    need(m)
                    chain(TS(E(1), E(1), oml, None, MUL))
                    V.wait_ge(S["hg_lf"], h + 1)
                    V.tensor_tensor_scan(E(3), C("hgreset"), E(2), 0.0, MUL, ADD).then_inc(S["hg_cum"], 1)
                    V.wait_ge(S["hg_cum"], h + 1)
                    TT(chunks(E(6)), chunks(E(3))[:, :, HG_CHUNK - 1:HG_CHUNK].broadcast_to([P, NCH, HG_CHUNK]),
                       chunks(E(3)), SUB).then_inc(S["hg_lc"], 1)
                    V.wait_ge(S["hg_ec"], 3 * h + 3)
                    wait_taken(V, out_at("hq", h))
                    TT(E(7), hq[:, h], E(4), MUL).then_inc(S["hg_ke"], 1)
                    TT(E(8), E(1), E(5), MUL).then_inc(S["hg_ke"], 1)
                    V.wait_ge(S["hg_el"], h + 1)
                    TT(E(9), E(1), E(6), MUL).then_inc(S["hg_ke"], 1)
                    V.wait_ge(S["hg_attp"], h + 1)
                    V.copy_predicated(hatt[:, :, :], C("hgmask").bitcast(u32).unsqueeze(1).broadcast_to([P, NB, P]),
                                      bank[4][:, :].rearrange("p (b q) -> p b q", q=P)).then_inc(S["hg_att"], 1)
                    for c in range(NCH - 1):
                        if c == 0:
                            V.wait_ge(S["hg_upd"], 4 * h + 4)
                        new = bank[4 + c % 4][:, P * (c // 4):P * (c // 4 + 1)]
                        if c == 0:
                            ins = V.tensor_copy(hS[:, 1], new)
                        else:
                            ins = STT(hS[:, c + 1], hS[:, c], hdec[:, c:c + 1], new, MUL, ADD)
                        if c % 4 == 3 or c == NCH - 2:
                            ins.then_inc(S["hg_updu"], 1)
                            V.wait_ge(S["hg_updu"], 4 * h + c // 4 + 1)
                        else:
                            chain(ins)
                for h in range(4):
                    V.wait_ge(S["hg_rms"], h + 1)
                    chain(V.reciprocal(E(2 + h), E(2 + h)))
                    chain(STT(hf[:, h], hf[:, h], PC("hg_norm", h), E(2 + h), MUL, MUL))
                    wait_taken(V, out_at("hg", h))
                    STT(E(6 + h), hg[:, h], 1.0, hf[:, h], ADD, MUL).then_inc(S["hg_yn"], 1)
                for h in range(4):
                    low_y(h, E(6 + h), order, 0.5)

            MIXERS = {0: mamba, 1: s5, 2: dsa, 3: hgrn}

            def mixers(layer):
                for order, g in enumerate(ORDER):
                    MIXERS[g](order, layer)
                    merge(g, order)

            V.memset(epsc[:, :], EPS).then_inc(S["p_seq"], 1)
            V.memset(half_pi[:, :], PI / 2).then_inc(S["p_seq"], 1)
            p = Order(V, S["p_seq"])
            p.n = 2

            def pdo(ins):
                p.need(p.do(ins))
            V.wait_ge(S["c_pos"], 16)
            V.wait_ge(S["c_con"], 16)
            pdo(V.tensor_copy(ang[:, 2], pos_i[:, :]))
            pdo(V.tensor_scalar(ang[:, 0], ang[:, 2], C("invfreq"), None, MUL))
            pdo(V.tensor_scalar(ang[:, 1], ang[:, 0], 1.0 / (2 * PI), ROUND, MUL, ADD))
            pdo(V.tensor_scalar(ang[:, 1], ang[:, 1], -ROUND, None, ADD))
            c1 = 6.28125
            c2 = float(np.float32(2 * PI - c1))
            c3 = 2 * PI - c1 - c2
            for c in (c1, c2, c3):
                pdo(V.scalar_tensor_tensor(ang[:, 0], ang[:, 1], -c, ang[:, 0], MUL, ADD))
            V.tensor_scalar(ang[:, 0], ang[:, 0], float(np.float32(3.1415925)), -float(np.float32(3.1415925)), ALU.min, ALU.max) \
             .then_inc(S["p_ang"], 1)
            V.wait_ge(S["p_ang"], 1)
            V.scalar_tensor_tensor(ang[:, 1], ang[:, 0], -1.0, ang[:, 0], MUL, ALU.max).then_inc(S["p_ang"], 1)
            V.wait_ge(S["c_gam"], 16)
            pdo(V.tensor_copy(gtmp[:, 2, 0], gam[:, 0]))
            for l in range(1, DEPTH):
                pdo(V.tensor_tensor(gtmp[:, 2, 0], gtmp[:, 2, 0], gam[:, l], ALU.max))
            for l in range(DEPTH):
                ins = V.tensor_tensor(gtmp[:, 0, l], gam[:, l], gtmp[:, 2, 0], SUB)
                if l < DEPTH - 1:
                    pdo(ins)
            ins.then_inc(S["p_gam1"], 1)
            V.wait_ge(S["p_trig"], 3)
            pdo(V.tensor_copy(gtmp[:, 3, 0], gtmp[:, 1, 0]))
            for l in range(1, DEPTH):
                pdo(V.tensor_tensor(gtmp[:, 3, 0], gtmp[:, 3, 0], gtmp[:, 1, l], ADD))
            pdo(V.reciprocal(gtmp[:, 3, 0], gtmp[:, 3, 0]))
            pdo(V.memset(lower[:, 0], 0.0))
            for l in range(1, DEPTH):
                pdo(V.tensor_tensor(gtmp[:, 4, 0], gtmp[:, 1, l], gtmp[:, 3, 0], MUL))
                pdo(V.tensor_tensor(lower[:, l], lower[:, l - 1], gtmp[:, 4, 0], ADD))
            V.sem_inc(S["p_gam2"], 1)
            with V.Fori(0, DEPTH) as layer:
                seq.n = 0
                for n in range(4):
                    split_lo(V, n)
                norm(0, "ffn1_norm")
                ffn(0, 0)
                norm(1, "mix_norm")
                mixers(layer)
                for i in range(KT):
                    V.wait_ge(S["merge_used"], KT * len(ORDER))
                    V.wait_ge(S["h_hi_done"], KT * 2 + i + 1)
                    V.tensor_tensor(h_lo[:, i], merged[:, i], h_hi[:, i].bitcast(f32), SUB).then_inc(S["h_done"], 1)
                for i in range(KT):
                    t = out_at("out", i)
                    wait_out(V, t)
                    V.scalar_tensor_tensor(x[:, i], bank[t % 4][:, :], 0.5, x[:, i], MUL, ADD).then_inc(free[t % 4], 1)
                norm(2, "ffn2_norm")
                V.wait_ge(S["lo_done"], FFN2_0 + 4)
                ffn(1, FFN2_0)
                end_of_layer(V, S["go_dve"])


def kernel(**inputs):
    import numpy as _np
    import concourse.bacc as _bacc
    from concourse import mybir as _mybir
    from concourse.bass_utils import run_bass_kernel_spmd as _run

    a = {k: _np.asarray(v) for k, v in inputs.items()}

    def lots(w):
        L, K, M = w.shape
        pad = -M % P
        if pad:
            w = _np.concatenate([w, _np.zeros((L, K, pad), w.dtype)], 2)
        return w.reshape(L, K // P, P, (M + pad) // P, P).transpose(0, 3, 2, 1, 4)

    def ffn_lots(w1, w3, w2):
        w1, w3, got, j0 = lots(w1), lots(w3), [], 0
        for J in THIRDS:
            for j in range(j0, j0 + J):
                got += [w1[:, j], w3[:, j]]
            w = lots(w2[:, P * j0:P * (j0 + J)])
            fill = _np.zeros((DEPTH, P, 8 - J, P), w.dtype)
            for i in range(KT):
                got.append(_np.concatenate([w[:, i], fill], 2))
            j0 += J
        return got

    w_in = a["w_in"]
    m2, s5, da = 0, 2 * BW + 256 + 8, 3 * BW + 256 + 8
    hg = da + 3 * BW + 256 + 64 + 4
    parts = dict(z=lots(w_in[:, :, 0:BW]), xbc=lots(w_in[:, :, BW:2 * BW + 256]), u=lots(w_in[:, :, s5:s5 + BW]),
                 q=lots(w_in[:, :, da:da + BW]), k=lots(w_in[:, :, da + BW:da + 2 * BW]),
                 v=lots(w_in[:, :, da + 2 * BW:da + 3 * BW]), qi=lots(w_in[:, :, da + 3 * BW:da + 3 * BW + 256]))
    ki = w_in[:, :, da + 3 * BW + 256:da + 3 * BW + 320]
    parts["ki"] = lots(_np.concatenate([ki, ki], 2))
    parts["small"] = lots(_np.concatenate([w_in[:, :, hg - 4:hg], w_in[:, :, s5 - 8:s5]], 2))
    for i, name in enumerate(("hq", "hf", "hv", "hg")):
        parts[name] = lots(w_in[:, :, hg + BW * i:hg + BW * (i + 1)])
    for g in range(4):
        parts["gate%d" % g] = lots(a["w_gate"][:, :, DM * g:DM * (g + 1)])
        w = lots(a["w_branch"][:, g])
        parts["branch%d" % g] = _np.concatenate([w[:, 0::2], w[:, 1::2]], 3)
    w = lots(a["s5_w_glu"])
    parts["glu"] = _np.concatenate([w[:, 0:4], w[:, 4:8]], 3)
    parts["out"] = lots(a["w_out"])
    stream = ffn_lots(a["ffn1_w1"], a["ffn1_w3"], a["ffn1_w2"]) + [parts[kind][:, i] for kind, i in MIX] \
        + ffn_lots(a["ffn2_w1"], a["ffn2_w3"], a["ffn2_w2"])
    w_lots = _np.stack(stream, 1).reshape(DEPTH * NLOT, P, 8 * P)

    def cols(v):
        return v.reshape(DEPTH, -1, P).transpose(0, 2, 1)

    def rows(v):
        return _np.repeat(v[:, None, :], P, 1)

    par = dict(ffn1_norm=cols(a["ffn1_norm"]), mix_norm=cols(a["mix_norm"]), ffn2_norm=cols(a["ffn2_norm"]),
               conv_w=_np.concatenate([cols(a["m2_conv_w"][:, k]) for k in range(4)], 2), conv_b=cols(a["m2_conv_b"]),
               dt_bias=rows(a["m2_dt_bias"]), a_log=rows(a["m2_a_log"]), m2_d=cols(_np.repeat(a["m2_d"], 64, 1)),
               m2_norm=cols(a["m2_norm"]), lam_re=cols(a["s5_lam_re"].reshape(DEPTH, -1)),
               lam_im=cols(a["s5_lam_im"].reshape(DEPTH, -1)), log_dt=cols(_np.repeat(a["s5_log_dt"], 64, 1)),
               s5_d=cols(a["s5_d"]), q_norm=cols(_np.tile(a["dsa_q_norm"], 2)), k_norm=cols(_np.tile(a["dsa_k_norm"], 2)),
               hg_norm=cols(a["hg_norm"]))
    par = _np.concatenate([par[k] for k in PAR_SIZES], 2)

    s5_in = _np.zeros((DEPTH, P, 4, 16, 32), _np.float32)
    for i, (name, perm) in enumerate((("s5_b_re", None), ("s5_b_im", None), ("s5_c_re", 1), ("s5_c_im", 1))):
        v = a[name] if perm is None else a[name].transpose(0, 1, 3, 2)
        v = v.reshape(DEPTH, 16, 2, 64, 16)
        for e in range(2):
            s5_in[:, 64 * e:64 * e + 64, i, :, 16 * e:16 * e + 16] = v[:, :, e].transpose(0, 2, 1, 3)

    con = _np.zeros((P, NCON), _np.float32)
    r = _np.arange(P)

    def put(name, v):
        con[:, CON_AT[name]:CON_AT[name] + CON_SIZES[name]] = v
    t = _np.arange(SEQ)
    put("ident", _np.eye(P))
    put("upper", t[None, :] >= r[:, None])
    put("blk", r[:, None] // 64 == r[None, :] // 64)
    put("rot", -1.0 * ((r[None, :] % 64 < 32) & (r[:, None] == r[None, :] + 32))
        + ((r[None, :] % 64 >= 32) & (r[:, None] == r[None, :] - 32)))
    put("hgmask", (r[:, None] // HG_CHUNK == r[None, :] // HG_CHUNK) & (r[:, None] <= r[None, :]))
    put("hgreset", (t % HG_CHUNK != 0)[None, :])
    put("tvec", t[None, :])
    put("cmask", _np.where(r[None, :] <= r[:, None], 0.0, NEG))
    put("invfreq", (_np.float32(10000.0) ** (-(r % 32).astype(_np.float32) / _np.float32(32)))[:, None])

    gamma = a["hg_gamma"].reshape(DEPTH, 4, P).transpose(2, 0, 1)
    arrays = dict(x=a["x"].reshape(SEQ, DM), positions=a["positions"].reshape(SEQ), w_lots=w_lots, par=par,
                  s5=s5_in.reshape(DEPTH, P, 2048), con=con, gamma=gamma)
    nc = _bacc.Bacc("TRN2", target_bir_lowering=False, num_devices=1)
    args, feed = [], {}
    for name, v in arrays.items():
        feed["in_" + name] = _np.ascontiguousarray(v)
        args.append(nc.dram_tensor("in_" + name, v.shape, _mybir.dt.from_np(v.dtype), kind="ExternalInput").ap())
    args.append(nc.dram_tensor("out_x", (SEQ, DM), _mybir.dt.float32, kind="ExternalOutput").ap())
    trunk(nc, *args)
    r = _run(nc, [feed], core_ids=[0])
    return r.results[0]["out_x"].reshape(1, SEQ, DM)
```

```python
import math
import numpy as np
import concourse.bass as bass
from concourse import mybir
from contextlib import ExitStack

DEPTH, SEQ, DM, DFF = 2, 512, 1024, 2816
BW = DM // 2
P = 128
KT = DM // P
NB = SEQ // P
BT = BW // P
EPS = 1e-6
TOPK = min(256, SEQ // 4)
HG_CHUNK = 32
NCH = SEQ // HG_CHUNK
S5_TILES = 16
PI = math.pi
ROUND = 12582912.0
ROUND13 = 1536.0
NEG = -1.0e30
TAKEN = -3.0e38

FF_TILES = DFF // P
THIRDS = [8, 8, 6]
FFN_LOTS = 2 * FF_TILES + KT * len(THIRDS)


ORDER = (1, 2, 0, 3)
TURN = {g: i for i, g in enumerate(ORDER)}


def script():
    def lots(*kinds):
        return [("lot", k, i) for k, n in kinds for i in range(n)]

    def weave(steps, fill):
        out, used = [], 0
        for i, step in enumerate(steps):
            out.append(step)
            upto = (i + 1) * len(fill) // len(steps)
            out += fill[used:upto]
            used = upto
        return out

    def phases(name, i, n=3):
        return [(name, i, phase) for phase in range(n)]

    def merges(g, a=0, b=KT // 2):
        return [step for pair in range(a, b)
                for step in (("gate", g, 2 * pair), ("gate", g, 2 * pair + 1), ("branch", g, pair))]

    def glus(a, b):
        return [("glu", i) for i in range(a, b)]
    s = [("s5_prep", 0)] + lots(("u", 4), ("small", 1)) + [("s5_prep", 1)]
    s += weave([("s5", st) for st in range(S5_TILES)], lots(("q", 4), ("k", 4), ("qi", 2), ("ki", 1)) + [("pair", "v", 0)])
    s += [("s5_end",), ("da_norm", 0, 0), ("pair", "v", 2), ("da_norm", 0, 1)] + glus(0, 2)
    s += [("da_norm", 1, 0)] + glus(2, 4) + merges(1, 0, 1) + [("da_norm", 1, 1)]
    s += weave([("da_index", 1), ("da_topk", 1), ("da_index", 2), ("da_topk", 2), ("da_index", 3), ("da_topk", 3)],
               merges(1, 1, 4))
    s += [("att_start",)] + weave([("att", u) for u in range(32)], lots(("xbc", 6))) + [("att_end",)]
    s += [("m2_dt",)] + lots(("z", 4)) + [("m2_conv",)] + merges(2, 0, 1) + [("m2_prep",)]
    s += weave([("m2_head", h) for h in range(8)], merges(2, 1, 4)) + [("m2_norm",)]
    s += lots(("hf", 4), ("hq", 2)) + [("m2_end",), ("lot", "hq", 2), ("lot", "hq", 3), ("hg_start",)]
    s += weave(phases("hg_gates", 0), [("pair", "hv", 0), ("pair", "hv", 2)] + lots(("hg", 1)))
    steps = []
    for h in range(4):
        work, gates = phases("hg_head", h), phases("hg_gates", h + 1) if h < 3 else []
        steps += [step for i in range(3) for step in work[i:i + 1] + gates[i:i + 1]]
    s += weave(steps, [("lot", "hg", i) for i in (1, 2, 3)] + merges(0))
    s += [("hg_norm",)] + merges(3) + [("out_start",)] + [("out", i) for i in range(KT)]
    return s


SCRIPT = script()


def mix_lots():
    lots = []
    for step in SCRIPT:
        if step[0] == "lot":
            lots.append(step[1:])
        elif step[0] == "pair":
            lots += [(step[1], step[2]), (step[1], step[2] + 1)]
        elif step[0] in ("glu", "out"):
            lots.append(step)
        elif step[0] in ("gate", "branch"):
            lots.append((step[0] + str(step[1]), step[2]))
    return lots


MIX = mix_lots()
MIX_LOTS = len(MIX)
NLOT = 2 * FFN_LOTS + MIX_LOTS
MIX0, FFN2_0 = FFN_LOTS, FFN_LOTS + MIX_LOTS


def outputs_of(kind):
    return 2 if kind == "glu" or kind.startswith("branch") else 1


OUT0 = [0]
for _n in range(NLOT):
    _mixing = FFN_LOTS <= _n < FFN_LOTS + MIX_LOTS
    OUT0.append(OUT0[-1] + (outputs_of(MIX[_n - FFN_LOTS][0]) if _mixing else 1))
USED_AT = [OUT0[_n + 1] for _n in range(NLOT)]
for _i, (_kind, _j) in enumerate(MIX):
    if _kind in ("v", "hv") and _j % 2 == 0:
        USED_AT[MIX0 + _i] += 1
        assert (MIX0 + _i) % 4 != 3, (_kind, _j, (MIX0 + _i) % 4)
LOT_AT = {MIX[_i]: MIX0 + _i for _i in range(MIX_LOTS)}


def out_at(kind, i, half=0):
    return OUT0[LOT_AT[(kind, i)]] + half


PAR_SIZES = dict(ffn1_norm=8, mix_norm=8, ffn2_norm=8, conv_w=24, conv_b=6, dt_bias=8, a_log=8, m2_d=4,
                 m2_norm=4, lam_re=16, lam_im=16, log_dt=16, s5_d=4, q_norm=1, k_norm=1, hg_norm=4)
PAR_AT, NPAR = {}, 0
for _name, _n in PAR_SIZES.items():
    PAR_AT[_name] = NPAR
    NPAR += _n
CON_SIZES = dict(ident=128, upper=512, blk=128, rot=128, hgmask=128, hgreset=512, tvec=512, cmask=128,
                 invfreq=1)
CON_AT, NCON = {}, 0
for _name, _n in CON_SIZES.items():
    CON_AT[_name] = NCON
    NCON += _n
UNITS = [(hp, b, e) for hp in range(4) for b in range(NB) for e in range(2)]
DA_OFF = [P * b * (b + 1) // 2 for b in range(NB)]
M2_OFF = [0, SEQ, 2 * SEQ - P, 3 * SEQ - 3 * P]


TILE = SEQ * 4
X_AT, H_AT, RING_AT = 0, 8, 24
MERGED_AT, YHL_AT, ARENA_AT = 48, 56, 64
CON_OFF = 97 * TILE + 96


def trunk(nc, x_in, positions, w_lots, par_in, s5_in, con_in, gamma_in, out):
    f32, f32r, i32, u32 = mybir.dt.float32, mybir.dt.float32r, mybir.dt.int32, mybir.dt.uint32
    ALU, ACT, AX = mybir.AluOpType, mybir.ActivationFunctionType, mybir.AxisListType
    MUL, ADD, SUB = ALU.mult, ALU.add, ALU.subtract
    AFT = ACT
    ctx = ExitStack()
    with ctx:
        def at(name, shape, dt, tile, byte=0):
            return nc.alloc_sbuf_tensor_at(name, shape, dt, offset=BASE + tile * TILE + byte)

        BASE = -(-nc.sbuf_base // 32) * 32

        x = at("x", [P, KT, SEQ], f32, X_AT)
        h_hi = at("h_hi", [P, KT, SEQ], f32r, H_AT)
        h_lo = at("h_lo", [P, KT, SEQ], f32r, H_AT + 8)
        raw = at("raw", [P, 4, 8, P], f32, RING_AT)
        w_hi = at("w_hi", [P, 4, 8, P], f32r, RING_AT + 8)
        w_lo = at("w_lo", [P, 4, 8, P], f32r, RING_AT + 16)
        merged = at("merged", [P, KT, SEQ], f32, MERGED_AT)
        y_hi = at("y_hi", [P, BT, SEQ], f32r, YHL_AT)
        y_lo = at("y_lo", [P, BT, SEQ], f32r, YHL_AT + 4)
        con = at("con", [P, NCON], f32, 0, CON_OFF)
        par_off = CON_OFF + -(-4 * NCON // 32) * 32
        par = at("par", [P, NPAR], f32, 0, par_off)
        tail = par_off + -(-4 * NPAR // 32) * 32
        lower = at("lower", [P, DEPTH, 4], f32, 0, tail)
        roundc = at("roundc", [P, 1], f32, 0, tail + 704 + 2 * TILE)
        epsc = at("epsc", [P, 1], f32, 0, tail + 32)
        half_pi = at("half_pi", [P, 1], f32, 0, tail + 64)
        rope_cos = at("rope_cos", [P, SEQ], f32, 0, tail + 96)
        rope_sin = at("rope_sin", [P, SEQ], f32, 0, tail + 96 + TILE)

        def C(name, a=0, b=None):
            k = CON_AT[name]
            return con[:, k + a:k + (CON_SIZES[name] if b is None else b)]

        def PR(name, a=0, b=None):
            k = PAR_AT[name]
            return par[:, k + a:k + (PAR_SIZES[name] if b is None else b)]

        def PC(name, i):
            return PR(name, i, i + 1)

        ident, ones = C("ident"), C("upper", P, 2 * P)

        small = at("small", [P, NB, 12], f32, 0, tail + 96 + 2 * TILE)
        m2_dt = at("m2_dt", [P, 3, NB, 8], f32, 0, tail + 288 + 2 * TILE)
        m2_ea = at("m2_ea", [P, 8], f32, 0, tail + 672 + 2 * TILE)
        A, M, Y = ARENA_AT, MERGED_AT, YHL_AT

        g_hi = at("g_hi", [P, 8, SEQ], f32r, M)
        g_lo = at("g_lo", [P, 8, SEQ], f32r, Y)
        silu_a = at("silu_a", [P, 2, SEQ], f32, A)
        gated = at("gated", [P, 2, SEQ], f32, A + 2)
        sq = at("sq", [P, 2, SEQ], f32, A + 28)
        rms = at("rms", [P, SEQ], f32, A + 30)
        normed = at("normed", [P, 2, SEQ], f32, A + 31)
        gate_th = at("gate_th", [P, 2, SEQ], f32, A + 10)

        s5_u = at("s5_u", [P, 4, SEQ], f32, A)
        s5_bc = at("s5_bc", [P, 4, 16, 32], f32, A + 4)
        s5_bb = at("s5_bb", [P, 2, 16, 32], f32, A + 8)
        s5_bbt = at("s5_bbt", [P, 2, 4, P], f32, A + 10)
        s5_k = at("s5_k", [P, 21, 16], f32, A + 32)
        s5_v0 = at("s5_v0", [P, 2, SEQ], f32, A + 4)
        s5_v1 = at("s5_v1", [P, 2, SEQ], f32, A + 8)
        s5_v = [s5_v0, s5_v1]
        s5_cos = at("s5_cos", [P, 2, SEQ], f32, M)
        s5_sin = at("s5_sin", [P, 2, SEQ], f32, M + 2)
        s5_ph = at("s5_ph", [P, 4, SEQ], f32, M + 4)
        s5_pr = at("s5_pr", [P, 4, SEQ], f32, Y)
        s5_s = at("s5_s", [P, 2, 2, SEQ], f32, Y + 4)
        s5_pq = at("s5_pq", [P, 2, SEQ], f32, A + 27)
        gel = at("gel", [P, 2, SEQ], f32, A + 8)
        gel_hi = at("gel_hi", [P, 4, SEQ], f32r, M)
        gel_lo = at("gel_lo", [P, 4, SEQ], f32r, M + 4)
        glu_th = at("glu_th", [P, 2, SEQ], f32, A + 4)
        glu_y = at("glu_y", [P, 2, SEQ], f32, A + 6)

        da_mb = at("da_mb", [P, 1280], f32, A)
        da_st = at("da_st", [P, 32, 4], f32, A + 2, TILE // 2)
        da_m8 = at("da_m8", [P, 8], f32, A + 2, TILE // 2 + 512)
        da_sc = at("da_sc", [P, SEQ], f32, A + 3)
        da_lg = at("da_lg", [P, 2, SEQ], f32, A + 4)
        da_p = at("da_p", [P, 2, SEQ], f32, A + 6)
        da_pt = at("da_pt", [P, 2, SEQ], f32, A + 8)
        da_qk = at("da_qk", [P, 8, SEQ], f32, A + 12)
        da_v = at("da_v", [P, NB, BW], f32, A + 20)
        da_qi = at("da_qi", [P, 2, SEQ], f32, A + 24)
        da_ki = at("da_ki", [P, SEQ], f32, A + 26)
        da_t = at("da_t", [P, 4, SEQ], f32, A + 27)
        da_r = at("da_r", [P, 4, SEQ], f32, A + 27)
        da_wk = at("da_wk", [P, SEQ], f32, A + 31)

        m2_xdt = at("m2_xdt", [P, NB, BW], f32, A)
        m2_e = at("m2_e", [P, 2, 1280], f32, A + 4)
        m2_rs = at("m2_rs", [P, SEQ], f32, A + 9)
        m2_xc = at("m2_xc", [P, 6, SEQ], f32, A + 12)
        m2_z = at("m2_z", [P, 4, SEQ], f32, A + 18)
        m2_cb = at("m2_cb", [P, 2, 1280], f32, A + 22)
        m2_xr = at("m2_xr", [P, 6, SEQ + 3], f32, A + 27)
        m2_yv = at("m2_yv", [P, 4, SEQ], f32, A + 27)
        m2_t = at("m2_t", [P, 2, SEQ], f32, A + 31)

        hq = at("hq", [P, 4, SEQ], f32, A)
        hf = at("hf", [P, 4, SEQ], f32, A + 4)
        hken = at("hken", [P, NB, P], f32, A + 8)
        hlb = at("hlb", [P, 2, 4], f32, A + 9)
        hdec = at("hdec", [P, 2, NCH], f32, A + 9, 64)
        hv = at("hv", [P, NB, BW], f32, A + 12)
        hg = at("hg", [P, 4, SEQ], f32, A + 16)
        he = at("he", [P, 2, 4, SEQ], f32, A + 20)
        hatt = at("hatt", [P, NB, P], f32, A + 28)
        hS = at("hS", [P, NCH, P], f32, A + 29)
        hsq = at("hsq", [P, 2, SEQ], f32, A + 29)

        x_nat = at("x_nat", [P, NB, DM], f32, ARENA_AT)
        pos_i = at("pos_i", [P, SEQ], i32, ARENA_AT + 16)
        ang = at("ang", [P, 4, SEQ], f32, ARENA_AT + 17)
        gam = at("gam", [P, DEPTH, 4], f32, ARENA_AT + 21)
        gtmp = at("gtmp", [P, 6, DEPTH, 4], f32, ARENA_AT + 22)
        o_nat = at("o_nat", [P, NB, DM], f32, ARENA_AT)

        bank = [nc.alloc_psum_tensor("bank%d" % i, [P, SEQ], f32) for i in range(8)]

        LAYER = """raw_in0 raw_in1 raw_in2 raw_in3 hi_done lo_done out_done free0 free1 free2 free3
            sq_done sq_used rms_ready normed_ready h_hi_done h_done g_hi_done g_done
            act_seq dve_seq par_in s5_in
            s5_k_ready s5_khi s5_pq_done m2_zs s5_pre s5_z s5_sim s5_bb_ready s5_bbt_psum s5_bbt_ready s5_phase s5_trig s5_bu s5_bu_used s5_state
            s5_y s5_y_used s5_gelu gel_hi_done gel_done glu_th_done glu_y_done y_hi_done y_done
            th_done merge_used merged_done
            da_idx_done da_sq da_ms da_rms da_qn da_rot da_rot_done da_rel da_relu da_relu_used da_score da_causal
            da_mask da_logit da_max da_exp da_prob da_pt_psum da_pt_ready da_pv da_pv_hi da_logit_used
            m2_dtb m2_abs m2_dt_ready m2_acs m2_acs_done m2_ct m2_xdt_done m2_conv m2_silu m2_cbp m2_cb_done m2_acb
            m2_seg m2_decay m2_m m2_yp m2_y m2_sq m2_ms m2_rms m2_yn
            hg_e hg_fg hg_lf hg_cum hg_ec hg_ke hg_ket hg_ken hg_attp hg_att hg_upd hg_updu hg_S hg_op
            hg_ex hg_o hg_sq hg_ms hg_rms hg_yn hg_lc hg_el
            layer_end""".split()
        sems = {}
        for name in LAYER:
            sems[name] = ctx.enter_context(nc.semaphore(name))
        for name in """go_sp go_act go_dve go_pe c_con c_x c_pos c_gam p_x p_xt p_ang p_trig p_gam1 p_gam2 p_seq
                e_x e_o e_out""".split():
            sems[name] = ctx.enter_context(nc.semaphore(name))
        S = sems
        first, last = sems[LAYER[0]].num, sems["layer_end"].num
        assert last - first == len(LAYER) - 1
        raw_in = [S["raw_in%d" % i] for i in range(4)]
        free = [S["free%d" % i] for i in range(4)]

        block = ctx.enter_context(nc.Block())

        def wait_out(eng, t):
            eng.wait_ge(S["out_done"], t + 1)

        def wait_taken(eng, t):
            t0, it = t if isinstance(t, tuple) else (t, 0)
            if isinstance(t, tuple) or t >= 0:
                eng.wait_ge(free[t0 % 4], it + (t0 // 4 + 1))

        def end_of_layer(eng, go):
            eng.drain()
            eng.sem_inc(S["layer_end"], 1)
            eng.wait_ge(go, 1)
            eng.sem_clear(go)

        def split_hi(act, n0, it=0):
            if isinstance(it, int) and n0 >= NLOT:
                return
            s = n0 % 4
            act.wait_ge(raw_in[s], 16 * (it + n0 // 4 + 1))
            if n0 >= 4:
                act.wait_ge(S["out_done"], USED_AT[n0 - 4] + 4 * it)
            act.activation(w_hi[:, s], raw[:, s], AFT.Copy).then_inc(S["hi_done"], 1)

        def split_lo(eng, n0, it=0):
            if isinstance(it, int) and n0 >= NLOT:
                return
            s = n0 % 4
            eng.wait_ge(S["hi_done"], n0 + 1 + 4 * it)
            eng.tensor_tensor(w_lo[:, s], raw[:, s], w_hi[:, s].bitcast(f32), SUB).then_inc(S["lo_done"], 1)

        class Order:

            def __init__(self, eng, sem):
                self.eng, self.sem, self.n = eng, sem, 0

            def do(self, ins):
                self.n += 1
                ins.then_inc(self.sem, 1)
                return self.n

            def need(self, n):
                self.eng.wait_ge(self.sem, n)

        def gsplit(n):
            return OUT0[n]

        @block.tensor
        def _(pe):
            def gemm(n0, it, xh, xl, nk, k0=0, t0=None, ready=None):
                s, t0 = n0 % 4, OUT0[n0] if t0 is None else t0
                pe.wait_ge(S["lo_done"], it * 4 + (n0 + 1))
                if t0 >= 4:
                    pe.wait_ge(free[t0 % 4], it + t0 // 4)
                b = bank[t0 % 4]
                for k in range(nk):
                    if ready is not None:
                        pe.wait_ge(S["h_done"], ready + k + 1)
                    pe.matmul(b[:, :], w_hi[:, s, k0 + k], xh[:, k], start=(k == 0), stop=False)
                    pe.matmul(b[:, :], w_hi[:, s, k0 + k], xl[:, k], start=False, stop=False)
                    m = pe.matmul(b[:, :], w_lo[:, s, k0 + k], xh[:, k], start=False, stop=(k == nk - 1))
                m.then_inc(S["out_done"], 1)

            def gemm_tokens(n0, cols, lots=1):
                s, w = n0 % 4, P * lots
                pe.wait_ge(S["lo_done"], n0 + lots)
                per = NB // lots
                for b in range(NB):
                    t = OUT0[n0] + b // per
                    if b % per == 0:
                        pe.wait_ge(free[t % 4], t // 4)
                    o = bank[t % 4][:, w * (b % per):w * (b % per) + (cols if lots == 1 else w)]
                    tok = slice(P * b, P * (b + 1))
                    wh, wl = (w_[:, s:s + lots, :, 0:cols] for w_ in (w_hi, w_lo))
                    for k in range(KT):
                        pe.matmul(o, h_hi[:, k, tok], wh[:, :, k], start=(k == 0), stop=False)
                        pe.matmul(o, h_lo[:, k, tok], wh[:, :, k], start=False, stop=False)
                        m = pe.matmul(o, h_hi[:, k, tok], wl[:, :, k], start=False, stop=(k == KT - 1))
                    if b % per == per - 1:
                        m.then_inc(S["out_done"], 1)

            def norm_sums(r):
                for i in range(KT):
                    pe.wait_ge(S["sq_done"], KT * r + i + 1)
                    pe.matmul(bank[7][:, :], ones, sq[:, i % 2], start=(i == 0), stop=(i == KT - 1)) \
                      .then_inc(S["sq_used"], 1)

            def ffn(which, nb):
                norm_sums(2 * which)
                n, g0 = nb, FF_TILES * which
                for J in THIRDS:
                    with pe.Fori(0, J // 2) as it:
                        for j in range(4):
                            first = n == nb and j == 0
                            gemm(n + j, it, h_hi, h_lo, KT, ready=KT * 3 * which if first else None)
                    n, g0 = n + 2 * J, g0 + J
                    pe.wait_ge(S["g_done"], g0)
                    with pe.Fori(0, 2) as it:
                        for j in range(4):
                            gemm(n + j, it, g_hi, g_lo, J)
                    n += KT

            def gemm_h(n):
                gemm(n, 0, h_hi, h_lo, KT, ready=KT if n == MIX0 else KT * 2 if n == LOT_AT[("out", 0)] else None)

            def lot(kind, i):
                if kind == "small":
                    gemm_tokens(LOT_AT[(kind, i)], 12)
                else:
                    gemm_h(LOT_AT[(kind, i)])

            def out(i):
                gemm_h(LOT_AT[("out", i)])

            def pair(kind, i):
                gemm_tokens(LOT_AT[(kind, i)], P, 2)

            def out_start():
                pass

            def glu(i):
                if i == 0:
                    pe.wait_ge(S["gel_done"], 4)
                n = LOT_AT[("glu", i)]
                for half in range(2):
                    gemm(n, 0, gel_hi, gel_lo, BT, k0=4 * half, t0=OUT0[n] + half)

            def gate(g, i):
                gemm_h(LOT_AT[("gate%d" % g, i)])

            def branch(g, pair):
                n = LOT_AT[("branch%d" % g, pair)]
                if pair == 0:
                    pe.wait_ge(S["y_done"], BT * (TURN[g] + 1))
                for half in range(2):
                    gemm(n, 0, y_hi, y_lo, BT, k0=BT * half, t0=OUT0[n] + half)

            def s5_prep(phase):
                if phase == 0:
                    return
                pe.wait_ge(S["s5_bb_ready"], 2)
                for c in range(2):
                    for jt in range(4):
                        m = pe.transpose(bank[4 + c][:, P * jt:P * (jt + 1)],
                                         s5_bb[:, c].rearrange("p s i -> p (s i)")[:, P * jt:P * (jt + 1)], ident)
                    m.then_inc(S["s5_bbt_psum"], 1)
                pe.wait_ge(S["s5_bbt_ready"], 2)

            def s5_drive(st):
                q, jt = st % 4, st // 4
                wait_taken(pe, out_at("u", jt))
                if st:
                    pe.wait_ge(S["s5_bu_used"], st)
                for c in range(2):
                    m = pe.matmul(bank[4 + c][:, :], s5_bbt[32 * q:32 * q + 32, c, jt], s5_u[32 * q:32 * q + 32, jt],
                                  start=True, stop=True)
                m.then_inc(S["s5_bu"], 1)

            def s5_read(st):
                q, jt = st % 4, st // 4
                if q == 0 and jt:
                    pe.wait_ge(S["s5_y_used"], jt)
                for c, ready in enumerate(("s5_state", "s5_sim")):
                    pe.wait_ge(S[ready], st + 1)
                    m = pe.matmul(bank[6][32 * q:32 * q + 32, :], s5_bc[:, 2 + c, st], s5_s[:, st % 2, c],
                                  start=(c == 0), stop=(c == 1))
                m.then_inc(S["s5_y"], 1)

            def s5(st):
                s5_drive(st)
                if st >= 2:
                    s5_read(st - 2)

            def s5_end():
                s5_read(S5_TILES - 2)
                s5_read(S5_TILES - 1)

            def da_norm(g, phase):
                if g == 0 and phase == 0:
                    pe.wait_ge(S["s5_y_used"], 4)
                for j in range(4 if phase == 0 else 0):
                    pe.wait_ge(S["da_sq"], 4 * g + j + 1)
                    pe.matmul(bank[4 + j][:, :], C("blk"), da_t[:, j], start=True, stop=True).then_inc(S["da_ms"], 1)
                for j in range(4 if phase == 1 else 0):
                    pe.wait_ge(S["da_qn"], 4 * g + j + 1)
                    pe.matmul(bank[4 + j][:, :], C("rot"), da_qk[:, 4 * g + j], start=True, stop=True) \
                      .then_inc(S["da_rot"], 1)

            def da_index(b):
                if b == 1:
                    pe.wait_ge(S["da_rot_done"], 8)
                    wait_taken(pe, out_at("ki", 0))
                else:
                    pe.wait_ge(S["da_relu"], 4 * (b - 1))
                for hh in range(4):
                    r = slice(64 * (hh % 2), 64 * (hh % 2) + 64)
                    m = pe.matmul(bank[4 + hh][:, 0:P * (b + 1)], da_qi[r, hh // 2, P * b:P * (b + 1)],
                                  da_ki[r, 0:P * (b + 1)], start=True, stop=True)
                m.then_inc(S["da_rel"], 1)

            def da_topk(b):
                pass

            def logits(u):
                hp, b, e = UNITS[u]
                r = slice(64 * e, 64 * e + 64)
                if u >= 2:
                    pe.wait_ge(S["da_max"], u - 1)
                pe.matmul(bank[4 + u % 2][:, 0:P * (b + 1)], da_qk[r, hp, P * b:P * (b + 1)],
                          da_qk[r, 4 + hp, 0:P * (b + 1)], start=True, stop=True).then_inc(S["da_logit"], 1)

            def turn(u):
                hp, b, e = UNITS[u]
                pe.wait_ge(S["da_prob"], u + 1)
                if u:
                    pe.wait_ge(S["da_pt_ready"], u)
                for j in range(b + 1):
                    m = pe.transpose(bank[6][:, P * j:P * (j + 1)], da_p[:, u % 2, P * j:P * (j + 1)], ident)
                m.then_inc(S["da_pt_psum"], 1)

            def values(u):
                hp, b, e = UNITS[u]
                h = 2 * hp + e
                pe.wait_ge(S["da_pt_ready"], u + 1)
                if u % 8 == 0 and hp:
                    pe.wait_ge(S["y_done"], BT * TURN[2] + hp)
                for j in range(b + 1):
                    m = pe.matmul(bank[7][64 * e:64 * e + 64, P * b:P * (b + 1)], da_v[:, j, 64 * h:64 * h + 64],
                                  da_pt[:, u % 2, P * j:P * (j + 1)], start=(j == 0), stop=(j == b))
                m.then_inc(S["da_pv"], 1)
            def att_start():
                pe.wait_ge(S["da_relu"], 12)
                logits(0)
                logits(1)

            def att(u):
                turn(u)
                if u + 2 < 32:
                    logits(u + 2)
                if u:
                    values(u - 1)

            def att_end():
                values(31)

            def m2_dt_(*a):
                pass

            def m2_conv():
                pass

            def m2_prep():
                pe.wait_ge(S["m2_dt_ready"], 1)
                for b in range(NB):
                    for j in range(b + 1):
                        m = pe.matmul(bank[4][:, 8 * b:8 * b + 8], C("upper", 0, P) if j == b else ones, m2_dt[:, 1, j],
                                      start=(j == 0), stop=(j == b))
                m.then_inc(S["m2_acs"], 1)
                pe.wait_ge(S["m2_silu"], 4)
                for b in range(NB):
                    if b >= 2:
                        pe.wait_ge(S["m2_xdt_done"], b - 1)
                    for i in range(4):
                        m = pe.transpose(bank[5 + b % 2][:, P * i:P * (i + 1)], m2_xc[:, i, P * b:P * (b + 1)], ident)
                    m.then_inc(S["m2_ct"], 1)
                pe.wait_ge(S["m2_silu"], 6)
                pe.wait_ge(S["m2_acs_done"], 1)
                for c in range(8):
                    g, j = c // 4, c % 4
                    r = slice(64 * g, 64 * g + 64)
                    if c >= 2:
                        pe.wait_ge(S["m2_cb_done"], c - 1)
                    pe.matmul(bank[4 + 3 * (c % 2)][:, 0:SEQ - P * j], m2_xc[r, 4, P * j:P * (j + 1)],
                              m2_xc[r, 5, P * j:SEQ], start=True, stop=True).then_inc(S["m2_cbp"], 1)
                pe.wait_ge(S["m2_cb_done"], 8)
                pe.wait_ge(S["m2_xdt_done"], 4)

            def decays(h):
                if h >= 2:
                    pe.wait_ge(S["m2_seg"], h - 1)
                for j in range(NB):
                    m = pe.matmul(bank[4 + h % 2][:, P * j:SEQ], m2_dt[:, 1, j, h:h + 1].broadcast_to([P, P]),
                                  C("upper", 0, SEQ - P * j), start=(j == 0), stop=(j == NB - 1))
                m.then_inc(S["m2_acb"], 1)

            def outs(h):
                pe.wait_ge(S["m2_m"], h + 1)
                if h % 2 == 0 and h >= 4:
                    pe.wait_ge(S["m2_y"], h // 2 - 1)
                e = 64 * (h % 2)
                for j in range(NB):
                    m = pe.matmul(bank[6 + h // 2 % 2][e:e + 64, P * j:SEQ], m2_xdt[:, j, 64 * h:64 * h + 64],
                                  m2_e[:, h % 2, M2_OFF[j]:M2_OFF[j] + SEQ - P * j], start=(j == 0), stop=(j == NB - 1))
                m.then_inc(S["m2_yp"], 1)
            def m2_head(h):
                if h == 0:
                    decays(0)
                if h < 7:
                    decays(h + 1)
                outs(h)

            def m2_norm():
                for i in range(BT):
                    pe.wait_ge(S["m2_sq"], i + 1)
                    pe.matmul(bank[4][:, :], ones, m2_t[:, i % 2], start=(i == 0), stop=(i == BT - 1)) \
                      .then_inc(S["m2_ms"], 1)

            def m2_end():
                pass

            def hg_start():
                pass

            def hg_gates(h, phase):
                pass

            def hg_head(h, phase):
                (hg_products, hg_updates, hg_outputs)[phase](h)

            def hg_products(h):
                scr = he[:, h % 2]
                pe.wait_ge(S["hg_ke"], 3 * h + 2)
                for j in range(NB):
                    t = slice(P * j, P * (j + 1))
                    m = pe.matmul(bank[4][:, t], scr[:, 2, t], hq[:, h, t], start=True, stop=True)
                m.then_inc(S["hg_attp"], 1)
                pe.wait_ge(S["hg_ke"], 3 * h + 3)
                if h:
                    pe.wait_ge(S["hg_o"], h)
                for j in range(NB):
                    t = slice(P * j, P * (j + 1))
                    m = pe.transpose(bank[5][:, t], scr[:, 3, t], ident)
                m.then_inc(S["hg_ket"], 1)

            def hg_updates(h):
                v = slice(P * h, P * (h + 1))
                pe.wait_ge(S["hg_ken"], h + 1)
                pe.wait_ge(S["hg_att"], h + 1)
                for j in range(NB):
                    for q in range(4 if j < NB - 1 else 3):
                        r = slice(32 * q, 32 * q + 32)
                        m = pe.matmul(bank[4 + q][:, P * j:P * (j + 1)], hken[r, j], hv[r, j, v], start=True, stop=True)
                m.then_inc(S["hg_upd"], 1)

            def hg_outputs(h):
                v = slice(P * h, P * (h + 1))
                pe.wait_ge(S["hg_updu"], h + 1)
                for j in range(NB):
                    t = slice(P * j, P * (j + 1))
                    m = pe.matmul(bank[5][:, t], hv[:, j, v], hatt[:, j], start=True, stop=False)
                    for c in range(4 * j, 4 * j + 4):
                        if c:
                            tc = slice(HG_CHUNK * c, HG_CHUNK * (c + 1))
                            m = pe.matmul(bank[5][:, tc], hS[:, c], hq[:, h, tc], start=False, stop=(c % 4 == 3))
                m.then_inc(S["hg_op"], 1)

            def hg_norm():
                for h in range(4):
                    pe.wait_ge(S["hg_sq"], h + 1)
                    if h == 0:
                        pe.wait_ge(S["hg_o"], 4)
                    pe.matmul(bank[4 + h][:, :], ones, hsq[:, h % 2], start=True, stop=True).then_inc(S["hg_ms"], 1)

            STEPS = dict(lot=lot, pair=pair, out=out, out_start=out_start, glu=glu, gate=gate, branch=branch,
                         s5_prep=s5_prep, s5=s5,
                         s5_end=s5_end, da_norm=da_norm, da_index=da_index, da_topk=da_topk, att_start=att_start,
                         att=att, att_end=att_end, m2_dt=m2_dt_, m2_conv=m2_conv, m2_prep=m2_prep, m2_head=m2_head,
                         m2_norm=m2_norm, m2_end=m2_end, hg_start=hg_start, hg_gates=hg_gates, hg_head=hg_head,
                         hg_norm=hg_norm)

            def mixing():
                for step in SCRIPT:
                    STEPS[step[0]](*step[1:])

            pe.wait_ge(S["c_con"], 16)
            pe.wait_ge(S["c_x"], 16)
            for i in range(KT):
                for b in range(NB):
                    m = pe.transpose(bank[i][:, P * b:P * (b + 1)], x_nat[:, b, P * i:P * (i + 1)], ident)
                m.then_inc(S["p_x"], 1)
            pe.wait_ge(S["p_xt"], KT)
            with pe.Fori(0, DEPTH) as layer:
                ffn(0, 0)
                norm_sums(1)
                mixing()
                ffn(1, FFN2_0)
                end_of_layer(pe, S["go_pe"])
            for b in range(NB):
                for i in range(KT):
                    m = pe.transpose(bank[2 * b + i // 4][:, P * (i % 4):P * (i % 4 + 1)],
                                     x[:, i, P * b:P * (b + 1)], ident)
                    if i % 4 == 3:
                        m.then_inc(S["e_x"], 1)

        @block.sync
        def _(sp):
            sp.dma_start(con[:, :], con_in).then_inc(S["c_con"], 16)
            sp.dma_start(x_nat[:, :, :], x_in.rearrange("(b p) d -> p b d", p=P)).then_inc(S["c_x"], 16)
            sp.dma_start(pos_i[:, :], positions.partition_broadcast(P)).then_inc(S["c_pos"], 16)
            sp.dma_start(gam[:, :, :], gamma_in).then_inc(S["c_gam"], 16)
            sp.wait_ge(S["p_xt"], KT)
            sp.wait_ge(S["p_gam2"], 1)
            sp.wait_ge(S["p_trig"], 3)
            with sp.Fori(0, DEPTH) as layer:
                sp.dma_start(par[:, :], par_in[layer]).then_inc(S["par_in"], 16)
                sp.dma_start(s5_bc[:, :, :, :].rearrange("p a b c -> p (a b c)"), s5_in[layer]) \
                  .then_inc(S["s5_in"], 16)
                for n in range(4):
                    sp.dma_start(raw[:, n].rearrange("p k m -> p (k m)"), w_lots[layer * NLOT + n]) \
                      .then_inc(raw_in[n], 16)
                with sp.Fori(1, NLOT // 4) as it:
                    for s in range(4):
                        sp.wait_ge(S["lo_done"], it * 4 + (s - 3))
                        sp.dma_start(raw[:, s].rearrange("p k m -> p (k m)"),
                                     w_lots[layer * NLOT + it * 4 + s]).then_inc(raw_in[s], 16)
                for n in range(NLOT // 4 * 4, NLOT):
                    sp.wait_ge(S["lo_done"], n - 3)
                    sp.dma_start(raw[:, n % 4].rearrange("p k m -> p (k m)"), w_lots[layer * NLOT + n]) \
                      .then_inc(raw_in[n % 4], 16)
                end_of_layer(sp, S["go_sp"])
            for b in range(NB):
                sp.wait_ge(S["e_o"], 2 * (b + 1))
                sp.dma_start(out[P * b:P * (b + 1), :], o_nat[:, b]).then_inc(S["e_out"], 16)
            sp.wait_ge(S["e_out"], 16 * NB)

        @block.gpsimd
        def _(pool):
            def after(kind, i):
                split_lo(pool, LOT_AT[(kind, i)] + 4)

            def s5_im(st):
                e = st % 2
                cs, sn, v = s5_cos[:, e], s5_sin[:, e], s5_v[e]
                pool.wait_ge(S["s5_z"], 2 * st + 2)
                if st:
                    pool.wait_ge(S["s5_sim"], st)
                pool.tensor_tensor(s5_pq[:, 0], v[:, 0], sn, MUL).then_inc(S["s5_pq_done"], 1)
                pool.tensor_tensor(s5_pq[:, 1], v[:, 1], cs, MUL).then_inc(S["s5_pq_done"], 1)
                pool.wait_ge(S["s5_pq_done"], 2 * (st + 1))
                if st >= 2:
                    pool.wait_ge(S["s5_y"], st - 1)
                pool.tensor_tensor(s5_s[:, e, 1], s5_pq[:, 0], s5_pq[:, 1], ADD).then_inc(S["s5_sim"], 1)

            def mixing():
                pool.wait_ge(S["lo_done"], MIX0 + 4)
                for step in SCRIPT:
                    if step[0] == "lot":
                        after(*step[1:])
                    elif step[0] == "pair":
                        after(step[1], step[2])
                        after(step[1], step[2] + 1)
                    elif step[0] in ("glu", "out"):
                        after(*step)
                    elif step[0] in ("gate", "branch"):
                        after(step[0] + str(step[1]), step[2])
                    elif step[0] == "s5":
                        s5_im(step[1])

            with pool.Fori(0, DEPTH) as layer:
                mixing()
                pool.wait_ge(S["layer_end"], 4)
                pool.sem_clear(range(first, last + 1))
                for go in ("go_sp", "go_act", "go_dve", "go_pe"):
                    pool.sem_inc(S[go], 1)

        @block.scalar
        def _(act):
            seq = Order(act, S["act_seq"])

            def norm(r, x_ready):
                for i in range(KT):
                    x_ready(i)
                    if KT * r + i >= 2:
                        act.wait_ge(S["sq_used"], KT * r + i - 1)
                    act.activation(sq[:, i % 2], x[:, i], AFT.Square).then_inc(S["sq_done"], 1)
                act.wait_ge(S["sq_used"], KT * (r + 1))
                act.activation(rms[:, :], bank[7][:, :], AFT.Sqrt, scale=1.0 / DM, bias=epsc[:, :]) \
                   .then_inc(S["rms_ready"], 1)
                high_parts(KT * r)

            def high_parts(n0):
                for i in range(KT):
                    act.wait_ge(S["normed_ready"], n0 + i + 1)
                    act.activation(h_hi[:, i], normed[:, i % 2], AFT.Copy).then_inc(S["h_hi_done"], 1)

            def ffn(which, nb):
                n, g0 = nb, FF_TILES * which
                for th, J in enumerate(THIRDS):
                    with act.Fori(0, J // 2) as it:
                        for q in range(2):
                            na, nbb = n + 2 * q, n + 2 * q + 1
                            ta, tb = OUT0[na], OUT0[nbb]
                            act.wait_ge(S["out_done"], it * 4 + (ta + 1))
                            if tb >= 4:
                                act.wait_ge(free[tb % 4], it + tb // 4)
                            act.activation(silu_a[:, q], bank[ta % 4][:, :], AFT.Silu).then_inc(free[ta % 4], 1)
                            split_hi(act, na + 4, it)
                            split_hi(act, nbb + 4, it)
                            act.wait_ge(free[tb % 4], it + (tb // 4 + 1))
                            act.activation(g_hi[:, it * 2 + q], gated[:, q], AFT.Copy).then_inc(S["g_hi_done"], 1)
                    n += 2 * J
                    if nb == FFN2_0 and th == len(THIRDS) - 1:
                        for j in range(KT):
                            split_hi(act, n + j + 4)
                    else:
                        with act.Fori(0, 2) as it:
                            for j in range(4):
                                split_hi(act, n + j + 4, it)
                    n += KT

            def evac(dst, n, func=AFT.Copy, **kw):
                t = OUT0[n]
                wait_out(act, t)
                src = bank[t % 4][:, :]
                act.activation(dst, src, func, **kw).then_inc(free[t % 4], 1)
                split_hi(act, n + 4)

            def chain(ins):
                seq.need(seq.do(ins))

            def split_y(g, i, src, scale=1.0):
                if TURN[g]:
                    wait_out(act, out_at("branch%d" % ORDER[TURN[g] - 1], KT // 2 - 1, 1))
                act.activation(y_hi[:, i], src, AFT.Copy, scale=scale).then_inc(S["y_hi_done"], 1)

            def pair(kind, i):
                n, dst = LOT_AT[(kind, i)], da_v if kind == "v" else hv
                for half in range(2):
                    t = OUT0[n] + half
                    wait_out(act, t)
                    src = bank[t % 4][:, :].rearrange("p (b m) -> p b m", b=2)
                    act.activation(dst[:, 2 * half:2 * half + 2, P * i:P * (i + 2)], src, AFT.Copy) \
                       .then_inc(free[t % 4], 1)
                split_hi(act, n + 4)
                split_hi(act, n + 5)

            def lot(kind, i):
                n = LOT_AT[(kind, i)]
                if kind == "u":
                    evac(s5_u[:, i], n)
                elif kind == "small":
                    t = OUT0[n]
                    wait_out(act, t)
                    src = bank[t % 4][:, :].rearrange("p (b m) -> p b m", m=P)[:, :, 0:12]
                    act.activation(small[:, :, :], src, AFT.Copy).then_inc(free[t % 4], 1)
                    split_hi(act, n + 4)
                elif kind in ("q", "k"):
                    evac(da_qk[:, 4 * "qk".index(kind) + i], n)
                elif kind == "qi":
                    evac(da_qi[:, i], n)
                elif kind == "ki":
                    evac(da_ki[:, :], n)
                elif kind == "xbc":
                    if i == 0:
                        act.wait_ge(S["da_idx_done"], 1)
                    evac(m2_xr[:, i, 3:3 + SEQ], n)
                elif kind == "z":
                    evac(m2_z[:, i], n)
                elif kind == "hf":
                    if i == 0:
                        act.wait_ge(S["m2_yp"], 8)
                        act.wait_ge(S["m2_m"], 8)
                    evac(hf[:, i], n)
                elif kind == "hq":
                    evac(hq[:, i], n)
                elif kind == "hg":
                    evac(hg[:, i], n, AFT.Tanh, scale=0.5)

            def out(i):
                split_hi(act, LOT_AT[("out", i)] + 4)

            def out_start():
                act.wait_ge(S["merge_used"], KT * len(ORDER))
                for i in range(KT):
                    act.activation(h_hi[:, i], merged[:, i], AFT.Copy).then_inc(S["h_hi_done"], 1)

            def gate(g, i):
                n = LOT_AT[("gate%d" % g, i)]
                t, done = OUT0[n], KT * TURN[g] + i
                wait_out(act, t)
                if done >= 2:
                    act.wait_ge(S["merge_used"], done - 1)
                act.activation(gate_th[:, i % 2], bank[t % 4][:, :], AFT.Tanh, scale=0.5).then_inc(free[t % 4], 1)
                split_hi(act, n + 4)

            def branch(g, pair):
                split_hi(act, LOT_AT[("branch%d" % g, pair)] + 4)

            K = lambda i: s5_k[:, i]

            def s5_pre(st):
                e, k1 = st % 2, slice(st, st + 1)
                if st >= 2:
                    act.wait_ge(S["s5_trig"], 2 * (st - 1))
                act.activation(s5_ph[:, 2 * e], C("tvec"), AFT.Copy, scale=K(9)[:, k1]).then_inc(S["s5_pre"], 1)
                act.activation(s5_ph[:, 2 * e + 1], C("tvec"), AFT.Identity, scale=K(5)[:, k1], bias=roundc[:, :]) \
                   .then_inc(S["s5_pre"], 1)

            def s5_trig(st):
                e = st % 2
                act.wait_ge(S["s5_phase"], st + 1)
                if st >= 2:
                    act.wait_ge(S["s5_state"], st - 1)
                    act.wait_ge(S["s5_sim"], st - 1)
                chain(act.activation(s5_ph[:, 2 * e + 1], s5_ph[:, 2 * e], AFT.Abs))
                act.activation(s5_sin[:, e], s5_ph[:, 2 * e], AFT.Sin, scale=2 * PI).then_inc(S["s5_trig"], 1)
                act.activation(s5_cos[:, e], s5_ph[:, 2 * e + 1], AFT.Sin, scale=-2 * PI, bias=half_pi[:, :]) \
                   .then_inc(S["s5_trig"], 1)

            def s5_prep(phase):
                if phase == 1:
                    for c in range(2):
                        act.wait_ge(S["s5_bbt_psum"], c + 1)
                        act.activation(s5_bbt[:, c].rearrange("p a b -> p (a b)"), bank[4 + c][:, :], AFT.Copy) \
                           .then_inc(S["s5_bbt_ready"], 1)
                    s5_trig(0)
                    return
                act.wait_ge(S["par_in"], 16)
                act.wait_ge(S["h_done"], 2 * KT)
                act.wait_ge(S["h_hi_done"], 2 * KT)
                act.activation(K(0), PR("log_dt"), AFT.Exp).then_inc(S["s5_k_ready"], 1)
                act.wait_ge(S["s5_k_ready"], 2)
                act.activation(K(3), K(1), AFT.Exp).then_inc(S["s5_k_ready"], 1)
                act.wait_ge(S["s5_k_ready"], 4)
                act.activation(K(7), K(5), AFT.Sin, scale=2 * PI).then_inc(S["s5_k_ready"], 1)
                act.activation(K(8), K(6), AFT.Sin, scale=-2 * PI, bias=half_pi[:, :]).then_inc(S["s5_k_ready"], 1)
                act.wait_ge(S["s5_khi"], 1)
                s5_pre(0)
                s5_pre(1)

            def s5(st):
                if st + 2 < S5_TILES:
                    s5_pre(st + 2)
                if st + 1 < S5_TILES:
                    s5_trig(st + 1)

            def s5_end():
                act.wait_ge(S["s5_y_used"], 4)
                for i in range(4):
                    if i >= 2:
                        act.wait_ge(S["gel_done"], i - 1)
                    chain(act.activation(gel[:, i % 2], s5_u[:, i], AFT.Gelu_apprx_tanh))
                    act.activation(gel_hi[:, i], gel[:, i % 2], AFT.Copy).then_inc(S["gel_hi_done"], 1)

            def glu(i):
                n = LOT_AT[("glu", i)]
                t = OUT0[n] + 1
                wait_out(act, t)
                if i >= 2:
                    act.wait_ge(S["glu_y_done"], i - 1)
                act.activation(glu_th[:, i % 2], bank[t % 4][:, :], AFT.Tanh, scale=0.5).then_inc(free[t % 4], 1)
                split_hi(act, n + 4)
                act.wait_ge(S["glu_y_done"], i + 1)
                split_y(1, i, glu_y[:, i % 2], scale=0.5)

            def da_norm(g, phase):
                if phase:
                    return
                if g:
                    act.wait_ge(S["da_rot_done"], 4)
                wait_taken(act, out_at("qk"[g], 3))
                for j in range(4):
                    act.activation(da_t[:, j], da_qk[:, 4 * g + j], AFT.Square).then_inc(S["da_sq"], 1)
                for j in range(4):
                    act.wait_ge(S["da_ms"], 4 * g + j + 1)
                    act.activation(da_t[:, j], bank[4 + j][:, :], AFT.Sqrt, scale=1.0 / 64, bias=epsc[:, :]) \
                       .then_inc(S["da_rms"], 1)

            def da_index(b):
                if b == 1:
                    act.wait_ge(S["da_rot_done"], 8)
                act.wait_ge(S["da_rel"], b)
                if b > 1:
                    act.wait_ge(S["da_score"], b - 1)
                for hh in range(4):
                    act.activation(da_r[:, hh, 0:P * (b + 1)], bank[4 + hh][:, 0:P * (b + 1)], AFT.Relu) \
                       .then_inc(S["da_relu"], 1)

            def da_topk(b):
                pass

            def exps(u):
                hp, b, e = UNITS[u]
                w = P * (b + 1)
                act.wait_ge(S["da_max"], u + 1)
                if u >= 2:
                    act.wait_ge(S["da_pt_psum"], u - 1)
                act.activation(da_p[:, u % 2, 0:w], da_lg[:, u % 2, 0:w], AFT.Exp, scale=0.125,
                               bias=da_st[:, u, 1:2], accum_out=da_st[:, u, 2:3]).then_inc(S["da_exp"], 1)

            def copy(u):
                hp, b, e = UNITS[u]
                w = P * (b + 1)
                act.wait_ge(S["da_pt_psum"], u + 1)
                if u >= 2:
                    act.wait_ge(S["da_pv"], u - 1)
                act.activation(da_pt[:, u % 2, 0:w], bank[6][:, 0:w], AFT.Copy).then_inc(S["da_pt_ready"], 1)
            def att_start():
                exps(0)

            def att(u):
                if u < 31:
                    exps(u + 1)
                copy(u)
                if u % 8 == 0 and u:
                    act.wait_ge(S["da_pv"], u)
                    split_y(2, u // 8 - 1, bank[7][:, :])

            def att_end():
                act.wait_ge(S["da_pv"], 32)
                split_y(2, 3, bank[7][:, :])

            def m2_dt_():
                act.wait_ge(S["m2_dtb"], 2)
                act.activation(m2_ea[:, :], PR("a_log"), AFT.Exp).then_inc(S["m2_abs"], 1)
                chain(act.activation(m2_dt[:, 1], m2_dt[:, 1], AFT.Exp, scale=-1.0))
                act.activation(m2_dt[:, 1], m2_dt[:, 1], AFT.Ln, bias=1.0).then_inc(S["m2_abs"], 1)

            def m2_conv():
                for i in range(4):
                    wait_taken(act, out_at("z", i))
                    act.activation(m2_z[:, i], m2_z[:, i], AFT.Silu).then_inc(S["m2_zs"], 1)
                for i in range(6):
                    act.wait_ge(S["m2_conv"], i + 1)
                    act.activation(m2_xc[:, i], m2_xc[:, i], AFT.Silu).then_inc(S["m2_silu"], 1)

            def m2_prep():
                pass

            def m2_head(h):
                act.wait_ge(S["m2_seg"], h + 1)
                act.activation(m2_e[:, h % 2], m2_e[:, h % 2], AFT.Exp).then_inc(S["m2_decay"], 1)

            def m2_norm():
                for i in range(BT):
                    act.wait_ge(S["m2_yn"], i + 1)
                    if i >= 2:
                        act.wait_ge(S["m2_ms"], i - 1)
                    act.activation(m2_t[:, i % 2], m2_yv[:, i], AFT.Square).then_inc(S["m2_sq"], 1)
                act.wait_ge(S["m2_ms"], 4)
                act.activation(m2_rs[:, :], bank[4][:, :], AFT.Sqrt, scale=1.0 / BW, bias=epsc[:, :]).then_inc(S["m2_rms"], 1)

            def m2_end():
                for i in range(BT):
                    act.wait_ge(S["m2_yn"], BT + i + 1)
                    split_y(0, i, m2_yv[:, i])

            def hg_start():
                for i in range(4):
                    wait_taken(act, out_at("hq", i))
                    act.activation(hq[:, i], hq[:, i], AFT.Silu).then_inc(S["hg_ex"], 1)

            def hg_gates(h, phase):
                X = [he[:, h % 2, i] for i in range(4)]
                if phase == 0:
                    if h >= 2:
                        act.wait_ge(S["hg_op"], h - 1)
                    wait_taken(act, out_at("hf", h))
                    chain(act.activation(X[0], hf[:, h], AFT.Exp, scale=-1.0))
                    act.activation(hf[:, h], hf[:, h], AFT.Exp).then_inc(S["hg_e"], 1)
                elif phase == 1:
                    act.wait_ge(S["hg_fg"], h + 1)
                    act.activation(X[0], X[0], AFT.Ln).then_inc(S["hg_lf"], 1)
                else:
                    act.wait_ge(S["hg_cum"], h + 1)
                    act.activation(X[0], X[1], AFT.Exp).then_inc(S["hg_ec"], 1)
                    act.activation(X[2], X[1], AFT.Exp, scale=-1.0).then_inc(S["hg_ec"], 1)
                    act.activation(hdec[:, h % 2], X[1][:, HG_CHUNK - 1::HG_CHUNK], AFT.Exp).then_inc(S["hg_ec"], 1)
                    act.wait_ge(S["hg_lc"], h + 1)
                    act.activation(X[3], X[3], AFT.Exp).then_inc(S["hg_el"], 1)

            def hg_head(h, phase):
                if phase == 0:
                    act.wait_ge(S["hg_ket"], h + 1)
                    act.activation(hken[:, :, :].rearrange("p a b -> p (a b)"), bank[5][:, :], AFT.Copy) \
                       .then_inc(S["hg_ken"], 1)
                elif phase == 2:
                    act.wait_ge(S["hg_op"], h + 1)
                    act.activation(hf[:, h], bank[5][:, :], AFT.Copy).then_inc(S["hg_o"], 1)

            def hg_norm():
                act.wait_ge(S["hg_o"], 4)
                for h in range(4):
                    if h >= 2:
                        act.wait_ge(S["hg_ms"], h - 1)
                    act.activation(hsq[:, h % 2], hf[:, h], AFT.Square).then_inc(S["hg_sq"], 1)
                for h in range(4):
                    act.wait_ge(S["hg_ms"], h + 1)
                    act.activation(he[:, 0, h], bank[4 + h][:, :], AFT.Sqrt, scale=1.0 / P, bias=epsc[:, :]) \
                       .then_inc(S["hg_rms"], 1)
                for h in range(4):
                    act.wait_ge(S["hg_yn"], h + 1)
                    split_y(3, h, he[:, 1, h], scale=0.5)

            STEPS = dict(lot=lot, pair=pair, out=out, out_start=out_start, glu=glu, gate=gate, branch=branch,
                         s5_prep=s5_prep, s5=s5,
                         s5_end=s5_end, da_norm=da_norm, da_index=da_index, da_topk=da_topk, att_start=att_start,
                         att=att, att_end=att_end, m2_dt=m2_dt_, m2_conv=m2_conv, m2_prep=m2_prep, m2_head=m2_head,
                         m2_norm=m2_norm, m2_end=m2_end, hg_start=hg_start, hg_gates=hg_gates, hg_head=hg_head,
                         hg_norm=hg_norm)

            def mixing():
                for step in SCRIPT:
                    STEPS[step[0]](*step[1:])

            for i in range(KT):
                act.wait_ge(S["p_x"], i + 1)
                act.activation(x[:, i], bank[i][:, :], AFT.Copy).then_inc(S["p_xt"], 1)
            act.wait_ge(S["p_ang"], 2)
            act.activation(rope_sin[:, :], ang[:, 0], AFT.Sin).then_inc(S["p_trig"], 1)
            act.activation(rope_cos[:, :], ang[:, 1], AFT.Sin, scale=-1.0, bias=half_pi[:, :]).then_inc(S["p_trig"], 1)
            act.wait_ge(S["p_gam1"], 1)
            act.activation(gtmp[:, 1], gtmp[:, 0], AFT.Exp).then_inc(S["p_trig"], 1)
            with act.Fori(0, DEPTH) as layer:
                seq.n = 0
                for n in range(4):
                    split_hi(act, n)
                norm(0, lambda i: None)
                ffn(0, 0)
                base = OUT0[FFN_LOTS - KT]
                norm(1, lambda i: wait_taken(act, (base + i, 0)))
                mixing()
                norm(2, lambda i: wait_taken(act, (out_at("out", i), 0)))
                ffn(1, FFN2_0)
                end_of_layer(act, S["go_act"])
            for b in range(NB):
                for half in range(2):
                    act.wait_ge(S["e_x"], 2 * b + half + 1)
                    act.activation(o_nat[:, b, BW * half:BW * (half + 1)], bank[2 * b + half][:, :], AFT.Copy) \
                       .then_inc(S["e_o"], 1)

        @block.vector
        def _(dve):
            seq = Order(dve, S["dve_seq"])
            do, need = seq.do, seq.need
            V = dve

            def norm(r, gain):
                V.wait_ge(S["rms_ready"], r + 1)
                n = do(V.reciprocal(rms[:, :], rms[:, :]))
                need(n)
                h0 = KT * (3 * r // 2)
                if r == 0:
                    V.wait_ge(S["par_in"], 16)

                def low(i):
                    V.wait_ge(S["h_hi_done"], h0 + i + 1)
                    V.tensor_tensor(h_lo[:, i], normed[:, i % 2], h_hi[:, i].bitcast(f32), SUB) \
                     .then_inc(S["h_done"], 1)
                for i in range(KT):
                    if i >= 2:
                        V.wait_ge(S["h_done"], h0 + i - 1)
                    V.scalar_tensor_tensor(normed[:, i % 2], x[:, i], PC(gain, i), rms[:, :], MUL, MUL) \
                     .then_inc(S["normed_ready"], 1)
                    if i:
                        low(i - 1)
                low(KT - 1)

            def ffn(which, nb):
                n, g0 = nb, FF_TILES * which
                for th, J in enumerate(THIRDS):
                    with V.Fori(0, J // 2) as it:
                        for q in range(2):
                            na, nbb = n + 2 * q, n + 2 * q + 1
                            ta, tb = OUT0[na], OUT0[nbb]
                            split_lo(V, na + 4, it)
                            V.wait_ge(free[ta % 4], it + (ta // 4 + 1))
                            V.wait_ge(S["out_done"], it * 4 + (tb + 1))
                            V.tensor_tensor(gated[:, q], silu_a[:, q], bank[tb % 4][:, :], MUL).then_inc(free[tb % 4], 1)
                            split_lo(V, nbb + 4, it)
                            V.wait_ge(S["g_hi_done"], it * 2 + (g0 + q + 1))
                            V.tensor_tensor(g_lo[:, it * 2 + q], gated[:, q], g_hi[:, it * 2 + q].bitcast(f32), SUB) \
                             .then_inc(S["g_done"], 1)
                    n, g0 = n + 2 * J, g0 + J

                    def down(j, it):
                        split_lo(V, n + j + 4, it)
                        t = OUT0[n + j]
                        V.wait_ge(S["out_done"], it * 4 + (t + 1))
                        i = it * 4 + j if not isinstance(it, int) else j
                        V.scalar_tensor_tensor(x[:, i], bank[t % 4][:, :], 0.5, x[:, i], MUL, ADD) \
                         .then_inc(free[t % 4], 1)
                    if nb == FFN2_0 and th == len(THIRDS) - 1:
                        for j in range(KT):
                            down(j, 0)
                    else:
                        with V.Fori(0, 2) as it:
                            for j in range(4):
                                down(j, it)
                    n += KT

            TT, TS, STT = V.tensor_tensor, V.tensor_scalar, V.scalar_tensor_tensor

            def chain(ins):
                need(do(ins))

            def low_y(g, i, src, scale=None):
                V.wait_ge(S["y_hi_done"], BT * TURN[g] + i + 1)
                hi = y_hi[:, i].bitcast(f32)
                ins = TT(y_lo[:, i], src, hi, SUB) if scale is None else STT(y_lo[:, i], src, scale, hi, MUL, SUB)
                ins.then_inc(S["y_done"], 1)

            def lot(kind, i):
                pass

            def pair(kind, i):
                pass

            def out(i):
                t = out_at("out", i)
                wait_out(V, t)
                STT(x[:, i], bank[t % 4][:, :], 0.5, x[:, i], MUL, ADD).then_inc(free[t % 4], 1)

            def out_start():
                V.wait_ge(S["merge_used"], KT * len(ORDER))
                for i in range(KT):
                    V.wait_ge(S["h_hi_done"], KT * 2 + i + 1)
                    TT(h_lo[:, i], merged[:, i], h_hi[:, i].bitcast(f32), SUB).then_inc(S["h_done"], 1)

            def gate(g, i):
                pass

            def branch(g, pair):
                for e in range(2):
                    i = 2 * pair + e
                    tp, tg = out_at("branch%d" % g, pair, e), out_at("gate%d" % g, i)
                    wait_taken(V, tg)
                    wait_out(V, tp)
                    STT(gate_th[:, e], gate_th[:, e], 1.0, bank[tp % 4][:, :], ADD, MUL).then_inc(free[tp % 4], 1)
                    wait_taken(V, tp)
                    if TURN[g] == 0:
                        V.tensor_copy(merged[:, i], gate_th[:, e]).then_inc(S["merge_used"], 1)
                    else:
                        V.wait_ge(S["merge_used"], KT * (TURN[g] - 1) + i + 1)
                        TT(merged[:, i], merged[:, i], gate_th[:, e], ADD).then_inc(S["merge_used"], 1)

            K = lambda i: s5_k[:, i]

            def s5_prep(phase):
                if phase == 1:
                    phases(0)
                    return
                V.wait_ge(S["s5_k_ready"], 1)
                chain(TT(K(2), PR("lam_im"), K(0), MUL))
                TT(K(1), PR("lam_re"), K(0), MUL).then_inc(S["s5_k_ready"], 1)
                chain(TS(K(2), K(2), 1.0 / (2 * PI), None, MUL))
                chain(TS(K(4), K(2), ROUND, -ROUND, ADD, ADD))
                chain(TT(K(5), K(2), K(4), SUB))
                V.wait_ge(S["s5_k_ready"], 3)
                STT(K(6), K(5), -1.0, K(5), MUL, ALU.max).then_inc(S["s5_k_ready"], 1)
                chain(TS(K(9), K(5), ROUND13, -ROUND13, ADD, ADD))
                TT(K(10), K(5), K(9), SUB).then_inc(S["s5_khi"], 1)
                V.wait_ge(S["s5_k_ready"], 6)
                do(TT(K(11), K(3), K(8), MUL))
                chain(TT(K(12), K(3), K(7), MUL))
                do(TS(K(13), K(11), -1.0, None, ADD))
                do(TT(K(14), PR("lam_re"), PR("lam_re"), MUL))
                chain(TT(K(15), PR("lam_im"), PR("lam_im"), MUL))
                chain(TT(K(14), K(14), K(15), ADD))
                do(V.reciprocal(K(14), K(14)))
                do(TT(K(15), K(13), PR("lam_re"), MUL))
                chain(TT(K(16), K(12), PR("lam_im"), MUL))
                do(TT(K(15), K(15), K(16), ADD))
                do(TT(K(17), K(12), PR("lam_re"), MUL))
                chain(TT(K(18), K(13), PR("lam_im"), MUL))
                chain(TT(K(17), K(17), K(18), SUB))
                do(TT(K(19), K(15), K(14), MUL))
                chain(TT(K(20), K(17), K(14), MUL))
                V.wait_ge(S["s5_in"], 16)
                qre, qim = (K(c).unsqueeze(2).broadcast_to([P, 16, 32]) for c in (19, 20))
                T = lambda i: s5_pr[:, i].rearrange("p (s c) -> p s c", c=32)
                do(TT(T(0), s5_bc[:, 0], qre, MUL))
                do(TT(T(1), s5_bc[:, 1], qim, MUL))
                do(TT(T(2), s5_bc[:, 1], qre, MUL))
                chain(TT(T(3), s5_bc[:, 0], qim, MUL))
                TT(s5_bb[:, 0], T(0), T(1), SUB).then_inc(S["s5_bb_ready"], 1)
                TT(s5_bb[:, 1], T(2), T(3), ADD).then_inc(S["s5_bb_ready"], 1)
                chain(TS(s5_bc[:, 3], s5_bc[:, 3], -1.0, None, MUL))
                V.wait_ge(S["s5_bb_ready"], 2)

            def phases(st):
                f, fr = s5_ph[:, 2 * (st % 2)], s5_ph[:, 2 * (st % 2) + 1]
                V.wait_ge(S["s5_pre"], 2 * (st + 1))
                chain(STT(f, fr, -ROUND, f, ADD, SUB))
                chain(STT(f, C("tvec"), K(10)[:, st:st + 1], f, MUL, SUB))
                TS(f, f, 0.5, -0.5, ALU.min, ALU.max).then_inc(S["s5_phase"], 1)

            def states(st):
                e = st % 2
                re, im, cs, sn = bank[4][:, :], bank[5][:, :], s5_cos[:, e], s5_sin[:, e]
                pr = [s5_pr[:, i] for i in range(4)]
                v = s5_v[e]
                V.wait_ge(S["s5_bu"], st + 1)
                V.wait_ge(S["s5_trig"], 2 * (st + 1))
                if st:
                    V.wait_ge(S["s5_state"], st)
                do(TT(pr[0], re, cs, MUL))
                n = do(TT(pr[1], im, sn, MUL))
                do(TT(pr[2], im, cs, MUL))
                TT(pr[3], re, sn, MUL).then_inc(S["s5_bu_used"], 1)
                need(n)
                if st >= 2:
                    V.wait_ge(S["s5_sim"], st - 1)
                n = do(TT(v[:, 0], pr[0], pr[1], ADD))
                V.wait_ge(S["s5_bu_used"], st + 1)
                m = do(TT(v[:, 1], pr[2], pr[3], SUB))
                mag = K(3)[:, st:st + 1].broadcast_to([P, SEQ])
                need(n)
                V.tensor_tensor_scan(v[:, 0], mag, v[:, 0], 0.0, MUL, ADD).then_inc(S["s5_z"], 1)
                need(m)
                V.tensor_tensor_scan(v[:, 1], mag, v[:, 1], 0.0, MUL, ADD).then_inc(S["s5_z"], 1)
                V.wait_ge(S["s5_z"], 2 * st + 1)
                do(TT(pr[0], v[:, 0], cs, MUL))
                V.wait_ge(S["s5_z"], 2 * st + 2)
                chain(TT(pr[1], v[:, 1], sn, MUL))
                if st >= 2:
                    V.wait_ge(S["s5_y"], st - 1)
                TT(s5_s[:, e, 0], pr[0], pr[1], SUB).then_inc(S["s5_state"], 1)

            def skip(jt):
                V.wait_ge(S["s5_y"], 4 * (jt + 1))
                STT(s5_u[:, jt], s5_u[:, jt], PC("s5_d", jt), bank[6][:, :], MUL, ADD).then_inc(S["s5_y_used"], 1)

            def s5(st):
                if st + 1 < S5_TILES:
                    phases(st + 1)
                states(st)
                if st % 4 == 1 and st > 4:
                    skip(st // 4 - 1)

            def s5_end():
                skip(3)
                for i in range(4):
                    V.wait_ge(S["gel_hi_done"], i + 1)
                    TT(gel_lo[:, i], gel[:, i % 2], gel_hi[:, i].bitcast(f32), SUB).then_inc(S["gel_done"], 1)

            def glu(i):
                n = LOT_AT[("glu", i)]
                t = OUT0[n]
                wait_out(V, t)
                wait_taken(V, t + 1)
                if i >= 2:
                    V.wait_ge(S["y_done"], i - 1)
                STT(glu_y[:, i % 2], glu_th[:, i % 2], 1.0, bank[t % 4][:, :], ADD, MUL).then_inc(free[t % 4], 1)
                wait_taken(V, t)
                V.sem_inc(S["glu_y_done"], 1)
                low_y(1, i, glu_y[:, i % 2], 0.5)

            def da_norm(g, phase):
                gain = ("q_norm", "k_norm")[g]
                for j in range(4 if phase == 0 else 0):
                    V.wait_ge(S["da_rms"], 4 * g + j + 1)
                    chain(V.reciprocal(da_t[:, j], da_t[:, j]))
                    STT(da_qk[:, 4 * g + j], da_qk[:, 4 * g + j], PR(gain), da_t[:, j], MUL, MUL) \
                        .then_inc(S["da_qn"], 1)
                for j in range(4 if phase == 1 else 0):
                    V.wait_ge(S["da_rot"], 4 * g + j + 1)
                    V.wait_ge(S["da_qn"], 4 * g + j + 1)
                    do(TT(da_t[:, j], bank[4 + j][:, :], rope_sin[:, :], MUL))
                    chain(TT(da_qk[:, 4 * g + j], da_qk[:, 4 * g + j], rope_cos[:, :], MUL))
                    TT(da_qk[:, 4 * g + j], da_qk[:, 4 * g + j], da_t[:, j], ADD).then_inc(S["da_rot_done"], 1)
            def da_index(b):
                if b == 1:
                    wait_taken(V, out_at("small", 0))
                    chain(V.tensor_copy(da_mb[:, 0:P], C("cmask")))
                w = P * (b + 1)
                for hh in range(4):
                    V.wait_ge(S["da_relu"], 4 * (b - 1) + hh + 1)
                    sc, r, wi = da_sc[:, 0:w], da_r[:, hh, 0:w], small[:, b, hh:hh + 1]
                    if hh == 0:
                        chain(TS(sc, r, wi, None, MUL))
                    elif hh < 3:
                        chain(STT(sc, r, wi, sc, MUL, ADD))
                    else:
                        STT(sc, r, wi, sc, MUL, ADD).then_inc(S["da_score"], 1)
                V.wait_ge(S["da_score"], b)
                chain(TT(da_sc[:, P * b:w], da_sc[:, P * b:w], C("cmask"), ADD))

            def da_topk(b):
                w = P * (b + 1)
                src = da_sc
                for r in range(TOPK // 8):
                    chain(V.max(da_m8[:, :], src[:, 0:w]))
                    chain(V.match_replace(da_wk[:, 0:w], da_m8[:, :], src[:, 0:w], TAKEN))
                    src = da_wk
                chain(TS(da_mb[:, DA_OFF[b]:DA_OFF[b] + w], da_wk[:, 0:w], -2.0e38, NEG, ALU.is_gt, MUL))
                if b == NB - 1:
                    V.sem_inc(S["da_idx_done"], 1)

            def masked(u):
                hp, b, e = UNITS[u]
                w = P * (b + 1)
                V.wait_ge(S["da_logit"], u + 1)
                if u >= 2:
                    V.wait_ge(S["da_exp"], u - 1)
                chain(V.tensor_tensor_reduce(out=da_lg[:, u % 2, 0:w], in0=bank[4 + u % 2][:, 0:w],
                                             in1=da_mb[:, DA_OFF[b]:DA_OFF[b] + w], scale=1.0, scalar=TAKEN,
                                             op0=ADD, op1=ALU.max, accum_out=da_st[:, u, 0:1]))
                TS(da_st[:, u, 1:2], da_st[:, u, 0:1], -0.125, None, MUL).then_inc(S["da_max"], 1)

            def normalise(u):
                hp, b, e = UNITS[u]
                w = P * (b + 1)
                V.wait_ge(S["da_exp"], u + 1)
                chain(V.reciprocal(da_st[:, u, 3:4], da_st[:, u, 2:3]))
                TS(da_p[:, u % 2, 0:w], da_p[:, u % 2, 0:w], da_st[:, u, 3:4], None, MUL).then_inc(S["da_prob"], 1)
            def att_start():
                masked(0)

            def att(u):
                if u < 31:
                    masked(u + 1)
                normalise(u)
                if u % 8 == 1 and u > 8:
                    low_y(2, u // 8 - 1, bank[7][:, :])

            def att_end():
                low_y(2, 3, bank[7][:, :])

            D = lambda i: m2_dt[:, i]
            heads = lambda a: a.unsqueeze(1).broadcast_to([P, NB, 8])

            def m2_dt_():
                TT(D(0), small[:, :, 4:12], heads(PR("dt_bias")), ADD).then_inc(S["m2_dtb"], 1)
                V.wait_ge(S["m2_dtb"], 1)
                STT(D(1), D(0), -1.0, D(0), MUL, ALU.max).then_inc(S["m2_dtb"], 1)

            def m2_conv():
                chain(V.memset(m2_xr[:, :, 0:3], 0.0))
                n = {}
                for k in (3, 2, 1, 0):
                    for i in range(6):
                        xs, wk = m2_xr[:, i, k:k + SEQ], PC("conv_w", 6 * k + i)
                        if k == 3:
                            wait_taken(V, out_at("xbc", i))
                            n[i] = do(TS(m2_xc[:, i], xs, wk, PC("conv_b", i), MUL, ADD))
                        else:
                            need(n[i])
                            ins = STT(m2_xc[:, i], xs, wk, m2_xc[:, i], MUL, ADD)
                            if k:
                                n[i] = do(ins)
                            else:
                                ins.then_inc(S["m2_conv"], 1)
                V.wait_ge(S["m2_abs"], 2)
                chain(STT(D(0), D(0), 0.0, D(1), ALU.max, ADD))
                STT(D(1), D(0), -1.0, heads(m2_ea[:, :]), MUL, MUL).then_inc(S["m2_dt_ready"], 1)

            def m2_prep():
                V.wait_ge(S["m2_acs"], 1)
                V.tensor_copy(D(2).rearrange("p b h -> p (b h)"), bank[4][:, 0:32]).then_inc(S["m2_acs_done"], 1)
                V.wait_ge(S["m2_acs_done"], 1)
                for b in range(NB):
                    V.wait_ge(S["m2_ct"], b + 1)
                    TT(m2_xdt[:, b].rearrange("p (h d) -> p h d", d=64),
                       bank[5 + b % 2][:, :].rearrange("p (h d) -> p h d", d=64),
                       D(0)[:, b].unsqueeze(2).broadcast_to([P, 8, 64]), MUL).then_inc(S["m2_xdt_done"], 1)
                for c in range(8):
                    g, j = c // 4, c % 4
                    V.wait_ge(S["m2_cbp"], c + 1)
                    w = SEQ - P * j
                    TT(m2_cb[:, g, M2_OFF[j]:M2_OFF[j] + w], bank[4 + 3 * (c % 2)][:, 0:w], C("upper", 0, w), MUL) \
                        .then_inc(S["m2_cb_done"], 1)
                V.wait_ge(S["m2_cb_done"], 8)

            def segments(h):
                V.wait_ge(S["m2_acb"], h + 1)
                if h >= 2:
                    V.wait_ge(S["m2_yp"], h - 1)
                for j in range(NB):
                    ins = TS(m2_e[:, h % 2, M2_OFF[j]:M2_OFF[j] + SEQ - P * j], bank[4 + h % 2][:, P * j:SEQ],
                             D(2)[:, j, h:h + 1], 0.0, SUB, ALU.min)
                    if j < NB - 1:
                        do(ins)
                ins.then_inc(S["m2_seg"], 1)

            def y_of(hp):
                V.wait_ge(S["m2_yp"], 2 * hp + 2)
                STT(m2_yv[:, hp], m2_xc[:, hp], PC("m2_d", hp), bank[6 + hp % 2][:, :], MUL, ADD) \
                    .then_inc(S["m2_y"], 1)
            def m2_head(h):
                if h == 0:
                    segments(0)
                V.wait_ge(S["m2_decay"], h + 1)
                TT(m2_e[:, h % 2], m2_e[:, h % 2], m2_cb[:, h // 4], MUL).then_inc(S["m2_m"], 1)
                if h < 7:
                    segments(h + 1)
                if h >= 2 and h % 2 == 0:
                    y_of(h // 2 - 1)

            def m2_norm():
                y_of(3)
                V.wait_ge(S["m2_zs"], 4)
                for i in range(BT):
                    V.wait_ge(S["m2_y"], i + 1)
                    TT(m2_yv[:, i], m2_yv[:, i], m2_z[:, i], MUL).then_inc(S["m2_yn"], 1)

            def m2_end():
                V.wait_ge(S["m2_rms"], 1)
                chain(V.reciprocal(m2_rs[:, :], m2_rs[:, :]))
                for i in range(BT):
                    STT(m2_yv[:, i], m2_yv[:, i], PC("m2_norm", i), m2_rs[:, :], MUL, MUL).then_inc(S["m2_yn"], 1)
                for i in range(BT):
                    low_y(0, i, m2_yv[:, i])

            def hg_start():
                V.wait_ge(S["y_done"], BT * (TURN[0] + 1))
                V.wait_ge(S["m2_yn"], 2 * BT)
                do(V.memset(hatt[:, :, :], 0.0))
                chain(V.tensor_copy(hlb[:, 0], lower[:, layer_at[0]]))
                chain(TS(hlb[:, 1], hlb[:, 0], -1.0, 1.0, MUL, ADD))

            chunks = lambda a: a.rearrange("p (c t) -> p c t", t=HG_CHUNK)

            def hg_gates(h, phase):
                X = [he[:, h % 2, i] for i in range(4)]
                if phase == 0:
                    V.wait_ge(S["hg_e"], h + 1)
                    do(TS(X[0], X[0], 1.0, None, ADD))
                    chain(TS(hf[:, h], hf[:, h], 1.0, None, ADD))
                    n = do(V.reciprocal(X[0], X[0]))
                    m = do(V.reciprocal(hf[:, h], hf[:, h]))
                    need(n)
                    TS(X[0], X[0], hlb[:, 1, h:h + 1], hlb[:, 0, h:h + 1], MUL, ADD).then_inc(S["hg_fg"], 1)
                    need(m)
                    chain(TS(hf[:, h], hf[:, h], hlb[:, 1, h:h + 1], None, MUL))
                elif phase == 1:
                    V.wait_ge(S["hg_lf"], h + 1)
                    V.tensor_tensor_scan(X[1], C("hgreset"), X[0], 0.0, MUL, ADD).then_inc(S["hg_cum"], 1)
                    V.wait_ge(S["hg_cum"], h + 1)
                    cum = chunks(X[1])
                    TT(chunks(X[3]), cum[:, :, HG_CHUNK - 1:HG_CHUNK].broadcast_to([P, NCH, HG_CHUNK]), cum, SUB) \
                        .then_inc(S["hg_lc"], 1)
                else:
                    V.wait_ge(S["hg_ex"], 4)
                    V.wait_ge(S["hg_ec"], 3 * h + 3)
                    TT(hq[:, h], hq[:, h], X[0], MUL).then_inc(S["hg_ke"], 1)
                    TT(X[2], hf[:, h], X[2], MUL).then_inc(S["hg_ke"], 1)
                    V.wait_ge(S["hg_el"], h + 1)
                    TT(X[3], hf[:, h], X[3], MUL).then_inc(S["hg_ke"], 1)

            def hg_head(h, phase):
                if phase == 0:
                    V.wait_ge(S["hg_attp"], h + 1)
                    V.copy_predicated(hatt[:, :, :], C("hgmask").bitcast(u32).unsqueeze(1).broadcast_to([P, NB, P]),
                                      bank[4][:, :].rearrange("p (b q) -> p b q", q=P)).then_inc(S["hg_att"], 1)
                elif phase == 1:
                    V.wait_ge(S["hg_upd"], h + 1)
                    for c in range(NCH - 1):
                        new = bank[4 + c % 4][:, P * (c // 4):P * (c // 4 + 1)]
                        if c == 0:
                            ins = V.tensor_copy(hS[:, 1], new)
                        else:
                            ins = STT(hS[:, c + 1], hS[:, c], hdec[:, h % 2, c:c + 1], new, MUL, ADD)
                        if c == NCH - 2:
                            ins.then_inc(S["hg_updu"], 1)
                        else:
                            chain(ins)

            def hg_norm():
                for h in range(4):
                    V.wait_ge(S["hg_rms"], h + 1)
                    chain(V.reciprocal(he[:, 0, h], he[:, 0, h]))
                    chain(STT(hf[:, h], hf[:, h], PC("hg_norm", h), he[:, 0, h], MUL, MUL))
                    wait_taken(V, out_at("hg", h))
                    STT(he[:, 1, h], hg[:, h], 1.0, hf[:, h], ADD, MUL).then_inc(S["hg_yn"], 1)
                for h in range(4):
                    low_y(3, h, he[:, 1, h], 0.5)

            layer_at = [None]

            STEPS = dict(lot=lot, pair=pair, out=out, out_start=out_start, glu=glu, gate=gate, branch=branch,
                         s5_prep=s5_prep, s5=s5,
                         s5_end=s5_end, da_norm=da_norm, da_index=da_index, da_topk=da_topk, att_start=att_start,
                         att=att, att_end=att_end, m2_dt=m2_dt_, m2_conv=m2_conv, m2_prep=m2_prep, m2_head=m2_head,
                         m2_norm=m2_norm, m2_end=m2_end, hg_start=hg_start, hg_gates=hg_gates, hg_head=hg_head,
                         hg_norm=hg_norm)

            def mixing(layer):
                layer_at[0] = layer
                for step in SCRIPT:
                    STEPS[step[0]](*step[1:])

            V.memset(epsc[:, :], EPS).then_inc(S["p_seq"], 1)
            V.memset(half_pi[:, :], PI / 2).then_inc(S["p_seq"], 1)
            V.memset(roundc[:, :], ROUND).then_inc(S["p_seq"], 1)
            p = Order(V, S["p_seq"])
            p.n = 3

            def pdo(ins):
                p.need(p.do(ins))
            V.wait_ge(S["c_pos"], 16)
            V.wait_ge(S["c_con"], 16)
            pdo(V.tensor_copy(ang[:, 2], pos_i[:, :]))
            pdo(V.tensor_scalar(ang[:, 0], ang[:, 2], C("invfreq"), None, MUL))
            pdo(V.tensor_scalar(ang[:, 1], ang[:, 0], 1.0 / (2 * PI), ROUND, MUL, ADD))
            pdo(V.tensor_scalar(ang[:, 1], ang[:, 1], -ROUND, None, ADD))
            c1 = 6.28125
            c2 = float(np.float32(2 * PI - c1))
            c3 = 2 * PI - c1 - c2
            for c in (c1, c2, c3):
                pdo(V.scalar_tensor_tensor(ang[:, 0], ang[:, 1], -c, ang[:, 0], MUL, ADD))
            V.tensor_scalar(ang[:, 0], ang[:, 0], float(np.float32(3.1415925)), -float(np.float32(3.1415925)), ALU.min, ALU.max) \
             .then_inc(S["p_ang"], 1)
            V.wait_ge(S["p_ang"], 1)
            V.scalar_tensor_tensor(ang[:, 1], ang[:, 0], -1.0, ang[:, 0], MUL, ALU.max).then_inc(S["p_ang"], 1)
            V.wait_ge(S["c_gam"], 16)
            pdo(V.tensor_copy(gtmp[:, 2, 0], gam[:, 0]))
            for l in range(1, DEPTH):
                pdo(V.tensor_tensor(gtmp[:, 2, 0], gtmp[:, 2, 0], gam[:, l], ALU.max))
            for l in range(DEPTH):
                ins = V.tensor_tensor(gtmp[:, 0, l], gam[:, l], gtmp[:, 2, 0], SUB)
                if l < DEPTH - 1:
                    pdo(ins)
            ins.then_inc(S["p_gam1"], 1)
            V.wait_ge(S["p_trig"], 3)
            pdo(V.tensor_copy(gtmp[:, 3, 0], gtmp[:, 1, 0]))
            for l in range(1, DEPTH):
                pdo(V.tensor_tensor(gtmp[:, 3, 0], gtmp[:, 3, 0], gtmp[:, 1, l], ADD))
            pdo(V.reciprocal(gtmp[:, 3, 0], gtmp[:, 3, 0]))
            pdo(V.memset(lower[:, 0], 0.0))
            for l in range(1, DEPTH):
                pdo(V.tensor_tensor(gtmp[:, 4, 0], gtmp[:, 1, l], gtmp[:, 3, 0], MUL))
                pdo(V.tensor_tensor(lower[:, l], lower[:, l - 1], gtmp[:, 4, 0], ADD))
            V.sem_inc(S["p_gam2"], 1)
            with V.Fori(0, DEPTH) as layer:
                seq.n = 0
                for n in range(4):
                    split_lo(V, n)
                norm(0, "ffn1_norm")
                ffn(0, 0)
                norm(1, "mix_norm")
                mixing(layer)
                norm(2, "ffn2_norm")
                V.wait_ge(S["lo_done"], FFN2_0 + 4)
                ffn(1, FFN2_0)
                end_of_layer(V, S["go_dve"])


def kernel(**inputs):
    import numpy as _np
    import concourse.bacc as _bacc
    from concourse import mybir as _mybir
    from concourse.bass_utils import run_bass_kernel_spmd as _run

    a = {k: _np.asarray(v) for k, v in inputs.items()}

    def lots(w):
        L, K, M = w.shape
        pad = -M % P
        if pad:
            w = _np.concatenate([w, _np.zeros((L, K, pad), w.dtype)], 2)
        return w.reshape(L, K // P, P, (M + pad) // P, P).transpose(0, 3, 2, 1, 4)

    def ffn_lots(w1, w3, w2):
        w1, w3, got, j0 = lots(w1), lots(w3), [], 0
        for J in THIRDS:
            for j in range(j0, j0 + J):
                got += [w1[:, j], w3[:, j]]
            w = lots(w2[:, P * j0:P * (j0 + J)])
            fill = _np.zeros((DEPTH, P, 8 - J, P), w.dtype)
            for i in range(KT):
                got.append(_np.concatenate([w[:, i], fill], 2))
            j0 += J
        return got

    w_in = a["w_in"]
    m2, s5, da = 0, 2 * BW + 256 + 8, 3 * BW + 256 + 8
    hg = da + 3 * BW + 256 + 64 + 4
    parts = dict(z=lots(w_in[:, :, 0:BW]), xbc=lots(w_in[:, :, BW:2 * BW + 256]), u=lots(w_in[:, :, s5:s5 + BW]),
                 q=lots(w_in[:, :, da:da + BW]), k=lots(w_in[:, :, da + BW:da + 2 * BW]),
                 v=lots(w_in[:, :, da + 2 * BW:da + 3 * BW]), qi=lots(w_in[:, :, da + 3 * BW:da + 3 * BW + 256]))
    ki = w_in[:, :, da + 3 * BW + 256:da + 3 * BW + 320]
    parts["ki"] = lots(_np.concatenate([ki, ki], 2))
    parts["small"] = lots(_np.concatenate([w_in[:, :, hg - 4:hg], w_in[:, :, s5 - 8:s5]], 2))
    for i, name in enumerate(("hq", "hf", "hv", "hg")):
        parts[name] = lots(w_in[:, :, hg + BW * i:hg + BW * (i + 1)])
    for g in range(4):
        parts["gate%d" % g] = lots(a["w_gate"][:, :, DM * g:DM * (g + 1)])
        w = lots(a["w_branch"][:, g])
        parts["branch%d" % g] = _np.concatenate([w[:, 0::2], w[:, 1::2]], 3)
    w = lots(a["s5_w_glu"])
    parts["glu"] = _np.concatenate([w[:, 0:4], w[:, 4:8]], 3)
    parts["out"] = lots(a["w_out"])
    stream = ffn_lots(a["ffn1_w1"], a["ffn1_w3"], a["ffn1_w2"]) + [parts[kind][:, i] for kind, i in MIX] \
        + ffn_lots(a["ffn2_w1"], a["ffn2_w3"], a["ffn2_w2"])
    w_lots = _np.stack(stream, 1).reshape(DEPTH * NLOT, P, 8 * P)

    def cols(v):
        return v.reshape(DEPTH, -1, P).transpose(0, 2, 1)

    def rows(v):
        return _np.repeat(v[:, None, :], P, 1)

    par = dict(ffn1_norm=cols(a["ffn1_norm"]), mix_norm=cols(a["mix_norm"]), ffn2_norm=cols(a["ffn2_norm"]),
               conv_w=_np.concatenate([cols(a["m2_conv_w"][:, k]) for k in range(4)], 2), conv_b=cols(a["m2_conv_b"]),
               dt_bias=rows(a["m2_dt_bias"]), a_log=rows(a["m2_a_log"]), m2_d=cols(_np.repeat(a["m2_d"], 64, 1)),
               m2_norm=cols(a["m2_norm"]), lam_re=cols(a["s5_lam_re"].reshape(DEPTH, -1)),
               lam_im=cols(a["s5_lam_im"].reshape(DEPTH, -1)), log_dt=cols(_np.repeat(a["s5_log_dt"], 64, 1)),
               s5_d=cols(a["s5_d"]), q_norm=cols(_np.tile(a["dsa_q_norm"], 2)), k_norm=cols(_np.tile(a["dsa_k_norm"], 2)),
               hg_norm=cols(a["hg_norm"]))
    par = _np.concatenate([par[k] for k in PAR_SIZES], 2)

    s5_in = _np.zeros((DEPTH, P, 4, 16, 32), _np.float32)
    for i, (name, perm) in enumerate((("s5_b_re", None), ("s5_b_im", None), ("s5_c_re", 1), ("s5_c_im", 1))):
        v = a[name] if perm is None else a[name].transpose(0, 1, 3, 2)
        v = v.reshape(DEPTH, 16, 2, 64, 16)
        for e in range(2):
            s5_in[:, 64 * e:64 * e + 64, i, :, 16 * e:16 * e + 16] = v[:, :, e].transpose(0, 2, 1, 3)

    con = _np.zeros((P, NCON), _np.float32)
    r = _np.arange(P)

    def put(name, v):
        con[:, CON_AT[name]:CON_AT[name] + CON_SIZES[name]] = v
    t = _np.arange(SEQ)
    put("ident", _np.eye(P))
    put("upper", t[None, :] >= r[:, None])
    put("blk", r[:, None] // 64 == r[None, :] // 64)
    put("rot", -1.0 * ((r[None, :] % 64 < 32) & (r[:, None] == r[None, :] + 32))
        + ((r[None, :] % 64 >= 32) & (r[:, None] == r[None, :] - 32)))
    put("hgmask", (r[:, None] // HG_CHUNK == r[None, :] // HG_CHUNK) & (r[:, None] <= r[None, :]))
    put("hgreset", (t % HG_CHUNK != 0)[None, :])
    put("tvec", t[None, :])
    put("cmask", _np.where(r[None, :] <= r[:, None], 0.0, NEG))
    put("invfreq", (_np.float32(10000.0) ** (-(r % 32).astype(_np.float32) / _np.float32(32)))[:, None])

    gamma = a["hg_gamma"].reshape(DEPTH, 4, P).transpose(2, 0, 1)
    arrays = dict(x=a["x"].reshape(SEQ, DM), positions=a["positions"].reshape(SEQ), w_lots=w_lots, par=par,
                  s5=s5_in.reshape(DEPTH, P, 2048), con=con, gamma=gamma)
    nc = _bacc.Bacc("TRN2", target_bir_lowering=False, num_devices=1)
    args, feed = [], {}
    for name, v in arrays.items():
        feed["in_" + name] = _np.ascontiguousarray(v)
        args.append(nc.dram_tensor("in_" + name, v.shape, _mybir.dt.from_np(v.dtype), kind="ExternalInput").ap())
    args.append(nc.dram_tensor("out_x", (SEQ, DM), _mybir.dt.float32, kind="ExternalOutput").ap())
    trunk(nc, *args)
    r = _run(nc, [feed], core_ids=[0])
    return r.results[0]["out_x"].reshape(1, SEQ, DM)
```

```python
import math
import numpy as np
import concourse.bass as bass
from concourse import mybir
from contextlib import ExitStack

DEPTH, SEQ, DM, DFF = 2, 512, 1024, 2816
BW = DM // 2
P = 128
KT = DM // P
NB = SEQ // P
BT = BW // P
EPS = 1e-6
TOPK = min(256, SEQ // 4)
HG_CHUNK = 32
NCH = SEQ // HG_CHUNK
S5_TILES = 16
PI = math.pi
ROUND = 12582912.0
ROUND13 = 1536.0
NEG = -1.0e30
TAKEN = -3.0e38

FF_TILES = DFF // P
THIRDS = [8, 8, 6]
FFN_LOTS = 2 * FF_TILES + KT * len(THIRDS)


ORDER = (1, 2, 0, 3)
TURN = {g: i for i, g in enumerate(ORDER)}


TOPK_PHASES = 8
HG_FILL = (1, 2, 1)
UNITS_BEFORE_TOPK = 22


def script():
    def lots(*kinds):
        return [("lot", k, i) for k, n in kinds for i in range(n)]

    def weave(steps, fill):
        out, used = [], 0
        for i, step in enumerate(steps):
            out.append(step)
            upto = (i + 1) * len(fill) // len(steps)
            out += fill[used:upto]
            used = upto
        return out

    def phases(name, i, n=3):
        return [(name, i, phase) for phase in range(n)]

    def merges(g, a=0, b=KT // 2):
        return [step for pair in range(a, b)
                for step in (("gate", g, 2 * pair), ("gate", g, 2 * pair + 1), ("branch", g, pair))]

    def glus(a, b):
        return [("glu", i) for i in range(a, b)]
    s = [("s5_prep", 0)] + lots(("u", 4), ("small", 1)) + [("s5_prep", 1), ("turn_small",)]
    s += weave([("s5", st) for st in range(S5_TILES)], lots(("q", 4), ("k", 4), ("qi", 2), ("ki", 1)) + [("pair", "v", 0)])
    topk = [phases("da_topk", b, TOPK_PHASES) for b in range(NB)]
    s += [("s5_end",), ("pair", "v", 2)]
    s += weave([("da_index", 1)] + topk[1] + [("da_index", 2), ("da_index", 3), ("da_norm", 0, 0)] + topk[2][0:1]
               + [("da_norm", 0, 1), ("da_norm", 1, 0)] + topk[2][1:3] + [("da_norm", 1, 1)] + topk[2][3:4],
               glus(0, 4) + merges(1, 0, 2))
    s += [("att_start",)]
    picks, n = topk[2][4:] + topk[3], UNITS_BEFORE_TOPK
    steps = [step for u in range(n)
             for step in [("att", u)] + picks[u * len(picks) // n:(u + 1) * len(picks) // n]]
    n = steps.index(("att", 15))
    s += weave(steps[:n], merges(1, 2, 4)) + steps[n:] + weave([("att", u) for u in range(UNITS_BEFORE_TOPK, 32)], lots(("xbc", 6))) + [("att_end",)]
    s += [("m2_decay",)] + lots(("z", 4)) + [("m2_conv",)] + merges(2, 0, 1)
    s += weave([("m2_prep", phase) for phase in range(5)] + [("m2_head", h) for h in range(8)], merges(2, 1, 4))
    s += lots(("hf", 1)) + [("m2_norm",)] + [("lot", "hf", i) for i in (1, 2, 3)] + lots(("hq", 2))
    s += [("m2_end",), ("lot", "hq", 2), ("lot", "hq", 3), ("hg_start",)]
    s += [("hg_gates", 0, 0), ("pair", "hv", 0), ("hg_gates", 0, 1), ("pair", "hv", 2), ("hg_gates", 0, 2),
          ("lot", "hg", 0)]
    fill = [("lot", "hg", i) for i in (1, 2, 3)] + merges(0)
    for h in range(4):
        for phase, n in enumerate(HG_FILL):
            s += [("hg_head", h, phase)] + ([("hg_gates", h + 1, phase)] if h < 3 else []) + fill[:n]
            fill = fill[n:]
        s += [("hg_norm", h)]
    s += fill
    last = merges(3)
    s += [("hg_end",)] + last[:-1] + [("out_start", 0)] + last[-1:] + [("out_start", 1)] + [("out", i) for i in range(KT)]
    return s


SCRIPT = script()


def mix_lots():
    lots = []
    for step in SCRIPT:
        if step[0] == "lot":
            lots.append(step[1:])
        elif step[0] == "pair":
            lots += [(step[1], step[2]), (step[1], step[2] + 1)]
        elif step[0] in ("glu", "out"):
            lots.append(step)
        elif step[0] in ("gate", "branch"):
            lots.append((step[0] + str(step[1]), step[2]))
    return lots


MIX = mix_lots()
MIX_LOTS = len(MIX)
NLOT = 2 * FFN_LOTS + MIX_LOTS
MIX0, FFN2_0 = FFN_LOTS, FFN_LOTS + MIX_LOTS


def outputs_of(kind):
    return 2 if kind == "glu" or kind.startswith("branch") else 1


OUT0 = [0]
for _n in range(NLOT):
    _mixing = FFN_LOTS <= _n < FFN_LOTS + MIX_LOTS
    OUT0.append(OUT0[-1] + (outputs_of(MIX[_n - FFN_LOTS][0]) if _mixing else 1))
USED_AT = [OUT0[_n + 1] for _n in range(NLOT)]
for _i, (_kind, _j) in enumerate(MIX):
    if _kind in ("v", "hv") and _j % 2 == 0:
        USED_AT[MIX0 + _i] += 1
        assert (MIX0 + _i) % 4 != 3, (_kind, _j, (MIX0 + _i) % 4)
LOT_AT = {MIX[_i]: MIX0 + _i for _i in range(MIX_LOTS)}


def out_at(kind, i, half=0):
    return OUT0[LOT_AT[(kind, i)]] + half


PAR_SIZES = dict(ffn1_norm=8, mix_norm=8, ffn2_norm=8, conv_w=24, conv_b=6, dt_bias=8, a_log=8, m2_d=4,
                 m2_norm=4, lam_re=16, lam_im=16, log_dt=16, s5_d=4, q_norm=1, k_norm=1, hg_norm=4)
PAR_AT, NPAR = {}, 0
for _name, _n in PAR_SIZES.items():
    PAR_AT[_name] = NPAR
    NPAR += _n
CON_SIZES = dict(ident=128, upper=512, blk=128, rot=128, hgmask=128, hgreset=512, tvec=512, cmask=128,
                 invfreq=8)
CON_AT, NCON = {}, 0
for _name, _n in CON_SIZES.items():
    CON_AT[_name] = NCON
    NCON += _n
UNITS = [(hp, b, e) for b in range(NB) for hp in range(4) for e in range(2)]
DA_OFF = [P * b * (b + 1) // 2 for b in range(NB)]
M2_OFF = [0, SEQ, 2 * SEQ - P, 3 * SEQ - 3 * P]


TILE = SEQ * 4
X_AT, H_AT, RING_AT = 0, 8, 24
MERGED_AT, YHL_AT, ARENA_AT = 48, 56, 64
CON_OFF = 97 * TILE + 96


def trunk(nc, x_in, positions, w_lots, par_in, s5_in, con_in, gamma_in, out):
    f32, f32r, i32, u32 = mybir.dt.float32, mybir.dt.float32r, mybir.dt.int32, mybir.dt.uint32
    ALU, ACT, AX = mybir.AluOpType, mybir.ActivationFunctionType, mybir.AxisListType
    MUL, ADD, SUB = ALU.mult, ALU.add, ALU.subtract
    AFT = ACT
    ctx = ExitStack()
    with ctx:
        def at(name, shape, dt, tile, byte=0):
            return nc.alloc_sbuf_tensor_at(name, shape, dt, offset=BASE + tile * TILE + byte)

        BASE = -(-nc.sbuf_base // 32) * 32

        x = at("x", [P, KT, SEQ], f32, X_AT)
        h_hi = at("h_hi", [P, KT, SEQ], f32r, H_AT)
        h_lo = at("h_lo", [P, KT, SEQ], f32r, H_AT + 8)
        raw = at("raw", [P, 4, 8, P], f32, RING_AT)
        w_hi = at("w_hi", [P, 4, 8, P], f32r, RING_AT + 8)
        w_lo = at("w_lo", [P, 4, 8, P], f32r, RING_AT + 16)
        merged = at("merged", [P, KT, SEQ], f32, MERGED_AT)
        y_hi = at("y_hi", [P, BT, SEQ], f32r, YHL_AT)
        y_lo = at("y_lo", [P, BT, SEQ], f32r, YHL_AT + 4)
        con = at("con", [P, NCON], f32, 0, CON_OFF)
        par_off = CON_OFF + -(-4 * NCON // 32) * 32
        par = at("par", [P, NPAR], f32, 0, par_off)
        tail = par_off + -(-4 * NPAR // 32) * 32
        lower = at("lower", [P, DEPTH, 4], f32, 0, tail)
        roundc = at("roundc", [P, 1], f32, 0, tail + 704 + 2 * TILE)
        eps_warm = at("eps_warm", [P, 2], f32, 0, tail + 32)
        epsc, warm = eps_warm[:, 0:1], eps_warm[:, 1:2]
        half_pi = at("half_pi", [P, 1], f32, 0, tail + 64)
        rope_cos = at("rope_cos", [P, SEQ], f32, 0, tail + 96)
        rope_sin = at("rope_sin", [P, SEQ], f32, 0, tail + 96 + TILE)

        def C(name, a=0, b=None):
            k = CON_AT[name]
            return con[:, k + a:k + (CON_SIZES[name] if b is None else b)]

        def PR(name, a=0, b=None):
            k = PAR_AT[name]
            return par[:, k + a:k + (PAR_SIZES[name] if b is None else b)]

        def PC(name, i):
            return PR(name, i, i + 1)

        ident, ones = C("ident"), C("upper", P, 2 * P)

        small = at("small", [P, NB, 12], f32, 0, tail + 96 + 2 * TILE)
        small_t = at("small_t", [P, SEQ], f32, ARENA_AT + 26)
        m2_dt = at("m2_dt", [P, 3, NB, 8], f32, 0, tail + 288 + 2 * TILE)
        m2_ea = at("m2_ea", [P, 8], f32, 0, tail + 672 + 2 * TILE)
        A, M, Y = ARENA_AT, MERGED_AT, YHL_AT

        g_hi = at("g_hi", [P, 8, SEQ], f32r, M)
        g_lo = at("g_lo", [P, 8, SEQ], f32r, Y)
        silu_a = at("silu_a", [P, 2, SEQ], f32, A)
        gated = at("gated", [P, 2, SEQ], f32, A + 2)
        sq = at("sq", [P, 2, SEQ], f32, A + 28)
        sq_sum = at("sq_sum", [P, SEQ], f32, A + 27)
        rms = at("rms", [P, NB], f32, A + 30)
        normed = at("normed", [P, 2, SEQ], f32, A + 31)
        gate_th = at("gate_th", [P, 2, SEQ], f32, A + 10)

        s5_u = at("s5_u", [P, 4, SEQ], f32, A)
        s5_bc = at("s5_bc", [P, 4, 16, 32], f32, A + 4)
        s5_bb = at("s5_bb", [P, 2, 16, 32], f32, A + 8)
        s5_bbt = at("s5_bbt", [P, 2, 4, P], f32, A + 10)
        s5_k = at("s5_k", [P, 21, 16], f32, A + 32)
        s5_v0 = at("s5_v0", [P, 2, SEQ], f32, A + 4)
        s5_v1 = at("s5_v1", [P, 2, SEQ], f32, A + 8)
        s5_v = [s5_v0, s5_v1]
        s5_cos = at("s5_cos", [P, 2, SEQ], f32, M)
        s5_sin = at("s5_sin", [P, 2, SEQ], f32, M + 2)
        s5_ph = at("s5_ph", [P, 4, SEQ], f32, M + 4)
        s5_pr = at("s5_pr", [P, 4, SEQ], f32, Y)
        s5_s = at("s5_s", [P, 2, 2, SEQ], f32, Y + 4)
        s5_vs = at("s5_vs", [P, SEQ], f32, A + 29)
        s5_pq = at("s5_pq", [P, 2, SEQ], f32, A + 27)
        gel = at("gel", [P, 2, SEQ], f32, A + 8)
        gel_hi = at("gel_hi", [P, 4, SEQ], f32r, M)
        gel_lo = at("gel_lo", [P, 4, SEQ], f32r, M + 4)
        glu_th = at("glu_th", [P, 2, SEQ], f32, A + 4)
        glu_y = at("glu_y", [P, 2, SEQ], f32, A + 6)

        da_mb = at("da_mb", [P, 1280], f32, A)
        da_st = at("da_st", [P, 32, 4], f32, A + 2, TILE // 2)
        da_m8 = at("da_m8", [P, 8], f32, A + 2, TILE // 2 + 512)
        da_sc = at("da_sc", [P, SEQ], f32, A + 3)
        da_sc2 = at("da_sc2", [P, SEQ], f32, A + 32)
        da_lg = at("da_lg", [P, 2, SEQ], f32, A + 4)
        da_p = at("da_p", [P, 2, SEQ], f32, A + 6)
        da_pt = at("da_pt", [P, 2, SEQ], f32, A + 8)
        da_qk = at("da_qk", [P, 8, SEQ], f32, A + 12)
        da_v = at("da_v", [P, NB, BW], f32, A + 20)
        da_qi = at("da_qi", [P, 2, SEQ], f32, A + 24)
        da_ki = at("da_ki", [P, SEQ], f32, A + 26)
        da_t = at("da_t", [P, 4, SEQ], f32, A + 27)
        da_r = at("da_r", [P, 4, SEQ], f32, A + 27)
        da_o = at("da_o", [P, 4, P], f32, A + 30)
        da_wk = at("da_wk", [P, SEQ], f32, A + 31)

        m2_xdt = at("m2_xdt", [P, NB, BW], f32, A)
        m2_e = at("m2_e", [P, 2, 1280], f32, A + 4)
        m2_rs = at("m2_rs", [P, SEQ], f32, A + 9)
        m2_xc = at("m2_xc", [P, 6, SEQ], f32, A + 12)
        m2_z = at("m2_z", [P, 4, SEQ], f32, A + 18)
        m2_cb = at("m2_cb", [P, 2, 1280], f32, A + 22)
        m2_xr = at("m2_xr", [P, 6, SEQ + 3], f32, A + 27)
        m2_yv = at("m2_yv", [P, 4, SEQ], f32, A + 27)
        m2_t = at("m2_t", [P, 2, SEQ], f32, A + 31)

        hq = at("hq", [P, 4, SEQ], f32, A)
        hf = at("hf", [P, 4, SEQ], f32, A + 4)
        hken = at("hken", [P, NB, P], f32, A + 8)
        hlb = at("hlb", [P, 2, 4], f32, A + 9)
        hdec = at("hdec", [P, 2, NCH], f32, A + 9, 64)
        hv = at("hv", [P, NB, BW], f32, A + 12)
        hg = at("hg", [P, 4, SEQ], f32, A + 16)
        he = at("he", [P, 2, 4, SEQ], f32, A + 20)
        hatt = at("hatt", [P, NB, P], f32, A + 28)
        hS = at("hS", [P, NCH, P], f32, A + 29)

        x_nat = at("x_nat", [P, NB, DM], f32, ARENA_AT)
        pos_i = at("pos_i", [P, SEQ], i32, ARENA_AT + 16)
        ang = at("ang", [P, 4, SEQ], f32, ARENA_AT + 17)
        gam = at("gam", [P, DEPTH, 4], f32, ARENA_AT + 21)
        gtmp = at("gtmp", [P, 6, DEPTH, 4], f32, ARENA_AT + 22)
        o_nat = at("o_nat", [P, NB, DM], f32, ARENA_AT)

        bank = [nc.alloc_psum_tensor("bank%d" % i, [P, SEQ], f32) for i in range(8)]

        LAYER = """raw_in0 raw_in1 raw_in2 raw_in3 hi_done lo_done out_done free0 free1 free2 free3 sq_done sq_used
            sq_sums rstd_ready rstd_spread rms_ready normed_ready h_hi_done h_done g_hi_done g_done act_seq
            dve_seq par_in s5_in s5_k_ready s5_khi s5_pq_done m2_zs s5_pre s5_z s5_sim s5_sre s5_bb_ready
            s5_bbt_psum s5_bbt_ready s5_phase s5_trig s5_bu s5_bu_used s5_state s5_y s5_y_used gel_hi_done
            gel_done glu_y_done y_hi_done y_done small_psum small_done merge_used da_idx_done da_sq da_ms
            da_rms da_qn da_rot da_rot_done da_rel da_relu da_score da_logit da_max da_exp da_prob
            da_pt_psum da_pt_ready da_pv da_o_done m2_dtb m2_abs m2_dt_ready m2_acs m2_acs_done m2_ct
            m2_xdt_done m2_conv m2_silu m2_cbp m2_cb_done m2_acb m2_seg m2_decay m2_m m2_yp m2_y m2_sq m2_ms
            m2_rms m2_yn hg_e hg_fg hg_lf hg_cum hg_ec hg_ke hg_ket hg_ken hg_attp hg_att hg_upd hg_updu
            hg_op hg_ln hg_ex hg_o hg_sq hg_ms hg_rms hg_yn hg_lc hg_el layer_end""".split()
        sems = {}
        for name in LAYER:
            sems[name] = ctx.enter_context(nc.semaphore(name))
        for name in """go_sp go_act go_dve go_pe c_con c_rest c_freq c_x0 c_x1 c_x2 c_x3 c_pos c_gam p_x p_xt p_ang p_trig p_gam1 p_gam2 p_seq
                e_x e_o e_out""".split():
            sems[name] = ctx.enter_context(nc.semaphore(name))
        S = sems
        first, last = sems[LAYER[0]].num, sems["layer_end"].num
        assert last - first == len(LAYER) - 1
        raw_in = [S["raw_in%d" % i] for i in range(4)]
        free = [S["free%d" % i] for i in range(4)]

        block = ctx.enter_context(nc.Block())

        def wait_out(eng, t):
            eng.wait_ge(S["out_done"], t + 1)

        def wait_taken(eng, t):
            t0, it = t if isinstance(t, tuple) else (t, 0)
            if isinstance(t, tuple) or t >= 0:
                eng.wait_ge(free[t0 % 4], it + (t0 // 4 + 1))

        def end_of_layer(eng, go):
            eng.drain()
            eng.sem_inc(S["layer_end"], 1)
            eng.wait_ge(go, 1)
            eng.sem_clear(go)

        def split_hi(act, n0, it=0):
            if isinstance(it, int) and n0 >= NLOT:
                return
            s = n0 % 4
            act.wait_ge(raw_in[s], 16 * (it + n0 // 4 + 1))
            if n0 >= 4:
                act.wait_ge(S["out_done"], USED_AT[n0 - 4] + 4 * it)
            act.activation(w_hi[:, s], raw[:, s], AFT.Copy).then_inc(S["hi_done"], 1)

        def split_lo(eng, n0, it=0):
            if isinstance(it, int) and n0 >= NLOT:
                return
            s = n0 % 4
            eng.wait_ge(S["hi_done"], n0 + 1 + 4 * it)
            eng.tensor_tensor(w_lo[:, s], raw[:, s], w_hi[:, s].bitcast(f32), SUB).then_inc(S["lo_done"], 1)

        class Order:

            def __init__(self, eng, sem):
                self.eng, self.sem, self.n = eng, sem, 0

            def do(self, ins):
                self.n += 1
                ins.then_inc(self.sem, 1)
                return self.n

            def need(self, n):
                self.eng.wait_ge(self.sem, n)

        @block.tensor
        def _(pe):
            def gemm(n0, it, xh, xl, nk, k0=0, t0=None, ready=None):
                s, t0 = n0 % 4, OUT0[n0] if t0 is None else t0
                begin(n0, it, t0)
                for k in range(nk):
                    if ready is not None:
                        pe.wait_ge(S[ready[0]], ready[1] + k + 1)
                    m = passes(bank[t0 % 4], s, k0 + k, xh, xl, k, nk)
                m.then_inc(S["out_done"], 1)

            def begin(n0, it, t0):
                pe.wait_ge(S["lo_done"], it * 4 + (n0 + 1))
                if t0 >= 4:
                    pe.wait_ge(free[t0 % 4], it + t0 // 4)

            def passes(b, s, kw, xh, xl, k, nk):
                pe.matmul(b[:, :], w_hi[:, s, kw], xh[:, k], start=(k == 0), stop=False)
                pe.matmul(b[:, :], w_hi[:, s, kw], xl[:, k], start=False, stop=False)
                return pe.matmul(b[:, :], w_lo[:, s, kw], xh[:, k], start=False, stop=(k == nk - 1))

            def gemm_first(n0, it, ready):
                for n in (n0, n0 + 1):
                    begin(n, it, OUT0[n])
                for k in range(KT):
                    pe.wait_ge(S["h_done"], ready + k + 1)
                    for n in (n0, n0 + 1):
                        m = passes(bank[OUT0[n] % 4], n % 4, k, h_hi, h_lo, k, KT)
                        if k == KT - 1:
                            m.then_inc(S["out_done"], 1)

            def gemm_tokens(n0, cols, lots=1):
                s, w = n0 % 4, P * lots
                pe.wait_ge(S["lo_done"], n0 + lots)
                per = NB // lots
                for b in range(NB):
                    t = OUT0[n0] + b // per
                    if b % per == 0:
                        pe.wait_ge(free[t % 4], t // 4)
                    o = bank[t % 4][:, w * (b % per):w * (b % per) + (cols if lots == 1 else w)]
                    tok = slice(P * b, P * (b + 1))
                    wh, wl = (w_[:, s:s + lots, :, 0:cols] for w_ in (w_hi, w_lo))
                    for k in range(KT):
                        pe.matmul(o, h_hi[:, k, tok], wh[:, :, k], start=(k == 0), stop=False)
                        pe.matmul(o, h_lo[:, k, tok], wh[:, :, k], start=False, stop=False)
                        m = pe.matmul(o, h_hi[:, k, tok], wl[:, :, k], start=False, stop=(k == KT - 1))
                    if b % per == per - 1:
                        m.then_inc(S["out_done"], 1)

            def norm_sums(r):
                pe.wait_ge(S["sq_used"], KT * (r + 1))
                for b in range(NB):
                    m = pe.matmul(bank[7][:, b:b + 1], sq_sum[:, P * b:P * (b + 1)], ones[:, 0:1], start=True, stop=True)
                m.then_inc(S["sq_sums"], 1)
                pe.wait_ge(S["rstd_ready"], r + 1)
                for b in range(NB):
                    m = pe.matmul(bank[6][:, P * b:P * (b + 1)], rms[:, b:b + 1].broadcast_to([P, P]), ident,
                                  start=True, stop=True)
                m.then_inc(S["rstd_spread"], 1)

            def ffn(which, nb):
                norm_sums(2 * which)
                n, g0 = nb, FF_TILES * which
                for J in THIRDS:
                    with pe.Fori(0, J // 2) as it:
                        if n == nb:
                            gemm_first(n, it, KT * 3 * which)
                        for j in range(2 if n == nb else 0, 4):
                            gemm(n + j, it, h_hi, h_lo, KT)
                    n, g0 = n + 2 * J, g0 + J
                    with pe.Fori(0, 2) as it:
                        for j in range(4):
                            gemm(n + j, it, g_hi, g_lo, J, ready=("g_done", g0 - J) if j == 0 else None)
                    n += KT

            def gemm_h(n):
                for first, ready in ((MIX0, KT), (LOT_AT[("out", 0)], KT * 2)):
                    if n in (first, first + 1):
                        if n == first:
                            gemm_first(n, 0, ready)
                        return
                gemm(n, 0, h_hi, h_lo, KT)

            def lot(kind, i):
                gemm_h(LOT_AT[(kind, i)])

            def out(i):
                gemm_h(LOT_AT[("out", i)])

            def pair(kind, i):
                gemm_tokens(LOT_AT[(kind, i)], P, 2)

            def out_start(phase):
                pass

            def glu(i):
                n = LOT_AT[("glu", i)]
                for half in range(2):
                    gemm(n, 0, gel_hi, gel_lo, BT, k0=4 * half, t0=OUT0[n] + half,
                         ready=("gel_done", 0) if i == half == 0 else None)

            def turn_small():
                wait_taken(pe, out_at("small", 0))
                for b in range(NB):
                    m = pe.transpose(bank[7][:, 16 * b:16 * b + 12], small_t[0:12, P * b:P * (b + 1)],
                                     C("ident")[0:12, 0:12])
                m.then_inc(S["small_psum"], 1)

            def gate(g, i):
                gemm_h(LOT_AT[("gate%d" % g, i)])

            def branch(g, pair):
                n, ready = LOT_AT[("branch%d" % g, pair)], None
                if pair == 0:
                    ready = ("y_done", BT * TURN[g])
                    if g == 2:
                        pe.wait_ge(S["y_done"], BT * (TURN[g] + 1))
                for half in range(2):
                    gemm(n, 0, y_hi, y_lo, BT, k0=BT * half, t0=OUT0[n] + half, ready=None if half else ready)

            def s5_prep(phase):
                if phase == 0:
                    return
                pe.wait_ge(S["s5_bb_ready"], 2)
                for c in range(2):
                    for jt in range(4):
                        m = pe.transpose(bank[4 + c][:, P * jt:P * (jt + 1)],
                                         s5_bb[:, c].rearrange("p s i -> p (s i)")[:, P * jt:P * (jt + 1)], ident)
                    m.then_inc(S["s5_bbt_psum"], 1)
                pe.wait_ge(S["s5_bbt_ready"], 2)

            def s5_drive(st):
                q, jt = st % 4, st // 4
                wait_taken(pe, out_at("u", jt))
                if st:
                    pe.wait_ge(S["s5_bu_used"], st)
                for c in range(2):
                    m = pe.matmul(bank[4 + c][:, :], s5_bbt[32 * q:32 * q + 32, c, jt], s5_u[32 * q:32 * q + 32, jt],
                                  start=True, stop=True)
                m.then_inc(S["s5_bu"], 1)

            def s5_read(st):
                q, jt = st % 4, st // 4
                if q == 0 and jt:
                    pe.wait_ge(S["s5_y_used"], jt)
                for c, ready in enumerate(("s5_sre", "s5_sim")):
                    pe.wait_ge(S[ready], st + 1)
                    m = pe.matmul(bank[6][32 * q:32 * q + 32, :], s5_bc[:, 2 + c, st], s5_s[:, st % 2, c],
                                  start=(c == 0), stop=(c == 1))
                m.then_inc(S["s5_y"], 1)

            def s5(st):
                s5_drive(st)
                if st >= 2:
                    s5_read(st - 2)

            def s5_end():
                s5_read(S5_TILES - 2)
                s5_read(S5_TILES - 1)

            def da_norm(g, phase):
                if g == 0 and phase == 0:
                    pe.wait_ge(S["da_relu"], 12)
                for j in range(4 if phase == 0 else 0):
                    pe.wait_ge(S["da_sq"], 4 * g + j + 1)
                    pe.matmul(bank[4 + j][:, :], C("blk"), da_t[:, j], start=True, stop=True).then_inc(S["da_ms"], 1)
                for j in range(4 if phase == 1 else 0):
                    pe.wait_ge(S["da_qn"], 4 * g + j + 1)
                    pe.matmul(bank[4 + j][:, :], C("rot"), da_qk[:, 4 * g + j], start=True, stop=True) \
                      .then_inc(S["da_rot"], 1)

            def da_index(b):
                if b == 1:
                    pe.wait_ge(S["s5_y_used"], 4)
                    wait_taken(pe, out_at("ki", 0))
                else:
                    pe.wait_ge(S["da_relu"], 4 * (b - 1))
                for hh in range(4):
                    r = slice(64 * (hh % 2), 64 * (hh % 2) + 64)
                    m = pe.matmul(bank[4 + hh][:, 0:P * (b + 1)], da_qi[r, hh // 2, P * b:P * (b + 1)],
                                  da_ki[r, 0:P * (b + 1)], start=True, stop=True)
                m.then_inc(S["da_rel"], 1)

            def da_topk(b, phase):
                pass

            def logits(u):
                hp, b, e = UNITS[u]
                r = slice(64 * e, 64 * e + 64)
                if u >= 2:
                    pe.wait_ge(S["da_max"], u - 1)
                pe.matmul(bank[4 + u % 2][:, 0:P * (b + 1)], da_qk[r, hp, P * b:P * (b + 1)],
                          da_qk[r, 4 + hp, 0:P * (b + 1)], start=True, stop=True).then_inc(S["da_logit"], 1)

            def turn(u):
                hp, b, e = UNITS[u]
                pe.wait_ge(S["da_prob"], u + 1)
                if u:
                    pe.wait_ge(S["da_pt_ready"], u)
                for j in range(b + 1):
                    m = pe.transpose(bank[6][:, P * j:P * (j + 1)], da_p[:, u % 2, P * j:P * (j + 1)], ident)
                m.then_inc(S["da_pt_psum"], 1)

            def values(u):
                hp, b, e = UNITS[u]
                h = 2 * hp + e
                pe.wait_ge(S["da_pt_ready"], u + 1)
                if u % 8 == 0 and b:
                    if b == 1:
                        pe.wait_ge(S["da_o_done"], 1)
                    else:
                        pe.wait_ge(S["y_done"], BT * TURN[2] + b)
                for j in range(b + 1):
                    m = pe.matmul(bank[7][64 * e:64 * e + 64, P * hp:P * (hp + 1)], da_v[:, j, 64 * h:64 * h + 64],
                                  da_pt[:, u % 2, P * j:P * (j + 1)], start=(j == 0), stop=(j == b))
                m.then_inc(S["da_pv"], 1)
            def att_start():
                pe.wait_ge(S["da_rot_done"], 8)
                logits(0)
                logits(1)

            def att(u):
                turn(u)
                if u + 2 < 32:
                    logits(u + 2)
                if u:
                    values(u - 1)

            def att_end():
                values(31)

            def m2_decay():
                pass

            def m2_conv():
                pass

            def m2_prep(phase):
                if phase == 0:
                    pe.wait_ge(S["m2_dt_ready"], 1)
                    for b in range(NB):
                        for j in range(b + 1):
                            m = pe.matmul(bank[4][:, 8 * b:8 * b + 8], C("upper", 0, P) if j == b else ones,
                                          m2_dt[:, 1, j], start=(j == 0), stop=(j == b))
                    m.then_inc(S["m2_acs"], 1)
                    pe.wait_ge(S["m2_silu"], 4)
                if phase in (1, 2):
                    for b in range(2 * phase - 2, 2 * phase):
                        if b >= 2:
                            pe.wait_ge(S["m2_xdt_done"], b - 1)
                        for i in range(4):
                            m = pe.transpose(bank[5 + b % 2][:, P * i:P * (i + 1)], m2_xc[:, i, P * b:P * (b + 1)],
                                             ident)
                        m.then_inc(S["m2_ct"], 1)
                if phase < 3:
                    return
                pe.wait_ge(S["m2_silu"], 6)
                pe.wait_ge(S["m2_acs_done"], 1)
                for c in range(4 * (phase - 3), 4 * (phase - 2)):
                    g, j = c // 4, c % 4
                    r = slice(64 * g, 64 * g + 64)
                    if c >= 2:
                        pe.wait_ge(S["m2_cb_done"], c - 1)
                    pe.matmul(bank[4 + 3 * (c % 2)][:, 0:SEQ - P * j], m2_xc[r, 4, P * j:P * (j + 1)],
                              m2_xc[r, 5, P * j:SEQ], start=True, stop=True).then_inc(S["m2_cbp"], 1)
                if phase == 4:
                    pe.wait_ge(S["m2_xdt_done"], 4)

            def decays(h):
                if h >= 2:
                    pe.wait_ge(S["m2_seg"], h - 1)
                for j in range(NB):
                    m = pe.matmul(bank[4 + h % 2][:, P * j:SEQ], m2_dt[:, 1, j, h:h + 1].broadcast_to([P, P]),
                                  C("upper", 0, SEQ - P * j), start=(j == 0), stop=(j == NB - 1))
                m.then_inc(S["m2_acb"], 1)

            def outs(h):
                pe.wait_ge(S["m2_m"], h + 1)
                if h % 2 == 0 and h >= 4:
                    pe.wait_ge(S["m2_y"], h // 2 - 1)
                e = 64 * (h % 2)
                for j in range(NB):
                    m = pe.matmul(bank[6 + h // 2 % 2][e:e + 64, P * j:SEQ], m2_xdt[:, j, 64 * h:64 * h + 64],
                                  m2_e[:, h % 2, M2_OFF[j]:M2_OFF[j] + SEQ - P * j], start=(j == 0), stop=(j == NB - 1))
                m.then_inc(S["m2_yp"], 1)
            def m2_head(h):
                if h == 0:
                    pe.wait_ge(S["m2_cb_done"], 8)
                    decays(0)
                if h < 7:
                    decays(h + 1)
                outs(h)

            def m2_norm():
                for i in range(BT):
                    pe.wait_ge(S["m2_sq"], i + 1)
                    pe.matmul(bank[4][:, :], ones, m2_t[:, i % 2], start=(i == 0), stop=(i == BT - 1)) \
                      .then_inc(S["m2_ms"], 1)

            def m2_end():
                pass

            def hg_start():
                pass

            def hg_gates(h, phase):
                pass

            def hg_head(h, phase):
                (hg_products, hg_updates, hg_outputs)[phase](h)

            def hg_products(h):
                scr = he[:, h % 2]
                pe.wait_ge(S["hg_ke"], 3 * h + 2)
                for j in range(NB):
                    t = slice(P * j, P * (j + 1))
                    m = pe.matmul(bank[4][:, t], scr[:, 2, t], hq[:, h, t], start=True, stop=True)
                m.then_inc(S["hg_attp"], 1)
                pe.wait_ge(S["hg_ke"], 3 * h + 3)
                if h:
                    pe.wait_ge(S["hg_o"], h)
                for j in range(NB):
                    t = slice(P * j, P * (j + 1))
                    m = pe.transpose(bank[5][:, t], scr[:, 3, t], ident)
                m.then_inc(S["hg_ket"], 1)

            def hg_updates(h):
                v = slice(P * h, P * (h + 1))
                if h:
                    pe.wait_ge(S["hg_ln"], h)
                pe.wait_ge(S["hg_ken"], h + 1)
                pe.wait_ge(S["hg_att"], h + 1)
                for j in range(NB):
                    for q in range(4 if j < NB - 1 else 3):
                        r = slice(32 * q, 32 * q + 32)
                        m = pe.matmul(bank[4 + q][:, P * j:P * (j + 1)], hken[r, j], hv[r, j, v], start=True, stop=True)
                m.then_inc(S["hg_upd"], 1)

            def hg_outputs(h):
                v = slice(P * h, P * (h + 1))
                pe.wait_ge(S["hg_updu"], h + 1)
                for j in range(NB):
                    t = slice(P * j, P * (j + 1))
                    m = pe.matmul(bank[5][:, t], hv[:, j, v], hatt[:, j], start=True, stop=False)
                    for c in range(4 * j, 4 * j + 4):
                        if c:
                            tc = slice(HG_CHUNK * c, HG_CHUNK * (c + 1))
                            m = pe.matmul(bank[5][:, tc], hS[:, c], hq[:, h, tc], start=False, stop=(c % 4 == 3))
                m.then_inc(S["hg_op"], 1)

            def hg_norm(h):
                pe.wait_ge(S["hg_sq"], h + 1)
                pe.matmul(bank[7][:, :], ones, he[:, h % 2, 1], start=True, stop=True).then_inc(S["hg_ms"], 1)

            def hg_end():
                pass

            STEPS = dict(lot=lot, pair=pair, turn_small=turn_small, out=out, out_start=out_start, glu=glu, gate=gate, branch=branch,
                         s5_prep=s5_prep, s5=s5,
                         s5_end=s5_end, da_norm=da_norm, da_index=da_index, da_topk=da_topk, att_start=att_start,
                         att=att, att_end=att_end, m2_decay=m2_decay, m2_conv=m2_conv, m2_prep=m2_prep, m2_head=m2_head,
                         m2_norm=m2_norm, m2_end=m2_end, hg_start=hg_start, hg_gates=hg_gates, hg_head=hg_head,
                         hg_norm=hg_norm, hg_end=hg_end)

            def mixing():
                for step in SCRIPT:
                    STEPS[step[0]](*step[1:])

            pe.wait_ge(S["c_con"], 16)
            for b in range(NB):
                pe.wait_ge(S["c_x%d" % b], 16)
                for i in range(KT):
                    m = pe.transpose(bank[i][:, P * b:P * (b + 1)], x_nat[:, b, P * i:P * (i + 1)], ident)
                    if b == NB - 1:
                        m.then_inc(S["p_x"], 1)
            pe.wait_ge(S["p_xt"], KT)
            with pe.Fori(0, DEPTH) as layer:
                ffn(0, 0)
                norm_sums(1)
                pe.wait_ge(S["c_rest"], 16)
                mixing()
                ffn(1, FFN2_0)
                end_of_layer(pe, S["go_pe"])
            for b in range(NB):
                for i in range(KT):
                    m = pe.transpose(bank[2 * b + i // 4][:, P * (i % 4):P * (i % 4 + 1)],
                                     x[:, i, P * b:P * (b + 1)], ident)
                    if i % 4 == 3:
                        m.then_inc(S["e_x"], 1)

        @block.sync
        def _(sp):
            first_cols, freq = CON_AT["blk"], CON_AT["invfreq"]
            sp.dma_start(pos_i[:, :], positions.partition_broadcast(P)).then_inc(S["c_pos"], 16)
            sp.dma_start(con[:, freq:NCON], con_in[:, freq:NCON]).then_inc(S["c_freq"], 16)
            sp.dma_start(gam[:, :, :], gamma_in).then_inc(S["c_gam"], 16)
            sp.dma_start(con[:, 0:first_cols], con_in[:, 0:first_cols]).then_inc(S["c_con"], 16)
            for b in range(NB):
                sp.dma_start(x_nat[:, b], x_in[P * b:P * (b + 1), :]).then_inc(S["c_x%d" % b], 16)
            sp.dma_start(con[:, first_cols:freq], con_in[:, first_cols:freq]).then_inc(S["c_rest"], 16)
            with sp.Fori(0, DEPTH) as layer:
                sp.dma_start(par[:, :], par_in[layer]).then_inc(S["par_in"], 16)
                for n in range(4):
                    sp.dma_start(raw[:, n].rearrange("p k m -> p (k m)"), w_lots[layer * NLOT + n]) \
                      .then_inc(raw_in[n], 16)
                sp.wait_ge(S["p_xt"], KT)
                sp.wait_ge(S["p_gam2"], 1)
                sp.wait_ge(S["p_trig"], 3)
                sp.dma_start(s5_bc[:, :, :, :].rearrange("p a b c -> p (a b c)"), s5_in[layer]) \
                  .then_inc(S["s5_in"], 16)
                with sp.Fori(1, NLOT // 4) as it:
                    for s in range(4):
                        sp.wait_ge(S["lo_done"], it * 4 + (s - 3))
                        sp.dma_start(raw[:, s].rearrange("p k m -> p (k m)"),
                                     w_lots[layer * NLOT + it * 4 + s]).then_inc(raw_in[s], 16)
                for n in range(NLOT // 4 * 4, NLOT):
                    sp.wait_ge(S["lo_done"], n - 3)
                    sp.dma_start(raw[:, n % 4].rearrange("p k m -> p (k m)"), w_lots[layer * NLOT + n]) \
                      .then_inc(raw_in[n % 4], 16)
                end_of_layer(sp, S["go_sp"])
            sp.wait_ge(S["c_rest"], 16)
            for b in range(NB):
                sp.wait_ge(S["e_o"], 2 * (b + 1))
                sp.dma_start(out[P * b:P * (b + 1), :], o_nat[:, b]).then_inc(S["e_out"], 16)
            sp.wait_ge(S["e_out"], 16 * NB)

        @block.gpsimd
        def _(pool):
            def after(kind, i):
                split_lo(pool, LOT_AT[(kind, i)] + 4)

            def s5_im(st):
                e = st % 2
                cs, sn, v = s5_cos[:, e], s5_sin[:, e], s5_v[e]
                pool.wait_ge(S["s5_z"], 2 * st + 2)
                if st:
                    pool.wait_ge(S["s5_sim"], st)
                pool.tensor_tensor(s5_pq[:, 0], v[:, 0], sn, MUL).then_inc(S["s5_pq_done"], 1)
                pool.tensor_tensor(s5_pq[:, 1], v[:, 1], cs, MUL).then_inc(S["s5_pq_done"], 1)
                pool.wait_ge(S["s5_pq_done"], 2 * (st + 1))
                if st >= 2:
                    pool.wait_ge(S["s5_y"], st - 1)
                pool.tensor_tensor(s5_s[:, e, 1], s5_pq[:, 0], s5_pq[:, 1], ADD).then_inc(S["s5_sim"], 1)
                pool.wait_ge(S["s5_state"], st + 1)
                pool.tensor_tensor(s5_s[:, e, 0], s5_s[:, e, 0], s5_vs[:, :], SUB).then_inc(S["s5_sre"], 1)

            def mixing():
                pool.wait_ge(S["lo_done"], MIX0 + 4)
                for step in SCRIPT:
                    if step[0] == "lot":
                        after(*step[1:])
                    elif step[0] == "pair":
                        after(step[1], step[2])
                        after(step[1], step[2] + 1)
                    elif step[0] in ("glu", "out"):
                        after(*step)
                    elif step[0] in ("gate", "branch"):
                        after(step[0] + str(step[1]), step[2])
                    elif step[0] == "s5":
                        s5_im(step[1])

            with pool.Fori(0, DEPTH) as layer:
                mixing()
                pool.wait_ge(S["layer_end"], 4)
                pool.sem_clear(range(first, last + 1))
                for go in ("go_sp", "go_act", "go_dve", "go_pe"):
                    pool.sem_inc(S[go], 1)

        @block.scalar
        def _(act):
            seq = Order(act, S["act_seq"])

            def chain(ins):
                seq.need(seq.do(ins))

            def square(r, i, t=None):
                if t is not None:
                    wait_taken(act, t)
                if KT * r + i >= 2:
                    act.wait_ge(S["sq_used"], KT * r + i - 1)
                act.activation(sq[:, i % 2], x[:, i], AFT.Square).then_inc(S["sq_done"], 1)
                if i == KT - 2:
                    act.activation(warm, epsc, AFT.Sqrt)

            def norm(r):
                if r == 0:
                    split_hi(act, 0)
                    split_hi(act, 1)
                act.wait_ge(S["sq_sums"], r + 1)
                act.activation(rms[:, 0:NB], bank[7][:, 0:NB], AFT.Sqrt, scale=1.0 / DM, bias=epsc[:, :]) \
                   .then_inc(S["rms_ready"], 1)
                for i in range(KT):
                    act.wait_ge(S["normed_ready"], KT * r + i + 1)
                    act.activation(h_hi[:, i], normed[:, i % 2], AFT.Copy).then_inc(S["h_hi_done"], 1)

            def ffn(which, nb):
                n, g0 = nb, FF_TILES * which
                for th, J in enumerate(THIRDS):
                    with act.Fori(0, J // 2) as it:
                        for q in range(2):
                            na, nbb = n + 2 * q, n + 2 * q + 1
                            ta, tb = OUT0[na], OUT0[nbb]
                            act.wait_ge(S["out_done"], it * 4 + (ta + 1))
                            if tb >= 4:
                                act.wait_ge(free[tb % 4], it + tb // 4)
                            act.activation(silu_a[:, q], bank[ta % 4][:, :], AFT.Silu).then_inc(free[ta % 4], 1)
                            split_hi(act, na + 4, it)
                            split_hi(act, nbb + 4, it)
                            act.wait_ge(free[tb % 4], it + (tb // 4 + 1))
                            act.activation(g_hi[:, it * 2 + q], gated[:, q], AFT.Copy).then_inc(S["g_hi_done"], 1)
                    n += 2 * J
                    if th == len(THIRDS) - 1:
                        for j in range(KT):
                            split_hi(act, n + j + 4)
                            if which == 0 and j >= 1:
                                square(1, j - 1, (OUT0[n + j - 1], 0))
                    else:
                        with act.Fori(0, 2) as it:
                            for j in range(4):
                                split_hi(act, n + j + 4, it)
                    n += KT

            def evac(dst, n, func=AFT.Copy, **kw):
                t = OUT0[n]
                wait_out(act, t)
                src = bank[t % 4][:, :]
                act.activation(dst, src, func, **kw).then_inc(free[t % 4], 1)
                split_hi(act, n + 4)

            def split_y(g, i, src, scale=1.0):
                if TURN[g]:
                    wait_out(act, out_at("branch%d" % ORDER[TURN[g] - 1], KT // 2 - 1, 1))
                act.activation(y_hi[:, i], src, AFT.Copy, scale=scale).then_inc(S["y_hi_done"], 1)

            def pair(kind, i):
                n, dst = LOT_AT[(kind, i)], da_v if kind == "v" else hv
                for half in range(2):
                    t = OUT0[n] + half
                    wait_out(act, t)
                    src = bank[t % 4][:, :].rearrange("p (b m) -> p b m", b=2)
                    act.activation(dst[:, 2 * half:2 * half + 2, P * i:P * (i + 2)], src, AFT.Copy) \
                       .then_inc(free[t % 4], 1)
                split_hi(act, n + 4)
                split_hi(act, n + 5)

            def lot(kind, i):
                n = LOT_AT[(kind, i)]
                if kind == "u":
                    evac(s5_u[:, i], n)
                elif kind == "small":
                    t = OUT0[n]
                    wait_out(act, t)
                    act.activation(small_t[0:12, :], bank[t % 4][0:12, :], AFT.Copy).then_inc(free[t % 4], 1)
                    split_hi(act, n + 4)
                elif kind in ("q", "k"):
                    evac(da_qk[:, 4 * "qk".index(kind) + i], n)
                elif kind == "qi":
                    evac(da_qi[:, i], n)
                elif kind == "ki":
                    evac(da_ki[:, :], n)
                elif kind == "xbc":
                    if i == 0:
                        act.wait_ge(S["da_idx_done"], 1)
                    evac(m2_xr[:, i, 3:3 + SEQ], n)
                elif kind == "z":
                    evac(m2_z[:, i], n)
                elif kind == "hf":
                    if i == 0:
                        act.wait_ge(S["m2_yp"], 8)
                        act.wait_ge(S["m2_m"], 8)
                    evac(hf[:, i], n)
                elif kind == "hq":
                    evac(hq[:, i], n)
                elif kind == "hg":
                    evac(hg[:, i], n, AFT.Tanh, scale=0.5)

            def out(i):
                split_hi(act, LOT_AT[("out", i)] + 4)
                if i:
                    square(2, i - 1, (out_at("out", i - 1), 0))

            def out_start(phase):
                wait_out(act, out_at("gate3", KT - 1))
                for i in (range(KT - 2), range(KT - 2, KT))[phase]:
                    act.wait_ge(S["merge_used"], KT * (len(ORDER) - 1) + i + 1)
                    act.activation(h_hi[:, i], merged[:, i], AFT.Copy).then_inc(S["h_hi_done"], 1)

            def turn_small():
                act.wait_ge(S["small_psum"], 1)
                src = bank[7][:, 0:64].rearrange("p (b m) -> p b m", m=16)[:, :, 0:12]
                act.activation(small[:, :, :], src, AFT.Copy).then_inc(S["small_done"], 1)

            def gate(g, i):
                n = LOT_AT[("gate%d" % g, i)]
                t, done = OUT0[n], KT * TURN[g] + i
                wait_out(act, t)
                if done >= 2:
                    act.wait_ge(S["merge_used"], done - 1)
                act.activation(gate_th[:, i % 2], bank[t % 4][:, :], AFT.Tanh, scale=0.5).then_inc(free[t % 4], 1)
                split_hi(act, n + 4)

            def branch(g, pair):
                split_hi(act, LOT_AT[("branch%d" % g, pair)] + 4)

            K = lambda i: s5_k[:, i]

            def s5_pre(st):
                e, k1 = st % 2, slice(st, st + 1)
                if st >= 2:
                    act.wait_ge(S["s5_trig"], 2 * (st - 1))
                act.activation(s5_ph[:, 2 * e], C("tvec"), AFT.Copy, scale=K(9)[:, k1]).then_inc(S["s5_pre"], 1)
                act.activation(s5_ph[:, 2 * e + 1], C("tvec"), AFT.Identity, scale=K(5)[:, k1], bias=roundc[:, :]) \
                   .then_inc(S["s5_pre"], 1)

            def s5_trig(st):
                e = st % 2
                act.wait_ge(S["s5_phase"], st + 1)
                if st >= 2:
                    act.wait_ge(S["s5_state"], st - 1)
                    act.wait_ge(S["s5_sim"], st - 1)
                chain(act.activation(s5_ph[:, 2 * e + 1], s5_ph[:, 2 * e], AFT.Abs))
                act.activation(s5_sin[:, e], s5_ph[:, 2 * e], AFT.Sin, scale=2 * PI).then_inc(S["s5_trig"], 1)
                act.activation(s5_cos[:, e], s5_ph[:, 2 * e + 1], AFT.Sin, scale=-2 * PI, bias=half_pi[:, :]) \
                   .then_inc(S["s5_trig"], 1)

            def s5_prep(phase):
                if phase == 1:
                    for c in range(2):
                        act.wait_ge(S["s5_bbt_psum"], c + 1)
                        act.activation(s5_bbt[:, c].rearrange("p a b -> p (a b)"), bank[4 + c][:, :], AFT.Copy) \
                           .then_inc(S["s5_bbt_ready"], 1)
                    s5_trig(0)
                    return
                act.wait_ge(S["par_in"], 16)
                act.wait_ge(S["h_done"], 2 * KT)
                act.wait_ge(S["h_hi_done"], 2 * KT)
                act.activation(K(0), PR("log_dt"), AFT.Exp).then_inc(S["s5_k_ready"], 1)
                act.wait_ge(S["s5_k_ready"], 2)
                act.activation(K(3), K(1), AFT.Exp).then_inc(S["s5_k_ready"], 1)
                act.wait_ge(S["s5_k_ready"], 4)
                act.activation(K(7), K(5), AFT.Sin, scale=2 * PI).then_inc(S["s5_k_ready"], 1)
                act.activation(K(8), K(6), AFT.Sin, scale=-2 * PI, bias=half_pi[:, :]).then_inc(S["s5_k_ready"], 1)
                act.wait_ge(S["s5_khi"], 1)
                s5_pre(0)
                s5_pre(1)

            def s5(st):
                if st + 2 < S5_TILES:
                    s5_pre(st + 2)
                if st + 1 < S5_TILES:
                    s5_trig(st + 1)

            def s5_end():
                act.wait_ge(S["s5_y_used"], 4)
                for i in range(4):
                    if i >= 2:
                        act.wait_ge(S["gel_done"], i - 1)
                    chain(act.activation(gel[:, i % 2], s5_u[:, i], AFT.Gelu_apprx_tanh))
                    act.activation(gel_hi[:, i], gel[:, i % 2], AFT.Copy).then_inc(S["gel_hi_done"], 1)

            def glu(i):
                n = LOT_AT[("glu", i)]
                t = OUT0[n] + 1
                wait_out(act, t)
                if i >= 2:
                    act.wait_ge(S["glu_y_done"], i - 1)
                act.activation(glu_th[:, i % 2], bank[t % 4][:, :], AFT.Tanh, scale=0.5).then_inc(free[t % 4], 1)
                split_hi(act, n + 4)
                act.wait_ge(S["glu_y_done"], i + 1)
                split_y(1, i, glu_y[:, i % 2], scale=0.5)

            def da_norm(g, phase):
                if phase:
                    return
                if g:
                    act.wait_ge(S["da_rot_done"], 4)
                else:
                    act.wait_ge(S["da_score"], 3)
                wait_taken(act, out_at("qk"[g], 3))
                for j in range(4):
                    act.activation(da_t[:, j], da_qk[:, 4 * g + j], AFT.Square).then_inc(S["da_sq"], 1)
                for j in range(4):
                    act.wait_ge(S["da_ms"], 4 * g + j + 1)
                    n = seq.do(act.activation(da_t[:, j], bank[4 + j][:, :], AFT.Ln, scale=1.0 / 64, bias=epsc[:, :]))
                for j in range(4):
                    seq.need(n - 3 + j)
                    act.activation(da_t[:, j], da_t[:, j], AFT.Exp, scale=-0.5).then_inc(S["da_rms"], 1)

            def da_index(b):
                act.wait_ge(S["da_rel"], b)
                if b > 1:
                    act.wait_ge(S["da_score"], b - 1)
                for hh in range(4):
                    act.activation(da_r[:, hh, 0:P * (b + 1)], bank[4 + hh][:, 0:P * (b + 1)], AFT.Relu) \
                       .then_inc(S["da_relu"], 1)

            def da_topk(b, phase):
                pass

            def exps(u):
                hp, b, e = UNITS[u]
                w = P * (b + 1)
                act.wait_ge(S["da_max"], u + 1)
                if u >= 2:
                    act.wait_ge(S["da_pt_psum"], u - 1)
                act.activation(da_p[:, u % 2, 0:w], da_lg[:, u % 2, 0:w], AFT.Exp, scale=0.125,
                               bias=da_st[:, u, 1:2], accum_out=da_st[:, u, 2:3]).then_inc(S["da_exp"], 1)

            def copy(u):
                hp, b, e = UNITS[u]
                w = P * (b + 1)
                act.wait_ge(S["da_pt_psum"], u + 1)
                if u >= 2:
                    act.wait_ge(S["da_pv"], u - 1)
                act.activation(da_pt[:, u % 2, 0:w], bank[6][:, 0:w], AFT.Copy).then_inc(S["da_pt_ready"], 1)
            def high_att(b, src=bank[7][:, :].rearrange("p (h t) -> p h t", t=P)):
                wait_out(act, out_at("branch%d" % ORDER[TURN[2] - 1], KT // 2 - 1, 1))
                act.activation(y_hi[:, :, P * b:P * (b + 1)], src, AFT.Copy).then_inc(S["y_hi_done"], 1)

            def att_start():
                exps(0)

            def att(u):
                if u < 31:
                    exps(u + 1)
                copy(u)
                if u % 8 == 0 and u:
                    act.wait_ge(S["da_pv"], u)
                    if u == 8:
                        act.wait_ge(S["da_rot_done"], 8)
                        act.activation(da_o[:, :, :].rearrange("p h t -> p (h t)"), bank[7][:, :], AFT.Copy) \
                           .then_inc(S["da_o_done"], 1)
                    elif u == 16:
                        high_att(0, da_o[:, :, :])
                        high_att(1)
                    else:
                        high_att(u // 8 - 1)

            def att_end():
                act.wait_ge(S["da_pv"], 32)
                high_att(3)

            def m2_decay():
                act.wait_ge(S["m2_dtb"], 2)
                act.activation(m2_ea[:, :], PR("a_log"), AFT.Exp).then_inc(S["m2_abs"], 1)
                chain(act.activation(m2_dt[:, 1], m2_dt[:, 1], AFT.Exp, scale=-1.0))
                act.activation(m2_dt[:, 1], m2_dt[:, 1], AFT.Ln, bias=1.0).then_inc(S["m2_abs"], 1)

            def m2_conv():
                for i in range(4):
                    wait_taken(act, out_at("z", i))
                    act.activation(m2_z[:, i], m2_z[:, i], AFT.Silu).then_inc(S["m2_zs"], 1)
                for i in range(6):
                    act.wait_ge(S["m2_conv"], i + 1)
                    act.activation(m2_xc[:, i], m2_xc[:, i], AFT.Silu).then_inc(S["m2_silu"], 1)

            def m2_prep(phase):
                pass

            def m2_head(h):
                for k in ((0, 1) if h == 0 else (h + 1,) if h < 7 else ()):
                    act.wait_ge(S["m2_seg"], k + 1)
                    act.activation(m2_e[:, k % 2], m2_e[:, k % 2], AFT.Exp).then_inc(S["m2_decay"], 1)

            def m2_norm():
                for i in range(BT):
                    act.wait_ge(S["m2_yn"], i + 1)
                    if i >= 2:
                        act.wait_ge(S["m2_ms"], i - 1)
                    act.activation(m2_t[:, i % 2], m2_yv[:, i], AFT.Square).then_inc(S["m2_sq"], 1)
                act.wait_ge(S["m2_ms"], 4)
                chain(act.activation(m2_rs[:, :], bank[4][:, :], AFT.Ln, scale=1.0 / BW, bias=epsc[:, :]))
                act.activation(m2_rs[:, :], m2_rs[:, :], AFT.Exp, scale=-0.5).then_inc(S["m2_rms"], 1)

            def m2_end():
                for i in range(BT):
                    act.wait_ge(S["m2_yn"], BT + i + 1)
                    split_y(0, i, m2_yv[:, i])

            def hg_start():
                for i in range(4):
                    wait_taken(act, out_at("hq", i))
                    act.activation(hq[:, i], hq[:, i], AFT.Silu).then_inc(S["hg_ex"], 1)

            def hg_gates(h, phase):
                X = [he[:, h % 2, i] for i in range(4)]
                if phase == 0:
                    if h >= 2:
                        act.wait_ge(S["hg_op"], h - 1)
                    wait_taken(act, out_at("hf", h))
                    chain(act.activation(X[0], hf[:, h], AFT.Exp, scale=-1.0))
                    act.activation(hf[:, h], hf[:, h], AFT.Exp).then_inc(S["hg_e"], 1)
                elif phase == 1:
                    act.wait_ge(S["hg_fg"], h + 1)
                    act.activation(X[0], X[0], AFT.Ln).then_inc(S["hg_lf"], 1)
                else:
                    act.wait_ge(S["hg_cum"], h + 1)
                    act.activation(X[0], X[1], AFT.Exp).then_inc(S["hg_ec"], 1)
                    act.activation(X[2], X[1], AFT.Exp, scale=-1.0).then_inc(S["hg_ec"], 1)
                    act.activation(hdec[:, h % 2], X[1][:, HG_CHUNK - 1::HG_CHUNK], AFT.Exp).then_inc(S["hg_ec"], 1)
                    act.wait_ge(S["hg_lc"], h + 1)
                    act.activation(X[3], X[3], AFT.Exp).then_inc(S["hg_el"], 1)

            def hg_head(h, phase):
                if phase == 0:
                    act.wait_ge(S["hg_ket"], h + 1)
                    act.activation(hken[:, :, :].rearrange("p a b -> p (a b)"), bank[5][:, :], AFT.Copy) \
                       .then_inc(S["hg_ken"], 1)
                elif phase == 2:
                    act.wait_ge(S["hg_op"], h + 1)
                    act.activation(hf[:, h], bank[5][:, :], AFT.Copy).then_inc(S["hg_o"], 1)
                    act.wait_ge(S["hg_o"], h + 1)
                    act.activation(he[:, h % 2, 1], hf[:, h], AFT.Square).then_inc(S["hg_sq"], 1)

            def hg_norm(h):
                X1 = he[:, h % 2, 1]
                act.wait_ge(S["hg_ms"], h + 1)
                act.activation(X1, bank[7][:, :], AFT.Ln, scale=1.0 / P, bias=epsc[:, :]).then_inc(S["hg_ln"], 1)
                act.wait_ge(S["hg_ln"], h + 1)
                act.activation(X1, X1, AFT.Exp, scale=-0.5).then_inc(S["hg_rms"], 1)

            def hg_end():
                for h in range(4):
                    act.wait_ge(S["hg_yn"], h + 1)
                    split_y(3, h, hf[:, h], scale=0.5)

            STEPS = dict(lot=lot, pair=pair, turn_small=turn_small, out=out, out_start=out_start, glu=glu, gate=gate, branch=branch,
                         s5_prep=s5_prep, s5=s5,
                         s5_end=s5_end, da_norm=da_norm, da_index=da_index, da_topk=da_topk, att_start=att_start,
                         att=att, att_end=att_end, m2_decay=m2_decay, m2_conv=m2_conv, m2_prep=m2_prep, m2_head=m2_head,
                         m2_norm=m2_norm, m2_end=m2_end, hg_start=hg_start, hg_gates=hg_gates, hg_head=hg_head,
                         hg_norm=hg_norm, hg_end=hg_end)

            def mixing():
                for step in SCRIPT:
                    STEPS[step[0]](*step[1:])

            act.wait_ge(S["p_ang"], 2)
            act.activation(rope_sin[:, :], ang[:, 0], AFT.Sin).then_inc(S["p_trig"], 1)
            act.activation(rope_cos[:, :], ang[:, 1], AFT.Sin, scale=-1.0, bias=half_pi[:, :]).then_inc(S["p_trig"], 1)
            act.wait_ge(S["p_gam1"], 1)
            act.activation(gtmp[:, 1], gtmp[:, 0], AFT.Exp).then_inc(S["p_trig"], 1)
            for i in range(KT):
                act.wait_ge(S["p_x"], i + 1)
                act.activation(x[:, i], bank[i][:, :], AFT.Copy).then_inc(S["p_xt"], 1)
            act.wait_ge(S["p_xt"], KT)
            with act.Fori(0, DEPTH) as layer:
                seq.n = 0
                for i in range(KT):
                    square(0, i)
                norm(0)
                split_hi(act, 2)
                split_hi(act, 3)
                ffn(0, 0)
                square(1, KT - 1, (OUT0[FFN_LOTS - 1], 0))
                norm(1)
                act.wait_ge(S["c_rest"], 16)
                mixing()
                square(2, KT - 1, (out_at("out", KT - 1), 0))
                norm(2)
                ffn(1, FFN2_0)
                end_of_layer(act, S["go_act"])
            for b in range(NB):
                for half in range(2):
                    act.wait_ge(S["e_x"], 2 * b + half + 1)
                    act.activation(o_nat[:, b, BW * half:BW * (half + 1)], bank[2 * b + half][:, :], AFT.Copy) \
                       .then_inc(S["e_o"], 1)

        @block.vector
        def _(dve):
            seq = Order(dve, S["dve_seq"])
            do, need = seq.do, seq.need

            def chain(ins):
                need(do(ins))
            V = dve

            def add_square(r, i):
                V.wait_ge(S["sq_done"], KT * r + i + 1)
                if i == 0:
                    if r:
                        V.wait_ge(S["sq_sums"], r)
                    V.tensor_copy(sq_sum[:, :], sq[:, 0]).then_inc(S["sq_used"], 1)
                else:
                    V.wait_ge(S["sq_used"], KT * r + i)
                    V.tensor_tensor(sq_sum[:, :], sq_sum[:, :], sq[:, i % 2], ADD).then_inc(S["sq_used"], 1)

            def square_sums(r):
                for i in range(KT):
                    add_square(r, i)

            def norm(r, gain):
                V.wait_ge(S["rms_ready"], r + 1)
                V.reciprocal(rms[:, 0:NB], rms[:, 0:NB]).then_inc(S["rstd_ready"], 1)
                V.wait_ge(S["rstd_spread"], r + 1)
                h0 = KT * (3 * r // 2)
                if r == 0:
                    V.wait_ge(S["par_in"], 16)

                def low(i):
                    V.wait_ge(S["h_hi_done"], h0 + i + 1)
                    V.tensor_tensor(h_lo[:, i], normed[:, i % 2], h_hi[:, i].bitcast(f32), SUB) \
                     .then_inc(S["h_done"], 1)
                for i in range(KT):
                    if i >= 2:
                        V.wait_ge(S["h_done"], h0 + i - 1)
                    V.scalar_tensor_tensor(normed[:, i % 2], x[:, i], PC(gain, i), bank[6][:, :], MUL, MUL) \
                     .then_inc(S["normed_ready"], 1)
                    if i:
                        low(i - 1)
                low(KT - 1)

            def ffn(which, nb):
                n, g0 = nb, FF_TILES * which
                for th, J in enumerate(THIRDS):
                    with V.Fori(0, J // 2) as it:
                        for q in range(2):
                            na, nbb = n + 2 * q, n + 2 * q + 1
                            ta, tb = OUT0[na], OUT0[nbb]
                            split_lo(V, na + 4, it)
                            V.wait_ge(free[ta % 4], it + (ta // 4 + 1))
                            V.wait_ge(S["out_done"], it * 4 + (tb + 1))
                            V.tensor_tensor(gated[:, q], silu_a[:, q], bank[tb % 4][:, :], MUL).then_inc(free[tb % 4], 1)
                            split_lo(V, nbb + 4, it)
                            V.wait_ge(S["g_hi_done"], it * 2 + (g0 + q + 1))
                            V.tensor_tensor(g_lo[:, it * 2 + q], gated[:, q], g_hi[:, it * 2 + q].bitcast(f32), SUB) \
                             .then_inc(S["g_done"], 1)
                    n, g0 = n + 2 * J, g0 + J

                    def down(j, it):
                        split_lo(V, n + j + 4, it)
                        t = OUT0[n + j]
                        V.wait_ge(S["out_done"], it * 4 + (t + 1))
                        i = it * 4 + j if not isinstance(it, int) else j
                        V.scalar_tensor_tensor(x[:, i], bank[t % 4][:, :], 0.5, x[:, i], MUL, ADD) \
                         .then_inc(free[t % 4], 1)
                    if th == len(THIRDS) - 1:
                        for j in range(KT):
                            down(j, 0)
                            if which == 0 and j >= 2:
                                add_square(1, j - 2)
                    else:
                        with V.Fori(0, 2) as it:
                            for j in range(4):
                                down(j, it)
                    n += KT

            TT, TS, STT = V.tensor_tensor, V.tensor_scalar, V.scalar_tensor_tensor

            def low_y(g, i, src, scale=None):
                V.wait_ge(S["y_hi_done"], BT * TURN[g] + i + 1)
                hi = y_hi[:, i].bitcast(f32)
                ins = TT(y_lo[:, i], src, hi, SUB) if scale is None else STT(y_lo[:, i], src, scale, hi, MUL, SUB)
                ins.then_inc(S["y_done"], 1)

            def lot(kind, i):
                pass

            def pair(kind, i):
                pass

            def out(i):
                t = out_at("out", i)
                wait_out(V, t)
                STT(x[:, i], bank[t % 4][:, :], 0.5, x[:, i], MUL, ADD).then_inc(free[t % 4], 1)
                if i >= 2:
                    add_square(2, i - 2)

            def out_start(phase):
                for i in (range(KT - 2), range(KT - 2, KT))[phase]:
                    V.wait_ge(S["merge_used"], KT * (len(ORDER) - 1) + i + 1)
                    V.wait_ge(S["h_hi_done"], KT * 2 + i + 1)
                    TT(h_lo[:, i], merged[:, i], h_hi[:, i].bitcast(f32), SUB).then_inc(S["h_done"], 1)

            def turn_small():
                pass

            def gate(g, i):
                pass

            def branch(g, pair):
                for e in range(2):
                    i = 2 * pair + e
                    tp, tg = out_at("branch%d" % g, pair, e), out_at("gate%d" % g, i)
                    wait_taken(V, tg)
                    wait_out(V, tp)
                    STT(gate_th[:, e], gate_th[:, e], 1.0, bank[tp % 4][:, :], ADD, MUL).then_inc(free[tp % 4], 1)
                    wait_taken(V, tp)
                    if TURN[g] == 0:
                        V.tensor_copy(merged[:, i], gate_th[:, e]).then_inc(S["merge_used"], 1)
                    else:
                        V.wait_ge(S["merge_used"], KT * (TURN[g] - 1) + i + 1)
                        TT(merged[:, i], merged[:, i], gate_th[:, e], ADD).then_inc(S["merge_used"], 1)

            K = lambda i: s5_k[:, i]

            def s5_prep(phase):
                if phase == 1:
                    phases(0)
                    return
                V.wait_ge(S["s5_k_ready"], 1)
                chain(TT(K(2), PR("lam_im"), K(0), MUL))
                TT(K(1), PR("lam_re"), K(0), MUL).then_inc(S["s5_k_ready"], 1)
                chain(TS(K(2), K(2), 1.0 / (2 * PI), None, MUL))
                chain(TS(K(4), K(2), ROUND, -ROUND, ADD, ADD))
                chain(TT(K(5), K(2), K(4), SUB))
                V.wait_ge(S["s5_k_ready"], 3)
                STT(K(6), K(5), -1.0, K(5), MUL, ALU.max).then_inc(S["s5_k_ready"], 1)
                chain(TS(K(9), K(5), ROUND13, -ROUND13, ADD, ADD))
                TT(K(10), K(5), K(9), SUB).then_inc(S["s5_khi"], 1)
                V.wait_ge(S["s5_k_ready"], 6)
                do(TT(K(11), K(3), K(8), MUL))
                chain(TT(K(12), K(3), K(7), MUL))
                do(TS(K(13), K(11), -1.0, None, ADD))
                do(TT(K(14), PR("lam_re"), PR("lam_re"), MUL))
                chain(TT(K(15), PR("lam_im"), PR("lam_im"), MUL))
                chain(TT(K(14), K(14), K(15), ADD))
                do(V.reciprocal(K(14), K(14)))
                do(TT(K(15), K(13), PR("lam_re"), MUL))
                chain(TT(K(16), K(12), PR("lam_im"), MUL))
                do(TT(K(15), K(15), K(16), ADD))
                do(TT(K(17), K(12), PR("lam_re"), MUL))
                chain(TT(K(18), K(13), PR("lam_im"), MUL))
                chain(TT(K(17), K(17), K(18), SUB))
                do(TT(K(19), K(15), K(14), MUL))
                chain(TT(K(20), K(17), K(14), MUL))
                V.wait_ge(S["s5_in"], 16)
                qre, qim = (K(c).unsqueeze(2).broadcast_to([P, 16, 32]) for c in (19, 20))
                T = lambda i: s5_pr[:, i].rearrange("p (s c) -> p s c", c=32)
                do(TT(T(0), s5_bc[:, 0], qre, MUL))
                do(TT(T(1), s5_bc[:, 1], qim, MUL))
                do(TT(T(2), s5_bc[:, 1], qre, MUL))
                chain(TT(T(3), s5_bc[:, 0], qim, MUL))
                TT(s5_bb[:, 0], T(0), T(1), SUB).then_inc(S["s5_bb_ready"], 1)
                TT(s5_bb[:, 1], T(2), T(3), ADD).then_inc(S["s5_bb_ready"], 1)
                chain(TS(s5_bc[:, 3], s5_bc[:, 3], -1.0, None, MUL))
                V.wait_ge(S["s5_bb_ready"], 2)

            def phases(st):
                f, fr = s5_ph[:, 2 * (st % 2)], s5_ph[:, 2 * (st % 2) + 1]
                V.wait_ge(S["s5_pre"], 2 * (st + 1))
                chain(STT(f, fr, -ROUND, f, ADD, SUB))
                chain(STT(f, C("tvec"), K(10)[:, st:st + 1], f, MUL, SUB))
                TS(f, f, 0.5, -0.5, ALU.min, ALU.max).then_inc(S["s5_phase"], 1)

            def states(st):
                e = st % 2
                re, im, cs, sn = bank[4][:, :], bank[5][:, :], s5_cos[:, e], s5_sin[:, e]
                pr = [s5_pr[:, i] for i in range(4)]
                v = s5_v[e]
                V.wait_ge(S["s5_bu"], st + 1)
                V.wait_ge(S["s5_trig"], 2 * (st + 1))
                if st:
                    V.wait_ge(S["s5_state"], st)
                do(TT(pr[0], re, cs, MUL))
                n = do(TT(pr[1], im, sn, MUL))
                do(TT(pr[2], im, cs, MUL))
                TT(pr[3], re, sn, MUL).then_inc(S["s5_bu_used"], 1)
                need(n)
                if st >= 2:
                    V.wait_ge(S["s5_sim"], st - 1)
                n = do(TT(v[:, 0], pr[0], pr[1], ADD))
                V.wait_ge(S["s5_bu_used"], st + 1)
                m = do(TT(v[:, 1], pr[2], pr[3], SUB))
                mag = K(3)[:, st:st + 1].broadcast_to([P, SEQ])
                need(n)
                V.tensor_tensor_scan(v[:, 0], mag, v[:, 0], 0.0, MUL, ADD).then_inc(S["s5_z"], 1)
                need(m)
                V.tensor_tensor_scan(v[:, 1], mag, v[:, 1], 0.0, MUL, ADD).then_inc(S["s5_z"], 1)
                V.wait_ge(S["s5_z"], 2 * st + 1)
                if st >= 2:
                    V.wait_ge(S["s5_y"], st - 1)
                do(TT(s5_s[:, e, 0], v[:, 0], cs, MUL))
                V.wait_ge(S["s5_z"], 2 * st + 2)
                if st:
                    V.wait_ge(S["s5_sre"], st)
                TT(s5_vs[:, :], v[:, 1], sn, MUL).then_inc(S["s5_state"], 1)

            def skip(jt):
                V.wait_ge(S["s5_y"], 4 * (jt + 1))
                STT(s5_u[:, jt], s5_u[:, jt], PC("s5_d", jt), bank[6][:, :], MUL, ADD).then_inc(S["s5_y_used"], 1)

            def s5(st):
                if st + 1 < S5_TILES:
                    phases(st + 1)
                states(st)
                if st % 4 == 1 and st > 4:
                    skip(st // 4 - 1)

            def s5_end():
                skip(3)
                for i in range(4):
                    V.wait_ge(S["gel_hi_done"], i + 1)
                    TT(gel_lo[:, i], gel[:, i % 2], gel_hi[:, i].bitcast(f32), SUB).then_inc(S["gel_done"], 1)

            def glu(i):
                n = LOT_AT[("glu", i)]
                t = OUT0[n]
                wait_out(V, t)
                wait_taken(V, t + 1)
                if i >= 2:
                    V.wait_ge(S["y_done"], i - 1)
                STT(glu_y[:, i % 2], glu_th[:, i % 2], 1.0, bank[t % 4][:, :], ADD, MUL).then_inc(free[t % 4], 1)
                wait_taken(V, t)
                V.sem_inc(S["glu_y_done"], 1)
                low_y(1, i, glu_y[:, i % 2], 0.5)

            def da_norm(g, phase):
                gain = ("q_norm", "k_norm")[g]
                for j in range(4 if phase == 0 else 0):
                    V.wait_ge(S["da_rms"], 4 * g + j + 1)
                    STT(da_qk[:, 4 * g + j], da_qk[:, 4 * g + j], PR(gain), da_t[:, j], MUL, MUL) \
                        .then_inc(S["da_qn"], 1)
                for j in range(4 if phase == 1 else 0):
                    V.wait_ge(S["da_rot"], 4 * g + j + 1)
                    V.wait_ge(S["da_qn"], 4 * g + j + 1)
                    do(TT(da_t[:, j], bank[4 + j][:, :], rope_sin[:, :], MUL))
                    chain(TT(da_qk[:, 4 * g + j], da_qk[:, 4 * g + j], rope_cos[:, :], MUL))
                    TT(da_qk[:, 4 * g + j], da_qk[:, 4 * g + j], da_t[:, j], ADD).then_inc(S["da_rot_done"], 1)
            def da_index(b):
                if b == 1:
                    V.wait_ge(S["small_done"], 1)
                    chain(V.tensor_copy(da_mb[:, 0:P], C("cmask")))
                w = P * (b + 1)
                scores = da_sc2 if b == 2 else da_sc
                for hh in range(4):
                    V.wait_ge(S["da_relu"], 4 * (b - 1) + hh + 1)
                    sc, r, wi = scores[:, 0:w], da_r[:, hh, 0:w], small[:, b, hh:hh + 1]
                    if hh == 0:
                        chain(TS(sc, r, wi, None, MUL))
                    elif hh < 3:
                        chain(STT(sc, r, wi, sc, MUL, ADD))
                    else:
                        STT(sc, r, wi, sc, MUL, ADD).then_inc(S["da_score"], 1)
                V.wait_ge(S["da_score"], b)
                chain(TT(scores[:, P * b:w], scores[:, P * b:w], C("cmask"), ADD))

            def da_topk(b, phase):
                w = P * (b + 1)
                rounds = TOPK // 8 // TOPK_PHASES
                for r in range(rounds * phase, rounds * (phase + 1)):
                    src = da_wk if r else da_sc2 if b == 2 else da_sc
                    chain(V.max(da_m8[:, :], src[:, 0:w]))
                    chain(V.match_replace(da_wk[:, 0:w], da_m8[:, :], src[:, 0:w], TAKEN))
                if phase < TOPK_PHASES - 1:
                    return
                chain(TS(da_mb[:, DA_OFF[b]:DA_OFF[b] + w], da_wk[:, 0:w], -2.0e38, NEG, ALU.is_gt, MUL))
                if b == NB - 1:
                    V.sem_inc(S["da_idx_done"], 1)

            def masked(u):
                hp, b, e = UNITS[u]
                w = P * (b + 1)
                V.wait_ge(S["da_logit"], u + 1)
                if u >= 2:
                    V.wait_ge(S["da_exp"], u - 1)
                chain(V.tensor_tensor_reduce(out=da_lg[:, u % 2, 0:w], in0=bank[4 + u % 2][:, 0:w],
                                             in1=da_mb[:, DA_OFF[b]:DA_OFF[b] + w], scale=1.0, scalar=TAKEN,
                                             op0=ADD, op1=ALU.max, accum_out=da_st[:, u, 0:1]))
                TS(da_st[:, u, 1:2], da_st[:, u, 0:1], -0.125, None, MUL).then_inc(S["da_max"], 1)

            def normalise(u):
                hp, b, e = UNITS[u]
                w = P * (b + 1)
                V.wait_ge(S["da_exp"], u + 1)
                chain(V.reciprocal(da_st[:, u, 3:4], da_st[:, u, 2:3]))
                TS(da_p[:, u % 2, 0:w], da_p[:, u % 2, 0:w], da_st[:, u, 3:4], None, MUL).then_inc(S["da_prob"], 1)
            def low_att(b, src=bank[7][:, :].rearrange("p (h t) -> p h t", t=P)):
                V.wait_ge(S["y_hi_done"], BT * TURN[2] + b + 1)
                t = slice(P * b, P * (b + 1))
                TT(y_lo[:, :, t], src, y_hi[:, :, t].bitcast(f32), SUB) \
                    .then_inc(S["y_done"], 1)

            def att_start():
                masked(0)

            def att(u):
                normalise(u)
                if u < 31:
                    masked(u + 1)
                if u == 17:
                    low_att(0, da_o[:, :, :])
                if u % 8 == 1 and u > 9:
                    low_att(u // 8 - 1)

            def att_end():
                low_att(3)

            D = lambda i: m2_dt[:, i]
            heads = lambda a: a.unsqueeze(1).broadcast_to([P, NB, 8])

            def m2_decay():
                TT(D(0), small[:, :, 4:12], heads(PR("dt_bias")), ADD).then_inc(S["m2_dtb"], 1)
                V.wait_ge(S["m2_dtb"], 1)
                STT(D(1), D(0), -1.0, D(0), MUL, ALU.max).then_inc(S["m2_dtb"], 1)

            def m2_conv():
                chain(V.memset(m2_xr[:, :, 0:3], 0.0))
                n = {}
                for k in (3, 2, 1, 0):
                    for i in range(6):
                        xs, wk = m2_xr[:, i, k:k + SEQ], PC("conv_w", 6 * k + i)
                        if k == 3:
                            wait_taken(V, out_at("xbc", i))
                            n[i] = do(TS(m2_xc[:, i], xs, wk, PC("conv_b", i), MUL, ADD))
                        else:
                            need(n[i])
                            ins = STT(m2_xc[:, i], xs, wk, m2_xc[:, i], MUL, ADD)
                            if k:
                                n[i] = do(ins)
                            else:
                                ins.then_inc(S["m2_conv"], 1)
                V.wait_ge(S["m2_abs"], 2)
                chain(STT(D(0), D(0), 0.0, D(1), ALU.max, ADD))
                STT(D(1), D(0), -1.0, heads(m2_ea[:, :]), MUL, MUL).then_inc(S["m2_dt_ready"], 1)

            def m2_prep(phase):
                if phase == 0:
                    V.wait_ge(S["m2_acs"], 1)
                    V.tensor_copy(D(2).rearrange("p b h -> p (b h)"), bank[4][:, 0:32]).then_inc(S["m2_acs_done"], 1)
                    V.wait_ge(S["m2_acs_done"], 1)
                for b in range(2 * phase - 2, 2 * phase) if phase in (1, 2) else ():
                    V.wait_ge(S["m2_ct"], b + 1)
                    TT(m2_xdt[:, b].rearrange("p (h d) -> p h d", d=64),
                       bank[5 + b % 2][:, :].rearrange("p (h d) -> p h d", d=64),
                       D(0)[:, b].unsqueeze(2).broadcast_to([P, 8, 64]), MUL).then_inc(S["m2_xdt_done"], 1)
                for c in range(4 * (phase - 3), 4 * (phase - 2)) if phase > 2 else ():
                    g, j = c // 4, c % 4
                    V.wait_ge(S["m2_cbp"], c + 1)
                    w = SEQ - P * j
                    TT(m2_cb[:, g, M2_OFF[j]:M2_OFF[j] + w], bank[4 + 3 * (c % 2)][:, 0:w], C("upper", 0, w), MUL) \
                        .then_inc(S["m2_cb_done"], 1)
                if phase == 4:
                    V.wait_ge(S["m2_cb_done"], 8)

            def segments(h):
                V.wait_ge(S["m2_acb"], h + 1)
                if h >= 2:
                    V.wait_ge(S["m2_yp"], h - 1)
                for j in range(NB):
                    ins = TS(m2_e[:, h % 2, M2_OFF[j]:M2_OFF[j] + SEQ - P * j], bank[4 + h % 2][:, P * j:SEQ],
                             D(2)[:, j, h:h + 1], 0.0, SUB, ALU.min)
                    if j < NB - 1:
                        do(ins)
                ins.then_inc(S["m2_seg"], 1)

            def y_of(hp):
                V.wait_ge(S["m2_yp"], 2 * hp + 2)
                STT(m2_yv[:, hp], m2_xc[:, hp], PC("m2_d", hp), bank[6 + hp % 2][:, :], MUL, ADD) \
                    .then_inc(S["m2_y"], 1)
            def m2_head(h):
                if h == 0:
                    segments(0)
                V.wait_ge(S["m2_decay"], h + 1)
                TT(m2_e[:, h % 2], m2_e[:, h % 2], m2_cb[:, h // 4], MUL).then_inc(S["m2_m"], 1)
                if h < 7:
                    segments(h + 1)
                if h >= 2 and h % 2 == 0:
                    y_of(h // 2 - 1)

            def m2_norm():
                y_of(3)
                V.wait_ge(S["m2_zs"], 4)
                for i in range(BT):
                    V.wait_ge(S["m2_y"], i + 1)
                    TT(m2_yv[:, i], m2_yv[:, i], m2_z[:, i], MUL).then_inc(S["m2_yn"], 1)

            def m2_end():
                V.wait_ge(S["m2_rms"], 1)
                for i in range(BT):
                    STT(m2_yv[:, i], m2_yv[:, i], PC("m2_norm", i), m2_rs[:, :], MUL, MUL).then_inc(S["m2_yn"], 1)
                for i in range(BT):
                    low_y(0, i, m2_yv[:, i])

            def hg_start():
                V.wait_ge(S["y_done"], BT * (TURN[0] + 1))
                V.wait_ge(S["m2_yn"], 2 * BT)
                do(V.memset(hatt[:, :, :], 0.0))
                chain(V.tensor_copy(hlb[:, 0], lower[:, layer_at[0]]))
                chain(TS(hlb[:, 1], hlb[:, 0], -1.0, 1.0, MUL, ADD))

            chunks = lambda a: a.rearrange("p (c t) -> p c t", t=HG_CHUNK)

            def hg_gates(h, phase):
                X = [he[:, h % 2, i] for i in range(4)]
                if phase == 0:
                    V.wait_ge(S["hg_e"], h + 1)
                    do(TS(X[0], X[0], 1.0, None, ADD))
                    chain(TS(hf[:, h], hf[:, h], 1.0, None, ADD))
                    n = do(V.reciprocal(X[0], X[0]))
                    m = do(V.reciprocal(hf[:, h], hf[:, h]))
                    need(n)
                    TS(X[0], X[0], hlb[:, 1, h:h + 1], hlb[:, 0, h:h + 1], MUL, ADD).then_inc(S["hg_fg"], 1)
                    need(m)
                    chain(TS(hf[:, h], hf[:, h], hlb[:, 1, h:h + 1], None, MUL))
                elif phase == 1:
                    V.wait_ge(S["hg_lf"], h + 1)
                    V.tensor_tensor_scan(X[1], C("hgreset"), X[0], 0.0, MUL, ADD).then_inc(S["hg_cum"], 1)
                    V.wait_ge(S["hg_cum"], h + 1)
                    cum = chunks(X[1])
                    TT(chunks(X[3]), cum[:, :, HG_CHUNK - 1:HG_CHUNK].broadcast_to([P, NCH, HG_CHUNK]), cum, SUB) \
                        .then_inc(S["hg_lc"], 1)
                else:
                    V.wait_ge(S["hg_ex"], 4)
                    V.wait_ge(S["hg_ec"], 3 * h + 3)
                    TT(hq[:, h], hq[:, h], X[0], MUL).then_inc(S["hg_ke"], 1)
                    TT(X[2], hf[:, h], X[2], MUL).then_inc(S["hg_ke"], 1)
                    V.wait_ge(S["hg_el"], h + 1)
                    TT(X[3], hf[:, h], X[3], MUL).then_inc(S["hg_ke"], 1)

            def hg_head(h, phase):
                if phase == 0:
                    V.wait_ge(S["hg_attp"], h + 1)
                    V.copy_predicated(hatt[:, :, :], C("hgmask").bitcast(u32).unsqueeze(1).broadcast_to([P, NB, P]),
                                      bank[4][:, :].rearrange("p (b q) -> p b q", q=P)).then_inc(S["hg_att"], 1)
                elif phase == 1:
                    V.wait_ge(S["hg_upd"], h + 1)
                    for c in range(NCH - 1):
                        new = bank[4 + c % 4][:, P * (c // 4):P * (c // 4 + 1)]
                        if c == 0:
                            ins = V.tensor_copy(hS[:, 1], new)
                        else:
                            ins = STT(hS[:, c + 1], hS[:, c], hdec[:, h % 2, c:c + 1], new, MUL, ADD)
                        if c == NCH - 2:
                            ins.then_inc(S["hg_updu"], 1)
                        else:
                            chain(ins)

            def hg_norm(h):
                V.wait_ge(S["hg_rms"], h + 1)
                chain(STT(hf[:, h], hf[:, h], PC("hg_norm", h), he[:, h % 2, 1], MUL, MUL))
                wait_taken(V, out_at("hg", h))
                STT(hf[:, h], hg[:, h], 1.0, hf[:, h], ADD, MUL).then_inc(S["hg_yn"], 1)

            def hg_end():
                for h in range(4):
                    low_y(3, h, hf[:, h], 0.5)

            layer_at = [None]

            STEPS = dict(lot=lot, pair=pair, turn_small=turn_small, out=out, out_start=out_start, glu=glu, gate=gate, branch=branch,
                         s5_prep=s5_prep, s5=s5,
                         s5_end=s5_end, da_norm=da_norm, da_index=da_index, da_topk=da_topk, att_start=att_start,
                         att=att, att_end=att_end, m2_decay=m2_decay, m2_conv=m2_conv, m2_prep=m2_prep, m2_head=m2_head,
                         m2_norm=m2_norm, m2_end=m2_end, hg_start=hg_start, hg_gates=hg_gates, hg_head=hg_head,
                         hg_norm=hg_norm, hg_end=hg_end)

            def mixing(layer):
                layer_at[0] = layer
                for step in SCRIPT:
                    STEPS[step[0]](*step[1:])

            V.memset(epsc[:, :], EPS).then_inc(S["p_seq"], 1)
            V.memset(half_pi[:, :], PI / 2).then_inc(S["p_seq"], 1)
            V.memset(roundc[:, :], ROUND).then_inc(S["p_seq"], 1)
            p = Order(V, S["p_seq"])
            p.n = 3

            def pdo(ins):
                p.need(p.do(ins))
            V.wait_ge(S["c_pos"], 16)
            V.wait_ge(S["c_freq"], 16)
            pdo(V.tensor_copy(ang[:, 2], pos_i[:, :]))
            pdo(V.tensor_scalar(ang[:, 0], ang[:, 2], C("invfreq", 0, 1), None, MUL))
            pdo(V.tensor_scalar(ang[:, 1], ang[:, 0], 1.0 / (2 * PI), ROUND, MUL, ADD))
            pdo(V.tensor_scalar(ang[:, 1], ang[:, 1], -ROUND, None, ADD))
            c1 = 6.28125
            c2 = float(np.float32(2 * PI - c1))
            c3 = 2 * PI - c1 - c2
            for c in (c1, c2, c3):
                pdo(V.scalar_tensor_tensor(ang[:, 0], ang[:, 1], -c, ang[:, 0], MUL, ADD))
            V.tensor_scalar(ang[:, 0], ang[:, 0], float(np.float32(3.1415925)), -float(np.float32(3.1415925)), ALU.min, ALU.max) \
             .then_inc(S["p_ang"], 1)
            V.wait_ge(S["p_ang"], 1)
            V.scalar_tensor_tensor(ang[:, 1], ang[:, 0], -1.0, ang[:, 0], MUL, ALU.max).then_inc(S["p_ang"], 1)
            V.wait_ge(S["c_gam"], 16)
            pdo(V.tensor_copy(gtmp[:, 2, 0], gam[:, 0]))
            for l in range(1, DEPTH):
                pdo(V.tensor_tensor(gtmp[:, 2, 0], gtmp[:, 2, 0], gam[:, l], ALU.max))
            for l in range(DEPTH):
                ins = V.tensor_tensor(gtmp[:, 0, l], gam[:, l], gtmp[:, 2, 0], SUB)
                if l < DEPTH - 1:
                    pdo(ins)
            ins.then_inc(S["p_gam1"], 1)
            V.wait_ge(S["p_trig"], 3)
            pdo(V.tensor_copy(gtmp[:, 3, 0], gtmp[:, 1, 0]))
            for l in range(1, DEPTH):
                pdo(V.tensor_tensor(gtmp[:, 3, 0], gtmp[:, 3, 0], gtmp[:, 1, l], ADD))
            pdo(V.reciprocal(gtmp[:, 3, 0], gtmp[:, 3, 0]))
            pdo(V.memset(lower[:, 0], 0.0))
            for l in range(1, DEPTH):
                pdo(V.tensor_tensor(gtmp[:, 4, 0], gtmp[:, 1, l], gtmp[:, 3, 0], MUL))
                pdo(V.tensor_tensor(lower[:, l], lower[:, l - 1], gtmp[:, 4, 0], ADD))
            V.sem_inc(S["p_gam2"], 1)
            with V.Fori(0, DEPTH) as layer:
                seq.n = 0
                square_sums(0)
                split_lo(V, 0)
                split_lo(V, 1)
                norm(0, "ffn1_norm")
                split_lo(V, 2)
                split_lo(V, 3)
                ffn(0, 0)
                add_square(1, KT - 2)
                add_square(1, KT - 1)
                norm(1, "mix_norm")
                V.wait_ge(S["c_con"], 16)
                V.wait_ge(S["c_rest"], 16)
                mixing(layer)
                add_square(2, KT - 2)
                add_square(2, KT - 1)
                norm(2, "ffn2_norm")
                V.wait_ge(S["lo_done"], FFN2_0 + 4)
                ffn(1, FFN2_0)
                end_of_layer(V, S["go_dve"])


def kernel(**inputs):
    import numpy as _np
    import concourse.bacc as _bacc
    from concourse import mybir as _mybir
    from concourse.bass_utils import run_bass_kernel_spmd as _run

    a = {k: _np.asarray(v) for k, v in inputs.items()}

    def lots(w):
        L, K, M = w.shape
        pad = -M % P
        if pad:
            w = _np.concatenate([w, _np.zeros((L, K, pad), w.dtype)], 2)
        return w.reshape(L, K // P, P, (M + pad) // P, P).transpose(0, 3, 2, 1, 4)

    def ffn_lots(w1, w3, w2):
        w1, w3, got, j0 = lots(w1), lots(w3), [], 0
        for J in THIRDS:
            for j in range(j0, j0 + J):
                got += [w1[:, j], w3[:, j]]
            w = lots(w2[:, P * j0:P * (j0 + J)])
            fill = _np.zeros((DEPTH, P, 8 - J, P), w.dtype)
            for i in range(KT):
                got.append(_np.concatenate([w[:, i], fill], 2))
            j0 += J
        return got

    w_in = a["w_in"]
    m2, s5, da = 0, 2 * BW + 256 + 8, 3 * BW + 256 + 8
    hg = da + 3 * BW + 256 + 64 + 4
    parts = dict(z=lots(w_in[:, :, 0:BW]), xbc=lots(w_in[:, :, BW:2 * BW + 256]), u=lots(w_in[:, :, s5:s5 + BW]),
                 q=lots(w_in[:, :, da:da + BW]), k=lots(w_in[:, :, da + BW:da + 2 * BW]),
                 v=lots(w_in[:, :, da + 2 * BW:da + 3 * BW]), qi=lots(w_in[:, :, da + 3 * BW:da + 3 * BW + 256]))
    ki = w_in[:, :, da + 3 * BW + 256:da + 3 * BW + 320]
    parts["ki"] = lots(_np.concatenate([ki, ki], 2))
    parts["small"] = lots(_np.concatenate([w_in[:, :, hg - 4:hg], w_in[:, :, s5 - 8:s5]], 2))
    for i, name in enumerate(("hq", "hf", "hv", "hg")):
        parts[name] = lots(w_in[:, :, hg + BW * i:hg + BW * (i + 1)])
    for g in range(4):
        parts["gate%d" % g] = lots(a["w_gate"][:, :, DM * g:DM * (g + 1)])
        w = lots(a["w_branch"][:, g])
        parts["branch%d" % g] = _np.concatenate([w[:, 0::2], w[:, 1::2]], 3)
    w = lots(a["s5_w_glu"])
    parts["glu"] = _np.concatenate([w[:, 0:4], w[:, 4:8]], 3)
    parts["out"] = lots(a["w_out"])
    stream = ffn_lots(a["ffn1_w1"], a["ffn1_w3"], a["ffn1_w2"]) + [parts[kind][:, i] for kind, i in MIX] \
        + ffn_lots(a["ffn2_w1"], a["ffn2_w3"], a["ffn2_w2"])
    w_lots = _np.stack(stream, 1).reshape(DEPTH * NLOT, P, 8 * P)

    def cols(v):
        return v.reshape(DEPTH, -1, P).transpose(0, 2, 1)

    def rows(v):
        return _np.repeat(v[:, None, :], P, 1)

    par = dict(ffn1_norm=cols(a["ffn1_norm"]), mix_norm=cols(a["mix_norm"]), ffn2_norm=cols(a["ffn2_norm"]),
               conv_w=_np.concatenate([cols(a["m2_conv_w"][:, k]) for k in range(4)], 2), conv_b=cols(a["m2_conv_b"]),
               dt_bias=rows(a["m2_dt_bias"]), a_log=rows(a["m2_a_log"]), m2_d=cols(_np.repeat(a["m2_d"], 64, 1)),
               m2_norm=cols(a["m2_norm"]), lam_re=cols(a["s5_lam_re"].reshape(DEPTH, -1)),
               lam_im=cols(a["s5_lam_im"].reshape(DEPTH, -1)), log_dt=cols(_np.repeat(a["s5_log_dt"], 64, 1)),
               s5_d=cols(a["s5_d"]), q_norm=cols(_np.tile(a["dsa_q_norm"], 2)), k_norm=cols(_np.tile(a["dsa_k_norm"], 2)),
               hg_norm=cols(a["hg_norm"]))
    par = _np.concatenate([par[k] for k in PAR_SIZES], 2)

    s5_in = _np.zeros((DEPTH, P, 4, 16, 32), _np.float32)
    for i, (name, perm) in enumerate((("s5_b_re", None), ("s5_b_im", None), ("s5_c_re", 1), ("s5_c_im", 1))):
        v = a[name] if perm is None else a[name].transpose(0, 1, 3, 2)
        v = v.reshape(DEPTH, 16, 2, 64, 16)
        for e in range(2):
            s5_in[:, 64 * e:64 * e + 64, i, :, 16 * e:16 * e + 16] = v[:, :, e].transpose(0, 2, 1, 3)

    con = _np.zeros((P, NCON), _np.float32)
    r = _np.arange(P)

    def put(name, v):
        con[:, CON_AT[name]:CON_AT[name] + CON_SIZES[name]] = v
    t = _np.arange(SEQ)
    put("ident", _np.eye(P))
    put("upper", t[None, :] >= r[:, None])
    put("blk", r[:, None] // 64 == r[None, :] // 64)
    put("rot", -1.0 * ((r[None, :] % 64 < 32) & (r[:, None] == r[None, :] + 32))
        + ((r[None, :] % 64 >= 32) & (r[:, None] == r[None, :] - 32)))
    put("hgmask", (r[:, None] // HG_CHUNK == r[None, :] // HG_CHUNK) & (r[:, None] <= r[None, :]))
    put("hgreset", (t % HG_CHUNK != 0)[None, :])
    put("tvec", t[None, :])
    put("cmask", _np.where(r[None, :] <= r[:, None], 0.0, NEG))
    put("invfreq", (_np.float32(10000.0) ** (-(r % 32).astype(_np.float32) / _np.float32(32)))[:, None])

    gamma = a["hg_gamma"].reshape(DEPTH, 4, P).transpose(2, 0, 1)
    arrays = dict(x=a["x"].reshape(SEQ, DM), positions=a["positions"].reshape(SEQ), w_lots=w_lots, par=par,
                  s5=s5_in.reshape(DEPTH, P, 2048), con=con, gamma=gamma)
    nc = _bacc.Bacc("TRN2", target_bir_lowering=False, num_devices=1)
    args, feed = [], {}
    for name, v in arrays.items():
        feed["in_" + name] = _np.ascontiguousarray(v)
        args.append(nc.dram_tensor("in_" + name, v.shape, _mybir.dt.from_np(v.dtype), kind="ExternalInput").ap())
    args.append(nc.dram_tensor("out_x", (SEQ, DM), _mybir.dt.float32, kind="ExternalOutput").ap())
    trunk(nc, *args)
    r = _run(nc, [feed], core_ids=[0])
    return r.results[0]["out_x"].reshape(1, SEQ, DM)
```
